# Optimizing a Trainium2 kernel written in Bass

```python
import math
import jax
import jax.numpy as jnp
from jax import lax
import numpy as np

D_MODEL = 1024
BATCH = 1
SEQ = 256
DEPTH = 2

GRID_W = 64
CTX_LEN = 256
N_MIXERS = 4
GROUP_WIDTH = D_MODEL // N_MIXERS
HEAD_DIM = 64
N_HEADS = GROUP_WIDTH // HEAD_DIM
MIX_WIDTH = N_MIXERS * GROUP_WIDTH
D_FF = 2816
CHUNK = 64
ATTN_BLOCK = 128
DIFF_QK_DIM = HEAD_DIM // 2
ROPE_BASE = 10000.0
RWKV_DECAY_LORA = 64
RWKV_ICLR_LORA = 64
RWKV_GATE_LORA = 160
RWKV_LNX_EPS = 64e-5
LN_EPS = 1e-5
MASK_NEG = -1e30
LB_FLOOR = 1e-30
MAX_NEG_LOG_STAB = 60.0
DEEPNORM_ALPHA = (2.0 * DEPTH) ** 0.25
DEEPNORM_BETA = (8.0 * DEPTH) ** -0.25

RWKV_COLS = (GROUP_WIDTH,) * 3 + (RWKV_DECAY_LORA,) * 2 + (RWKV_ICLR_LORA,) * 2 + (RWKV_GATE_LORA,)
DIFF_COLS = (GROUP_WIDTH,) * 3
HGRN_COLS = (GROUP_WIDTH,) * 5
MLSTM_COLS = (GROUP_WIDTH,) * 4 + (N_HEADS,) * 4
GROUP_COLS = (sum(RWKV_COLS), sum(DIFF_COLS), sum(HGRN_COLS), sum(MLSTM_COLS))
IN_COLS = sum(GROUP_COLS)

kernel_name = 'hybrid_rwkv7_diffattn_hgrn2_mlstm_dit_block'

def _split(x, sizes):
    offs = [int(o) for o in np.cumsum(sizes)[:-1]]
    return jnp.split(x, offs, axis=-1)

def _heads(x):
    return x.reshape(x.shape[:-1] + (N_HEADS, x.shape[-1] // N_HEADS))

def _norm(y, gain, bias=None, eps=LN_EPS, rms=False):
    yf = y.astype(jnp.float32)
    if not rms:
        yf = yf - jnp.mean(yf, axis=-1, keepdims=True)
    yf = yf * lax.rsqrt(jnp.mean(jnp.square(yf), axis=-1, keepdims=True) + eps) * gain
    if bias is not None:
        yf = yf + bias
    return yf.astype(y.dtype)

def _l2_normalize(x, eps=1e-12):
    xf = x.astype(jnp.float32)
    return (xf / jnp.maximum(jnp.linalg.norm(xf, axis=-1, keepdims=True), eps)).astype(x.dtype)

def _neighbours(z):
    zero = jnp.zeros_like(z[:, :1])
    return jnp.concatenate([zero, z[:, :-1]], axis=1), jnp.concatenate([z[:, 1:], zero], axis=1)

def _dwconv3(z, w, b):
    prev, nxt = _neighbours(z)
    return prev * w[0] + z * w[1] + nxt * w[2] + b

def _modulate(h, shift, scale):
    return h * (1.0 + scale) + shift

def _adaln(cond, w, b):
    mod = (jax.nn.silu(cond) @ w + b)[:, None, :]
    return jnp.split(mod, 6, axis=-1)

def _to_chunks(x):
    B, T, H = x.shape[:3]
    x = x.reshape((B, T // CHUNK, CHUNK, H) + x.shape[3:])
    return jnp.moveaxis(jnp.moveaxis(x, 1, 0), 3, 2)

def _from_chunks(y):
    nc, B, H, C = y.shape[:4]
    y = jnp.moveaxis(jnp.moveaxis(y, 2, 3), 0, 1)
    return y.reshape((B, nc * C, H) + y.shape[4:])

def _bidir_scan(scan_fn, ctx_dirs, lat_dirs, init):
    flip = lambda xs: tuple(jnp.flip(t, axis=1) for t in xs)
    dtype = lat_dirs[0][0].dtype
    y_ctx, y_lat = [], []
    for d in range(2):
        cx, lx = ctx_dirs[d], lat_dirs[d]
        if d == 1:
            cx, lx = flip(cx), flip(lx)
        s_ctx, yc = scan_fn(cx, init)
        _, yl = scan_fn(lx, s_ctx)
        if d == 1:
            yc, yl = flip((yc, yl))
        y_ctx.append(yc)
        y_lat.append(yl)
    return (y_ctx[0] + y_ctx[1]).astype(dtype), (y_lat[0] + y_lat[1]).astype(dtype)

def _rwkv7_scan(inputs, state):
    r, w, k, v, a, b = (jnp.moveaxis(t.astype(jnp.float32), 1, 0) for t in inputs)

    def step(S, xt):
        r_t, w_t, k_t, v_t, a_t, b_t = xt
        sa = jnp.einsum('bhvk,bhk->bhv', S, a_t)
        S = S * w_t[:, :, None, :] + sa[..., None] * b_t[:, :, None, :] + v_t[..., None] * k_t[:, :, None, :]
        return S, jnp.einsum('bhvk,bhk->bhv', S, r_t)

    S, y = lax.scan(step, state, (r, w, k, v, a, b))
    return S, jnp.moveaxis(y, 0, 1)

def _rwkv7_features(p, mu, w0, w2, a0, a2, g2, k_k, k_a):
    prev, nxt = _neighbours(p)
    p = p + (0.5 * (prev + nxt) - p) * mu
    r, k, v, wd_f, wd_b, ad_f, ad_b, gd = _split(p, RWKV_COLS)
    rh, kh, vh = _heads(r), _heads(k), _heads(v)
    kk = _l2_normalize(kh * k_k.reshape(N_HEADS, HEAD_DIM))
    ka = k_a.reshape(N_HEADS, HEAD_DIM)
    dirs = []
    for d, (wd, ad) in enumerate(((wd_f, ad_f), (wd_b, ad_b))):
        w_log = -jax.nn.softplus(-(w0[d] + jnp.tanh(wd) @ w2[d]).astype(jnp.float32)) - 0.5
        decay = jnp.exp(-jnp.exp(w_log))
        a = _heads(jax.nn.sigmoid(a0[d] + ad @ a2[d]))
        kd = kh * (1.0 + (a - 1.0) * ka)
        dirs.append((rh, _heads(decay), kd, vh, -kk, kk * a))
    g = jax.nn.sigmoid(gd) @ g2
    return rh, vh, g, dirs

def _rwkv7_mixer(p_ctx, p_lat, mu, w0, w2, a0, a2, g2, k_k, k_a, r_k, lnx_g, lnx_b):
    f_ctx = _rwkv7_features(p_ctx, mu, w0, w2, a0, a2, g2, k_k, k_a)
    f_lat = _rwkv7_features(p_lat, mu, w0, w2, a0, a2, g2, k_k, k_a)
    init = jnp.zeros((p_lat.shape[0], N_HEADS, HEAD_DIM, HEAD_DIM), jnp.float32)
    y_ctx, y_lat = _bidir_scan(_rwkv7_scan, f_ctx[3], f_lat[3], init)
    gn_g, gn_b = lnx_g.reshape(N_HEADS, HEAD_DIM), lnx_b.reshape(N_HEADS, HEAD_DIM)
    rk = r_k.reshape(N_HEADS, HEAD_DIM)

    def readout(feats, y):
        rh, vh, g, dirs = feats
        y = _norm(y, gn_g, gn_b, eps=RWKV_LNX_EPS)
        bonus = jnp.sum(rh * (dirs[0][2] + dirs[1][2]) * rk, axis=-1, keepdims=True) * vh
        return (y + bonus).reshape(g.shape) * g

    return readout(f_ctx, y_ctx), readout(f_lat, y_lat)

def _axial_rope(n_tokens):
    rows = n_tokens // GRID_W
    row = jnp.repeat(jnp.arange(rows, dtype=jnp.float32), GRID_W)
    col = jnp.tile(jnp.arange(GRID_W, dtype=jnp.float32), rows)
    n_freq = DIFF_QK_DIM // 4
    inv_freq = ROPE_BASE ** (-jnp.arange(n_freq, dtype=jnp.float32) / n_freq)
    ang = jnp.concatenate([row[:, None] * inv_freq, col[:, None] * inv_freq], axis=-1)
    return jnp.cos(ang), jnp.sin(ang)

def _apply_rope(x, cos, sin):
    half = x.shape[-1] // 2
    x1, x2 = x[..., :half], x[..., half:]
    cos = cos[:, None, None, :].astype(x.dtype)
    sin = sin[:, None, None, :].astype(x.dtype)
    return jnp.concatenate([x1 * cos - x2 * sin, x2 * cos + x1 * sin], axis=-1)

def _diff_attention(p_ctx, p_lat, lam_vecs, norm_g, layer):
    lam_init = 0.8 - 0.6 * math.exp(-0.3 * layer)
    lv = lam_vecs.astype(jnp.float32)
    lam = jnp.exp(jnp.sum(lv[0] * lv[1])) - jnp.exp(jnp.sum(lv[2] * lv[3])) + lam_init

    def qkv(p):
        B, T = p.shape[:2]
        q, k, v = _split(p, DIFF_COLS)
        return (q.reshape(B, T, N_HEADS, 2, DIFF_QK_DIM), k.reshape(B, T, N_HEADS, 2, DIFF_QK_DIM),
                v.reshape(B, T, N_HEADS, HEAD_DIM))

    qc, kc, vc = qkv(p_ctx)
    ql, kl, vl = qkv(p_lat)
    B, N = p_lat.shape[:2]
    cos, sin = _axial_rope(N)
    ql, kl = _apply_rope(ql, cos, sin), _apply_rope(kl, cos, sin)
    scale = DIFF_QK_DIM ** -0.5

    def attend(q, k, v):
        s = jnp.einsum('bqhcd,bkhcd->bhcqk', q, k).astype(jnp.float32) * scale
        pr = jax.nn.softmax(s, axis=-1)
        pr = pr[:, :, 0] - lam * pr[:, :, 1]
        return jnp.einsum('bhqk,bkhd->bqhd', pr.astype(v.dtype), v)

    y_ctx = attend(qc, kc, vc)
    k_all = jnp.concatenate([kc, kl], axis=1)
    v_all = jnp.concatenate([vc, vl], axis=1)
    nblk = N // ATTN_BLOCK
    qb = jnp.moveaxis(ql.reshape(B, nblk, ATTN_BLOCK, N_HEADS, 2, DIFF_QK_DIM), 1, 0)
    y_lat = lax.map(lambda q: attend(q, k_all, v_all), qb)
    y_lat = jnp.moveaxis(y_lat, 0, 1).reshape(B, N, N_HEADS, HEAD_DIM)

    def finish(y):
        return (_norm(y, norm_g, rms=True) * (1.0 - lam_init)).reshape(y.shape[0], y.shape[1], GROUP_WIDTH)

    return finish(y_ctx), finish(y_lat)

def _gla_chunk_scan(inputs, state):
    q, k, v, logf = (t.astype(jnp.float32) for t in inputs)
    causal = jnp.tril(jnp.ones((CHUNK, CHUNK), dtype=bool))

    def step(S, blk):
        qc, kc, vc, gc = blk
        b = jnp.cumsum(gc, axis=2)
        diff = b[:, :, :, None, :] - b[:, :, None, :, :]
        pair_decay = jnp.where(causal[:, :, None], jnp.exp(jnp.minimum(diff, 0.0)), 0.0)
        att = jnp.einsum('bhtd,bhsd,bhtsd->bhts', qc, kc, pair_decay)
        o = jnp.einsum('bhtd,bhdv->bhtv', qc * jnp.exp(b), S) + jnp.einsum('bhts,bhsv->bhtv', att, vc)
        b_end = b[:, :, -1:, :]
        S = jnp.exp(b_end[:, :, 0, :, None]) * S + jnp.einsum('bhsd,bhsv->bhdv', kc * jnp.exp(b_end - b), vc)
        return S, o

    S, o = lax.scan(step, state, tuple(_to_chunks(t) for t in (q, k, v, logf)))
    return S, _from_chunks(o)

def _hgrn2_features(p, lb):
    q, f_f, f_b, i, g = _split(p, HGRN_COLS)
    qh, ih = _heads(jax.nn.silu(q)), _heads(i)
    log_lb, log_1mlb = jnp.log(jnp.maximum(lb, LB_FLOOR)), jnp.log1p(-lb)
    dirs = []
    for f in (f_f, f_b):
        f = f.astype(jnp.float32)
        logf = jnp.logaddexp(log_lb, log_1mlb + jax.nn.log_sigmoid(f))
        k = (1.0 - lb) * jax.nn.sigmoid(-f)
        dirs.append((qh, _heads(k), ih, _heads(logf)))
    return g, dirs

def _hgrn2_mixer(p_ctx, p_lat, lb, norm_g):
    g_c, dirs_c = _hgrn2_features(p_ctx, lb)
    g_l, dirs_l = _hgrn2_features(p_lat, lb)
    init = jnp.zeros((p_lat.shape[0], N_HEADS, HEAD_DIM, HEAD_DIM), jnp.float32)
    o_c, o_l = _bidir_scan(_gla_chunk_scan, dirs_c, dirs_l, init)
    out = lambda o, g: _norm(o, norm_g, rms=True).reshape(g.shape) * jax.nn.silu(g)
    return out(o_c, g_c), out(o_l, g_l)

def _mlstm_chunk_scan(inputs, state):
    q, k, v, ig, logf = (t.astype(jnp.float32) for t in inputs)
    causal = jnp.tril(jnp.ones((CHUNK, CHUNK), dtype=bool))

    def step(carry, blk):
        C, n, m = carry
        qc, kc, vc, ic, fc = blk
        b = jnp.cumsum(fc, axis=-1)
        log_w = jnp.where(causal, b[..., :, None] - b[..., None, :] + ic[..., None, :], MASK_NEG)
        log_inter = b + m[..., None]
        m_t = jnp.maximum(log_inter, jnp.max(log_w, axis=-1))
        w = jnp.exp(log_w - m_t[..., None]) * jnp.einsum('bhtd,bhsd->bhts', qc, kc)
        w_inter = jnp.exp(log_inter - m_t)
        num = w_inter[..., None] * jnp.einsum('bhtd,bhdv->bhtv', qc, C) + jnp.einsum('bhts,bhsv->bhtv', w, vc)
        den = w_inter * jnp.einsum('bhtd,bhd->bht', qc, n) + jnp.sum(w, axis=-1)
        floor = jnp.exp(jnp.minimum(-m_t, MAX_NEG_LOG_STAB))
        h = num / jnp.maximum(jnp.abs(den), floor)[..., None]
        m_new = m_t[..., -1]
        kw = kc * jnp.exp(b[..., -1:] - b + ic - m_new[..., None])[..., None]
        decay = jnp.exp(b[..., -1] + m - m_new)
        C = decay[..., None, None] * C + jnp.einsum('bhsd,bhsv->bhdv', kw, vc)
        n = decay[..., None] * n + jnp.sum(kw, axis=2)
        return (C, n, m_new), h

    state, h = lax.scan(step, state, tuple(_to_chunks(t) for t in (q, k, v, ig, logf)))
    return state, _from_chunks(h)

def _mlstm_features(p, conv_w, conv_b, gate_b):
    q, k, v, o, i_f, i_b, f_f, f_b = _split(p, MLSTM_COLS)
    qk = jax.nn.silu(_dwconv3(jnp.concatenate([q, k], axis=-1), conv_w, conv_b))
    q, k = jnp.split(qk, 2, axis=-1)
    qh, kh, vh = _heads(q), _heads(k) * HEAD_DIM ** -0.5, _heads(v)
    dirs = ((qh, kh, vh, i_f + gate_b[0], jax.nn.log_sigmoid((f_f + gate_b[2]).astype(jnp.float32))),
            (qh, kh, vh, i_b + gate_b[1], jax.nn.log_sigmoid((f_b + gate_b[3]).astype(jnp.float32))))
    return o, dirs

def _mlstm_mixer(p_ctx, p_lat, conv_w, conv_b, gate_b, norm_g):
    o_c, dirs_c = _mlstm_features(p_ctx, conv_w, conv_b, gate_b)
    o_l, dirs_l = _mlstm_features(p_lat, conv_w, conv_b, gate_b)
    B = p_lat.shape[0]
    init = (jnp.zeros((B, N_HEADS, HEAD_DIM, HEAD_DIM), jnp.float32),
            jnp.zeros((B, N_HEADS, HEAD_DIM), jnp.float32),
            jnp.zeros((B, N_HEADS), jnp.float32))
    h_c, h_l = _bidir_scan(_mlstm_chunk_scan, dirs_c, dirs_l, init)
    gn = norm_g.reshape(N_HEADS, HEAD_DIM)
    out = lambda h, o: _norm(h, gn).reshape(o.shape) * jax.nn.sigmoid(o)
    return out(h_c, o_c), out(h_l, o_l)

def _conv_ffn(h, w_up, conv_w, conv_b, w_down):
    gate, val = jnp.split(h @ w_up, 2, axis=-1)
    return (jax.nn.gelu(_dwconv3(gate, conv_w, conv_b)) * val) @ w_down

def setup_inputs(seed: int = 0) -> dict:
    key = jax.random.key(seed)
    keys = iter(jax.random.split(key, 48))
    f32 = jnp.float32

    def nrm(shape, scale):
        return jax.random.normal(next(keys), shape, f32) * scale

    def unif(shape, lo, hi):
        return jax.random.uniform(next(keys), shape, f32, lo, hi)

    L, D, GW = DEPTH, D_MODEL, GROUP_WIDTH
    centre_tap = jnp.array([0.0, 1.0, 0.0], f32)[:, None]
    gate_slot = jnp.array([0.0, 0.0, 1.0, 0.0, 0.0, 1.0], f32)[None, :, None]
    return {
        'x': nrm((BATCH, SEQ, D), 1.0),
        'c': nrm((BATCH, D), 1.0),
        'ctx': nrm((BATCH, CTX_LEN, D), 1.0),
        'c_ctx': nrm((D,), 1.0),
        'ada_w': nrm((L, D, 6 * D), 0.2 * D ** -0.5),
        'ada_b': (nrm((L, 6, D), 0.02) + gate_slot).reshape(L, 6 * D),
        'w_in': nrm((L, D, IN_COLS), D ** -0.5),
        'rwkv_mu': unif((L, sum(RWKV_COLS)), 0.0, 1.0),
        'rwkv_w0': unif((L, 2, GW), -6.0, -1.0),
        'rwkv_w2': nrm((L, 2, RWKV_DECAY_LORA, GW), 0.5 * RWKV_DECAY_LORA ** -0.5),
        'rwkv_a0': nrm((L, 2, GW), 0.3),
        'rwkv_a2': nrm((L, 2, RWKV_ICLR_LORA, GW), 0.5 * RWKV_ICLR_LORA ** -0.5),
        'rwkv_g2': nrm((L, RWKV_GATE_LORA, GW), RWKV_GATE_LORA ** -0.5),
        'rwkv_k_k': 0.85 + nrm((L, GW), 0.02),
        'rwkv_k_a': 1.0 + nrm((L, GW), 0.02),
        'rwkv_r_k': nrm((L, GW), 0.1),
        'rwkv_lnx_g': 1.0 + nrm((L, GW), 0.02),
        'rwkv_lnx_b': nrm((L, GW), 0.02),
        'diff_lambda': nrm((L, 4, DIFF_QK_DIM), 0.1),
        'diff_norm_g': 1.0 + nrm((L, HEAD_DIM), 0.02),
        'hgrn_lb_logits': nrm((L, GW), 0.1),
        'hgrn_norm_g': 1.0 + nrm((L, HEAD_DIM), 0.02),
        'mlstm_conv_w': nrm((L, 3, 2 * GW), 0.3) + centre_tap,
        'mlstm_conv_b': nrm((L, 2 * GW), 0.02),
        'mlstm_gate_b': jnp.concatenate([nrm((L, 2, N_HEADS), 0.1), unif((L, 2, N_HEADS), 3.0, 6.0)], axis=1),
        'mlstm_norm_g': 1.0 + nrm((L, GW), 0.02),
        'w_out': nrm((L, MIX_WIDTH, D), DEEPNORM_BETA * MIX_WIDTH ** -0.5),
        'ffn_w_up': nrm((L, D, 2 * D_FF), D ** -0.5),
        'ffn_conv_w': nrm((L, 3, D_FF), 0.3) + centre_tap,
        'ffn_conv_b': nrm((L, D_FF), 0.02),
        'ffn_w_down': nrm((L, D_FF, D), DEEPNORM_BETA * D_FF ** -0.5),
        'ln_g': 1.0 + nrm((L, 2, D), 0.02),
        'ln_b': nrm((L, 2, D), 0.02),
    }

def reference(x, c, ctx, c_ctx, ada_w, ada_b, w_in, rwkv_mu, rwkv_w0, rwkv_w2, rwkv_a0, rwkv_a2, rwkv_g2,
              rwkv_k_k, rwkv_k_a, rwkv_r_k, rwkv_lnx_g, rwkv_lnx_b, diff_lambda, diff_norm_g, hgrn_lb_logits,
              hgrn_norm_g, mlstm_conv_w, mlstm_conv_b, mlstm_gate_b, mlstm_norm_g, w_out, ffn_w_up, ffn_conv_w,
              ffn_conv_b, ffn_w_down, ln_g, ln_b):
    lb_w = jax.nn.softmax(hgrn_lb_logits.astype(jnp.float32), axis=0)
    lower_bounds = jnp.cumsum(lb_w, axis=0) - lb_w[0]
    h_x, h_c = x, ctx
    for layer in range(DEPTH):
        mod_lat = _adaln(c, ada_w[layer], ada_b[layer])
        mod_ctx = _adaln(c_ctx[None, :], ada_w[layer], ada_b[layer])
        p_lat = _split(_modulate(h_x, mod_lat[0], mod_lat[1]) @ w_in[layer], GROUP_COLS)
        p_ctx = _split(_modulate(h_c, mod_ctx[0], mod_ctx[1]) @ w_in[layer], GROUP_COLS)
        y_a = _rwkv7_mixer(p_ctx[0], p_lat[0], rwkv_mu[layer], rwkv_w0[layer], rwkv_w2[layer], rwkv_a0[layer],
                           rwkv_a2[layer], rwkv_g2[layer], rwkv_k_k[layer], rwkv_k_a[layer], rwkv_r_k[layer],
                           rwkv_lnx_g[layer], rwkv_lnx_b[layer])
        y_b = _diff_attention(p_ctx[1], p_lat[1], diff_lambda[layer], diff_norm_g[layer], layer)
        y_c = _hgrn2_mixer(p_ctx[2], p_lat[2], lower_bounds[layer], hgrn_norm_g[layer])
        y_d = _mlstm_mixer(p_ctx[3], p_lat[3], mlstm_conv_w[layer], mlstm_conv_b[layer], mlstm_gate_b[layer],
                           mlstm_norm_g[layer])

        def sublayers(h, mod, side):
            y = jnp.concatenate([y_a[side], y_b[side], y_c[side], y_d[side]], axis=-1) @ w_out[layer]
            h = _norm(DEEPNORM_ALPHA * h + mod[2] * y, ln_g[layer, 0], ln_b[layer, 0])
            f = _conv_ffn(_modulate(h, mod[3], mod[4]), ffn_w_up[layer], ffn_conv_w[layer], ffn_conv_b[layer],
                          ffn_w_down[layer])
            return _norm(DEEPNORM_ALPHA * h + mod[5] * f, ln_g[layer, 1], ln_b[layer, 1])

        if layer < DEPTH - 1:
            h_c = sublayers(h_c, mod_ctx, 0)
        h_x = sublayers(h_x, mod_lat, 1)
    return h_x


_drawn_inputs = setup_inputs


def setup_inputs(seed=0):
    import zlib

    import numpy as np

    out = dict(_drawn_inputs(seed))
    spreads = {}
    factors = {'rwkv_w2': 8.0,
     'rwkv_a0': 3.618,
     'rwkv_k_k': 38.143,
     'rwkv_k_a': 8.0,
     'rwkv_lnx_g': 35.673,
     'rwkv_lnx_b': 25.909,
     'diff_lambda': 5.516,
     'diff_norm_g': 8.0,
     'hgrn_lb_logits': 8.0,
     'hgrn_norm_g': 32.388,
     'mlstm_conv_b': 8.0,
     'mlstm_norm_g': 31.027,
     'ffn_conv_b': 8.0}
    for name, (base, spread) in spreads.items():
        noise = np.random.default_rng([zlib.crc32(name.encode()), seed]).standard_normal(out[name].shape)
        drawn = base * np.exp(spread * noise) if base else spread * noise
        out[name] = jnp.asarray(drawn.astype(out[name].dtype))
    for name, factor in factors.items():
        out[name] = (out[name] * factor).astype(out[name].dtype)
    return out
```

```python
from contextlib import ExitStack

import numpy as np
import concourse.bass as bass
from concourse import mybir

F32 = mybir.dt.float32
I32 = mybir.dt.int32
ALU = mybir.AluOpType
ACT = mybir.ActivationFunctionType
AX_X = mybir.AxisListType.X

P = 128
D = 1024
KD = D // P
SIDE = 256
T = 2 * SIDE
TILES = T // P
DEPTH = 2
HEADS = 4
HD = 64
FF = 2816
KF = FF // P
ALPHA = (2.0 * DEPTH) ** 0.25
LN_EPS = 1e-5
LNX_EPS = 64e-5
ORDER = ((0, 1, 2, 3), (1, 0, 3, 2))
LEVELS = 7

T_R, T_K, T_V, T_WD, T_AD, T_GD, T_GD2 = 0, 2, 4, 6, 7, 8, 9
GATE_ROW = 32
T_DQ, T_DK, T_DV = 10, 12, 14
T_HQ, T_HF, T_HB, T_HI, T_HG = 16, 18, 20, 22, 24
T_MQ, T_MK, T_MV, T_MO = 26, 28, 30, 32
IN_TILES = 34

C_ID = 0
C_TRI = C_ID + P
C_STRICT = C_TRI + 2 * P
C_BASE = C_STRICT + 2 * P
C_ONES = C_BASE + 2 * P
C_HONES = C_ONES + P
C_ROT = C_HONES + P
C_COS = C_ROT + P
C_SIN = C_COS + SIDE
C_LEVEL = C_SIN + SIDE
C_SELH = C_LEVEL + 2 * LEVELS * P
C_SELP = C_SELH + HEADS * P
C_SEL2 = C_SELP + 2 * P
N_CONST = C_SEL2 + 2 * P

_o = 0


def _cols(n):
    global _o
    _o += n
    return _o - n


Q_MU, Q_W0, Q_A0, Q_KK, Q_KA, Q_RK, Q_XG, Q_XB = (_cols(n) for n in (10, 4, 4, 2, 2, 2, 2, 2))
Q_DN, Q_HN, Q_LB, Q_MCW, Q_MCB, Q_MN = (_cols(n) for n in (1, 1, 4, 12, 4, 2))
Q_FCW, Q_FCB, Q_GB, Q_LAM, Q_EPS, Q_LORA = (_cols(n) for n in (3 * KF, KF, 16, 128, 4, 1024))
N_PAR = _o


class Stage:

    zeroed, made = [], 0

    def __init__(self, nc):
        Stage.made += 1
        self.nc, self.sems, self.tag = nc, {}, Stage.made

    def __enter__(self):
        return self

    def __call__(self, name):
        if name not in self.sems:
            self.sems[name] = self.nc.alloc_semaphore(f"{name}_{self.tag}")
        return self.sems[name]

    def __exit__(self, *exc):
        if exc[0] is None:
            for sem in Stage.zeroed:
                self.nc.release_semaphore(sem)
            for sem in self.sems.values():
                self.nc.sync.sem_clear(sem)
            Stage.zeroed = list(self.sems.values())


def linker(eng, sem):
    count = [0]

    def link(ins):
        count[0] += 1
        ins.then_inc(sem, 1)
        eng.wait_ge(sem, count[0])

    return link


def build(nc, A, out):
    Stage.zeroed, Stage.made = [], 0
    with ExitStack() as ctx:
        def sb(name, cols):
            return ctx.enter_context(nc.sbuf_tensor(name, [P, cols], F32))

        const = sb("const", N_CONST)
        par = sb("par", N_PAR)
        h = sb("h", TILES * D)
        pr = sb("pr", IN_TILES * T)
        work = sb("work", 13312)
        mix = sb("mix", KD * T)
        ring = sb("ring", 4 * KD * P)
        gate = sb("gate", 4 * D)
        modc = sb("modc", 48 * 2)
        cond = sb("cond", KD * 2)
        fcol = sb("fcol", 16)
        ps = [ctx.enter_context(nc.psum_tensor(f"ps{i}", [P, 512], F32)) for i in range(8)]

        def c(o, n=P, rows=P):
            return const[0:rows, o:o + n]

        ident = c(C_ID)
        stored = ctx.enter_context(nc.semaphore("stored"))
        E = dict(stored=stored, nc=nc, A=A, out=out, c=c, const=const, ident=ident, par=par, h=h, pr=pr, work=work, mix=mix,
                 ring=ring, gate=gate, modc=modc, cond=cond, fcol=fcol, ps=ps)
        load_inputs(E)
        for layer in range(DEPTH):
            adaln(E, layer)
            input_projection(E, layer)
            conv_and_sigmoids(E, layer)
            diff_attention(E, layer)
            mlstm(E, layer)
            hgrn(E, layer)
            rwkv(E, layer)
            output_projection(E, layer)
            ffn(E, layer)
        store_output(E)


def load_inputs(E):
    nc, A, par, const, h, cond, ps = (E[k] for k in ("nc", "A", "par", "const", "h", "cond", "ps"))
    work = E["work"]
    with Stage(nc) as S, nc.Block() as block:
        S("in"); S("c")

        @block.sync
        def _(sp):
            sp.dma_start(cond[:, :], A["cond"]).then_inc(S("c"), 16)
            sp.dma_start(const[:, :], A["const"]).then_inc(S("in"), 16)
            sp.dma_start(h[:, :].rearrange("p (j d) -> p j d", j=TILES)[:, 0:2, :],
                         A["ctx"].rearrange("(j p) d -> p j d", p=P)).then_inc(S("in"), 16)
            sp.dma_start(h[:, :].rearrange("p (j d) -> p j d", j=TILES)[:, 2:4, :],
                         A["x"].rearrange("(j p) d -> p j d", p=P)).then_inc(S("in"), 16)
            sp.wait_ge(S("in"), 48)

        @block.scalar
        def _(act):
            act.wait_ge(S("c"), 16)
            nc.scalar.activation(work[:, 0:16], cond[:, :], ACT.Sigmoid).then_inc(S("sig"), 1)

        @block.vector
        def _(dve):
            dve.wait_ge(S("sig"), 1)
            nc.vector.tensor_tensor(cond[:, :], cond[:, :], work[:, 0:16], ALU.mult)


def adaln(E, layer):
    nc, A, c, par, pr, gate, modc, cond, ps, work = (
        E[k] for k in ("nc", "A", "c", "par", "pr", "gate", "modc", "cond", "ps", "work"))
    NB, SLOTS, W = 12, 4, KD * 512
    rows = work[0:2, 0:2 * 512]
    bias = work[0:2, 1024:1024 + NB * 512]
    with Stage(nc) as S, nc.Block() as block:
        S("link")

        @block.sync
        def _(sp):
            sp.dma_start(bias, A["ada_b"][layer]).then_inc(S("bias"), 16)
            sp.dma_start(par[:, :], A["par"][layer]).then_inc(S("par"), 16)
            for n in range(NB):
                if n >= SLOTS:
                    sp.wait_ge(S("mm"), n - SLOTS + 1)
                sp.dma_start(pr[:, (n % SLOTS) * W:(n % SLOTS + 1) * W],
                             A["ada_w"][layer, n]).then_inc(S(f"w{n % SLOTS}"), 16)
            sp.wait_ge(S("par"), 16)

        @block.tensor
        def _(pe):
            def products(n):
                pe.wait_ge(S(f"w{n % SLOTS}"), 16 * (n // SLOTS + 1))
                if n >= 2:
                    pe.wait_ge(S("row"), n - 1)
                for k in range(KD):
                    mm = nc.tensor.matmul(ps[n % 2][0:2, :], cond[:, 2 * k:2 * k + 2],
                                          pr[:, (n % SLOTS) * W + k * 512:(n % SLOTS) * W + (k + 1) * 512],
                                          start=(k == 0), stop=(k == KD - 1))
                mm.then_inc(S("mm"), 1)

            def spread(n):
                pe.wait_ge(S("row"), n + 1)
                if n >= 1:
                    pe.wait_ge(S("spread_out"), n)
                row = rows[:, (n % 2) * 512:(n % 2 + 1) * 512]
                if n // 2 in (2, 5):
                    for side in range(2):
                        mm = nc.tensor.matmul(ps[2 + side][:, :], c(C_SEL2 + side * P, P, 2), row, start=True, stop=True)
                else:
                    for b in range(4):
                        mm = nc.tensor.matmul(ps[2][:, 2 * b:2 * b + 2], row[:, b * P:(b + 1) * P],
                                              c(C_ID, 2, 2), start=True, stop=True)
                mm.then_inc(S("spread"), 1)

            for n in range(NB):
                products(n)
                if n >= 1:
                    spread(n - 1)
            spread(NB - 1)

        @block.vector
        def _(dve):
            dve.wait_ge(S("bias"), 16)
            for n in range(NB + 1):
                if n < NB:
                    dve.wait_ge(S("mm"), n + 1)
                    if n >= 2:
                        dve.wait_ge(S("spread"), n - 1)
                    nc.vector.tensor_tensor(rows[:, (n % 2) * 512:(n % 2 + 1) * 512], ps[n % 2][0:2, :],
                                            bias[:, n * 512:(n + 1) * 512], ALU.add).then_inc(S("row"), 1)
                if n >= 1:
                    m = n - 1
                    dve.wait_ge(S("spread"), m + 1)
                    if m // 2 in (2, 5):
                        g = m // 2 // 3
                        for side in range(2):
                            o = (2 * g + side) * D + (m % 2) * 512
                            ins = nc.vector.tensor_copy(gate[:, o:o + 512], ps[2 + side][:, :])
                    else:
                        ins = nc.vector.tensor_scalar(modc[:, 8 * m:8 * m + 8], ps[2][:, 0:8],
                                                      1.0 if m // 2 in (1, 4) else 0.0, None, ALU.add)
                    ins.then_inc(S("spread_out"), 1)


def transpose_modulate(E, S, pe=None, dve=None, act=None, shift=0, scale=1):
    nc, h, ps, work, modc, ident = (E[k] for k in ("nc", "h", "ps", "work", "modc", "ident"))
    for k in range(KD):
        if pe:
            if k >= 4:
                pe.wait_ge(S(f"hT{k % 2}"), 2 * (k // 2 - 1))
            for j in range(TILES):
                mm = nc.tensor.transpose(ps[4 + k % 4][:, j * P:(j + 1) * P],
                                         h[:, j * D + k * P:j * D + (k + 1) * P], ident)
            mm.then_inc(S("turned"), 1)
        elif (k % 2 == 0) == bool(dve):
            (dve or act).wait_ge(S("turned"), k + 1)
            for side in range(2):
                o, i = work[:, k * T + side * SIDE:k * T + (side + 1) * SIDE], ps[4 + k % 4][:, side * SIDE:(side + 1) * SIDE]
                a = modc[:, (scale * KD + k) * 2 + side:(scale * KD + k) * 2 + side + 1]
                b = modc[:, (shift * KD + k) * 2 + side:(shift * KD + k) * 2 + side + 1]
                if dve:
                    nc.vector.tensor_scalar(o, i, a, b, ALU.mult, ALU.add).then_inc(S("hT0"), 1)
                else:
                    nc.scalar.activation(o, i, ACT.Identity, bias=b, scale=a).then_inc(S("hT1"), 1)


def input_projection(E, layer):
    nc, A, ps, work, pr, ring = (E[k] for k in ("nc", "A", "ps", "work", "pr", "ring"))
    SLOTS, W = 4, KD * P
    with Stage(nc) as S, nc.Block() as block:
        S("turned"); S("out0"); S("out1")

        @block.sync
        def _(sp):
            for m in range(IN_TILES):
                if m >= SLOTS:
                    sp.wait_ge(S("mm"), m - SLOTS + 1)
                sp.dma_start(ring[:, (m % SLOTS) * W:(m % SLOTS + 1) * W],
                             A["w_in"][layer, m]).then_inc(S(f"w{m % SLOTS}"), 16)

        @block.tensor
        def _(pe):
            transpose_modulate(E, S, pe=pe)
            pe.wait_ge(S("hT0"), KD)
            pe.wait_ge(S("hT1"), KD)
            for m in range(IN_TILES):
                pe.wait_ge(S(f"w{m % SLOTS}"), 16 * (m // SLOTS + 1))
                if m >= 4:
                    pe.wait_ge(S(f"out{m % 2}"), m // 2 - 1)
                for k in range(KD):
                    mm = nc.tensor.matmul(ps[m % 4][:, :], ring[:, (m % SLOTS) * W + k * P:(m % SLOTS) * W + (k + 1) * P],
                                          work[:, k * T:(k + 1) * T], start=(k == 0), stop=(k == KD - 1))
                mm.then_inc(S("mm"), 1)

        @block.vector
        def _(dve):
            transpose_modulate(E, S, dve=dve, shift=0, scale=1)
            for m in range(0, IN_TILES, 2):
                dve.wait_ge(S("mm"), m + 1)
                nc.vector.tensor_copy(pr[:, m * T:(m + 1) * T], ps[m % 4][:, :]).then_inc(S("out0"), 1)

        @block.scalar
        def _(act):
            transpose_modulate(E, S, act=act, shift=0, scale=1)
            for m in range(1, IN_TILES, 2):
                act.wait_ge(S("mm"), m + 1)
                nc.scalar.copy(pr[:, m * T:(m + 1) * T], ps[m % 4][:, :]).then_inc(S("out1"), 1)


def tiles(t, first, n):
    return t[:, first * T:(first + n) * T]


def sides(ap, n):
    return ap.rearrange("p (n s t) -> p n s t", n=n, s=2)


def conv_and_sigmoids(E, layer):
    nc, par, pr, work = (E[k] for k in ("nc", "par", "pr", "work"))
    with Stage(nc) as S, nc.Block() as block:
        S("link")
        sf = work[:, 0:4 * T]
        tmp = work[:, 4 * T:4 * T + 10 * T]

        @block.vector
        def _(dve):
            link = linker(dve, S("link"))

            def pc(o, i=0, rows=P):
                return par[0:rows, o + i:o + i + 1]

            t = tmp[:, 0:4 * T]
            z = tiles(pr, T_MQ, 4)
            for i in range(4):
                ins = nc.vector.tensor_scalar(tiles(t, i, 1), tiles(z, i, 1), pc(Q_MCW, 3 * i + 1), pc(Q_MCB, i), ALU.mult, ALU.add)
            link(ins)
            for i in range(4):
                zi, ti = sides(tiles(z, i, 1), 1)[:, 0], sides(tiles(t, i, 1), 1)[:, 0]
                ins = nc.vector.scalar_tensor_tensor(out=ti[:, :, 1:], in0=zi[:, :, :-1], scalar=pc(Q_MCW, 3 * i), in1=ti[:, :, 1:],
                                                     op0=ALU.mult, op1=ALU.add)
            link(ins)
            for i in range(4):
                zi, ti = sides(tiles(z, i, 1), 1)[:, 0], sides(tiles(t, i, 1), 1)[:, 0]
                ins = nc.vector.scalar_tensor_tensor(out=ti[:, :, :-1], in0=zi[:, :, 1:], scalar=pc(Q_MCW, 3 * i + 2), in1=ti[:, :, :-1],
                                                     op0=ALU.mult, op1=ALU.add)
            ins.then_inc(S("conv"), 1)
            dve.wait_ge(S("conv_sig"), 1)
            link(nc.vector.tensor_tensor(tiles(pr, T_MQ, 2), tiles(t, 0, 2), tiles(pr, T_MQ, 2), ALU.mult))
            link(nc.vector.scalar_tensor_tensor(out=tiles(pr, T_MK, 2), in0=tiles(t, 2, 2), scalar=HD ** -0.5, in1=tiles(pr, T_MK, 2),
                                                op0=ALU.mult, op1=ALU.mult))

            for first, n, rows in ((0, 9, P), (9, 1, 32)):
                z = sides(pr[0:rows, first * T:(first + n) * T], n)
                u = sides(tmp[0:rows, first * T:(first + n) * T], n)
                nc.vector.tensor_tensor(u[:, :, :, 1:-1], z[:, :, :, :-2], z[:, :, :, 2:], ALU.add)
                nc.vector.tensor_copy(u[:, :, :, 0], z[:, :, :, 1])
                ins = nc.vector.tensor_copy(u[:, :, :, SIDE - 1], z[:, :, :, SIDE - 2])
            link(ins)
            for first, n, rows in ((0, 9, P), (9, 1, 32)):
                z, u = pr[0:rows, first * T:(first + n) * T], tmp[0:rows, first * T:(first + n) * T]
                ins = nc.vector.scalar_tensor_tensor(out=u, in0=u, scalar=0.5, in1=z, op0=ALU.mult, op1=ALU.subtract)
            link(ins)
            for i in (6, 7, 8, 9, 0, 1, 2, 3, 4, 5):
                rows = P if i < 9 else 32
                z, u = pr[0:rows, i * T:(i + 1) * T], tmp[0:rows, i * T:(i + 1) * T]
                ins = nc.vector.scalar_tensor_tensor(out=z, in0=u, scalar=pc(Q_MU, i, rows), in1=z, op0=ALU.mult, op1=ALU.add)
                if i == 9:
                    ins.then_inc(S("shifted"), 1)
            ins.then_inc(S("tmp_free"), 1)
            for n, (t0, o) in enumerate(((T_HQ, 0), (T_HG, 2))):
                dve.wait_ge(S("silu_sig"), n + 1)
                nc.vector.tensor_tensor(tiles(pr, t0, 2), tiles(pr, t0, 2), tiles(tmp, o, 2), ALU.mult)

        @block.scalar
        def _(act):
            nc.scalar.activation(sf, tiles(pr, T_HF, 4), ACT.Sigmoid).then_inc(S("sf"), 1)
            nc.scalar.activation(tiles(pr, T_MO, 2), tiles(pr, T_MO, 2), ACT.Sigmoid)
            act.wait_ge(S("sf"), 1)
            nc.scalar.activation(tiles(pr, T_HF, 4), tiles(pr, T_HF, 4), ACT.Sigmoid, scale=-1.0)
            act.wait_ge(S("conv"), 1)
            nc.scalar.activation(tiles(pr, T_MQ, 4), tiles(tmp, 0, 4), ACT.Sigmoid).then_inc(S("conv_sig"), 1)
            act.wait_ge(S("shifted"), 1)
            nc.scalar.activation(tiles(pr, T_WD, 1), tiles(pr, T_WD, 1), ACT.Tanh)
            nc.scalar.activation(tiles(pr, T_GD, 1), tiles(pr, T_GD, 1), ACT.Sigmoid)
            nc.scalar.activation(pr[0:32, T_GD2 * T:(T_GD2 + 1) * T], pr[0:32, T_GD2 * T:(T_GD2 + 1) * T], ACT.Sigmoid)
            act.wait_ge(S("tmp_free"), 1)
            for t0, o in ((T_HQ, 0), (T_HG, 2)):
                nc.scalar.activation(tiles(tmp, o, 2), tiles(pr, t0, 2), ACT.Sigmoid).then_inc(S("silu_sig"), 1)


def active(layer):
    return (0, 1, 2, 3) if layer < DEPTH - 1 else (2, 3)


def span(layer):
    lo = active(layer)[0] * P
    return lo, T - lo


def two(t, layer):
    lo, n = span(layer)
    return t.rearrange("p (i t) -> p i t", i=2)[:, :, lo:]


def head_sums(E, pe, src, banks, layer):
    nc, c, ps = E["nc"], E["c"], E["ps"]
    lo, n = span(layer)
    for i in range(2):
        mm = nc.tensor.matmul(ps[banks[i]][:, lo:], c(C_HONES), src[:, i * T + lo:(i + 1) * T], start=True, stop=True)
    return mm


def diff_attention(E, layer):
    nc, A, c, par, pr, work, mix, ps, ident = (E[k] for k in ("nc", "A", "c", "par", "pr", "work", "mix", "ps", "ident"))
    act_tiles = active(layer)
    units = [(i, j, hh) for i in range(2) for j in act_tiles for hh in range(2)]
    lam_init = 0.8 - 0.6 * float(np.exp(-0.3 * layer))
    scale = (HD // 2) ** -0.5
    vT = work[:, 2048:2048 + 1024]
    e = work[:, 3072:3072 + 2048]
    prob = work[:, 5120:5120 + 1024]
    pT = work[:, 6144:6144 + 1024]
    rtmp = work[:, 7168:7168 + 1024]
    y = work[:, 8192:8192 + 1024]
    st = work[:, 9216:9216 + 256]
    sq = work[:, 9472:9472 + 1024]

    with Stage(nc) as S, nc.Block() as block:
        for n in ("link", "link_act"):
            S(n)

        def keys(j):
            return (0, SIDE) if j < 2 else (0, T)

        @block.tensor
        def _(pe):
            for m in range(4):
                mm = nc.tensor.matmul(ps[m // 2][:, (m % 2) * SIDE:(m % 2 + 1) * SIDE], c(C_ROT),
                                      pr[:, (T_DQ + m) * T + SIDE:(T_DQ + m + 1) * T], start=True, stop=True)
            mm.then_inc(S("rot"), 1)
            for j in range(TILES):
                for i in range(2):
                    mm = nc.tensor.transpose(ps[2 + j // 2][:, (j % 2) * 256 + i * P:(j % 2) * 256 + (i + 1) * P],
                                             pr[:, (T_DV + i) * T + j * P:(T_DV + i) * T + (j + 1) * P], ident)
            mm.then_inc(S("vT"), 1)
            pe.wait_ge(S("roped"), 1)
            pe.wait_ge(S("vT_out"), 1)

            def scores(u):
                i, j, hh = units[u]
                if u >= 1:
                    pe.wait_ge(S("exp"), 2 * u)
                lo, n = keys(j)
                for q in range(2):
                    r = hh * HD + q * 32
                    mm = nc.tensor.matmul(ps[q][:, 0:n], pr[r:r + 32, (T_DQ + i) * T + j * P:(T_DQ + i) * T + (j + 1) * P],
                                          pr[r:r + 32, (T_DK + i) * T:(T_DK + i) * T + n], start=True, stop=True,
                                          tile_position=(r, 0))
                mm.then_inc(S("scores"), 1)

            def turn(u):
                pe.wait_ge(S("prob"), u + 1)
                if u >= 2:
                    pe.wait_ge(S("pT"), u - 1)
                n = keys(units[u][1])[1]
                for b in range(n // P):
                    mm = nc.tensor.transpose(ps[2 + u % 2][:, b * P:(b + 1) * P],
                                             prob[:, (u % 2) * T + b * P:(u % 2) * T + (b + 1) * P], ident)
                mm.then_inc(S("turned"), 1)

            def values(u):
                i, j, hh = units[u]
                pe.wait_ge(S("pT"), u + 1)
                n = keys(j)[1] // P
                for b in range(n):
                    mm = nc.tensor.matmul(ps[4 + i][hh * HD:(hh + 1) * HD, j * P:(j + 1) * P],
                                          vT[:, b * 256 + i * P + hh * HD:b * 256 + i * P + (hh + 1) * HD],
                                          pT[:, (u % 2) * T + b * P:(u % 2) * T + (b + 1) * P],
                                          start=(b == 0), stop=(b == n - 1))
                mm.then_inc(S("values"), 1)

            for u in range(len(units) + 2):
                if u < len(units):
                    scores(u)
                if 1 <= u <= len(units):
                    turn(u - 1)
                if u >= 2:
                    values(u - 2)
            pe.wait_ge(S("sq"), 1)
            head_sums(E, pe, sq, (6, 7), layer).then_inc(S("ss"), 1)

        @block.vector
        def _(dve):
            link = linker(dve, S("link"))
            lam = par[:, Q_LAM:Q_LAM + 128].rearrange("p (a b d) -> p a b d", a=2, b=2)
            link(nc.vector.tensor_tensor(st[:, 0:64].rearrange("p (a d) -> p a d", a=2), lam[:, :, 0, :], lam[:, :, 1, :], ALU.mult))
            nc.vector.tensor_reduce(st[:, 64:66], st[:, 0:64].rearrange("p (a d) -> p a d", a=2), AX_X, ALU.add).then_inc(S("lam_in"), 1)
            cosb = c(C_COS, SIDE).rearrange("p (i t) -> p i t", i=1).to_broadcast([P, 4, SIDE])
            sinb = c(C_SIN, SIDE).rearrange("p (i t) -> p i t", i=1).to_broadcast([P, 4, SIDE])
            qk = tiles(pr, T_DQ, 4).rearrange("p (m t) -> p m t", m=4)[:, :, SIDE:]
            rt = rtmp.rearrange("p (m t) -> p m t", m=4)
            dve.wait_ge(S("rot"), 1)
            for b in range(2):
                nc.vector.tensor_tensor(rt[:, 2 * b:2 * b + 2, :], ps[b][:, :].rearrange("p (m t) -> p m t", m=2),
                                        sinb[:, 0:2, :], ALU.mult)
            link(nc.vector.tensor_tensor(qk, qk, cosb, ALU.mult))
            nc.vector.tensor_tensor(qk, qk, rt, ALU.add).then_inc(S("roped"), 1)
            dve.wait_ge(S("lam_exp"), 1)
            link(nc.vector.tensor_tensor(st[:, 68:69], st[:, 67:68], st[:, 66:67], ALU.subtract))
            link(nc.vector.tensor_scalar(st[:, 69:70], st[:, 68:69], -lam_init, None, ALU.add))

            def maxima(u):
                dve.wait_ge(S("scores"), u + 1)
                if u >= 2:
                    dve.wait_ge(S("exp"), 2 * u - 2)
                n = keys(units[u][1])[1]
                for q in range(2):
                    ins = nc.vector.tensor_reduce(st[:, 80 + 8 * (u % 2) + q:81 + 8 * (u % 2) + q], ps[q][:, 0:n], AX_X, ALU.max)
                link(ins)
                s = 80 + 8 * (u % 2)
                nc.vector.tensor_scalar(st[:, s + 2:s + 4], st[:, s:s + 2], -scale, None, ALU.mult).then_inc(S("max"), 1)

            def combine(u):
                s = 80 + 8 * (u % 2)
                n = keys(units[u][1])[1]
                dve.wait_ge(S("exp"), 2 * u + 2)
                link(nc.vector.reciprocal(st[:, s + 6:s + 8], st[:, s + 4:s + 6]))
                link(nc.vector.tensor_tensor(st[:, s + 7:s + 8], st[:, s + 7:s + 8], st[:, 69:70], ALU.mult))
                e0, e1 = (e[:, (u % 2) * 1024 + q * 512:(u % 2) * 1024 + q * 512 + n] for q in range(2))
                link(nc.vector.tensor_scalar(e1, e1, st[:, s + 7:s + 8], None, ALU.mult))
                if u >= 2:
                    dve.wait_ge(S("turned"), u - 1)
                nc.vector.scalar_tensor_tensor(out=prob[:, (u % 2) * T:(u % 2) * T + n], in0=e0, scalar=st[:, s + 6:s + 7], in1=e1,
                                               op0=ALU.mult, op1=ALU.add).then_inc(S("prob"), 1)

            for u in range(len(units) + 1):
                if u < len(units):
                    maxima(u)
                if u >= 1:
                    combine(u - 1)
            dve.wait_ge(S("values"), len(units))
            lo, n = span(layer)
            for i in range(2):
                ins = nc.vector.tensor_copy(y[:, i * T + lo:(i + 1) * T], ps[4 + i][:, lo:])
            link(ins)
            nc.vector.tensor_tensor(two(sq, layer), two(y, layer), two(y, layer), ALU.mult).then_inc(S("sq"), 1)
            dve.wait_ge(S("rn"), 1)
            link(nc.vector.tensor_tensor(two(y, layer), two(y, layer), two(sq, layer), ALU.mult))
            nc.vector.tensor_scalar(two(tiles(mix, 2, 2), layer), two(y, layer), par[:, Q_DN:Q_DN + 1], 1.0 - lam_init,
                                    ALU.mult, ALU.mult)

        @block.scalar
        def _(act):
            act.wait_ge(S("vT"), 1)
            nc.scalar.copy(vT[:, 0:512], ps[2][:, :])
            nc.scalar.copy(vT[:, 512:1024], ps[3][:, :]).then_inc(S("vT_out"), 1)
            act.wait_ge(S("lam_in"), 1)
            nc.scalar.activation(st[:, 66:68], st[:, 64:66], ACT.Exp).then_inc(S("lam_exp"), 1)

            def exps(u):
                s = 80 + 8 * (u % 2)
                n = keys(units[u][1])[1]
                act.wait_ge(S("max"), u + 1)
                if u >= 2:
                    act.wait_ge(S("prob"), u - 1)
                for q in range(2):
                    nc.scalar.activation(e[:, (u % 2) * 1024 + q * 512:(u % 2) * 1024 + q * 512 + n], ps[q][:, 0:n], ACT.Exp,
                                         bias=st[:, s + 2 + q:s + 3 + q], scale=scale,
                                         accum_out=st[:, s + 4 + q:s + 5 + q]).then_inc(S("exp"), 1)

            def pt_out(u):
                n = keys(units[u][1])[1]
                act.wait_ge(S("turned"), u + 1)
                if u >= 2:
                    act.wait_ge(S("values"), u - 1)
                nc.scalar.copy(pT[:, (u % 2) * T:(u % 2) * T + n], ps[2 + u % 2][:, 0:n]).then_inc(S("pT"), 1)

            for u in range(len(units) + 1):
                if u < len(units):
                    exps(u)
                if u >= 1:
                    pt_out(u - 1)
            inverse_rms(E, S, act, (6, 7), sq, layer, 1.0 / HD, Q_EPS)


def inverse_rms(E, S, act, banks, dst, layer, scale, eps):
    nc, ps, par = E["nc"], E["ps"], E["par"]
    lo, n = span(layer)
    act.wait_ge(S("ss"), 1)
    for i in range(2):
        ins = nc.scalar.activation(dst[:, i * T + lo:(i + 1) * T], ps[banks[i]][:, lo:], ACT.Ln, bias=par[:, eps:eps + 1], scale=scale)
    ins.then_inc(S("ln"), 1)
    act.wait_ge(S("ln"), 1)
    nc.scalar.activation(two(dst, layer), two(dst, layer), ACT.Exp, scale=-0.5).then_inc(S("rn"), 1)


def mlstm(E, layer):
    nc, c, par, pr, work, mix, ps, ident = (E[k] for k in ("nc", "c", "par", "pr", "work", "mix", "ps", "ident"))
    js = active(layer)
    lo0, n0 = span(layer)
    PADW = P + SIDE
    o = [2048]

    def take(n):
        o[0] += n
        return work[:, o[0] - n:o[0]]

    vT = take(1024)
    w = take(4096)
    x = take(1024)
    pad = take(3072)[0:4, :]
    brow = take(1024)[0:4, :]
    floor = pr[0:4, T_DQ * T:(T_DQ + 2) * T]
    small = pr[:, (T_DQ + 2) * T:(T_DQ + 3) * T]
    gt = small[:, 0:64].rearrange("p (j g) -> p j g", j=TILES)
    lf = small[:, 64:96]
    la, lb_, gc = small[:, 96:128], small[:, 128:160], small[:, 160:192]
    ys = tiles(pr, T_DQ + 3, 2)
    y = tiles(mix, 6, 2)
    sq = x

    def padded(d, pp):
        return pad[:, (2 * d + pp) * 2 * PADW:(2 * d + pp + 1) * 2 * PADW].rearrange("p (s t) -> p s t", s=2)

    def own(d, pp, shift=0):
        a = P - shift if d == 0 else shift
        return padded(d, pp)[:, :, a:a + SIDE]

    def reach(d, s):
        lo = s * P if d == 0 else (0 if s < 2 else SIDE)
        return max(lo, lo0), (T if (d == 0 or s != 2) else 3 * P)

    def earlier(d, j):
        return ORDER[d][:ORDER[d].index(j)]

    with Stage(nc) as S, nc.Block() as block:
        for n in ("link", "vT", "gates", "rows", "cols", "mb", "qk", "w", "values", "x", "e"):
            S(n)

        @block.tensor
        def _(pe):
            for j in range(TILES):
                mm = nc.tensor.transpose(ps[0][:, j * 64:(j + 1) * 64], pr[0:64, T_GD2 * T + j * P:T_GD2 * T + (j + 1) * P], c(C_ID, 64, 64))
            mm.then_inc(S("gates"), 1)
            for j in range(TILES):
                for i in range(2):
                    mm = nc.tensor.transpose(ps[1 + j // 2][:, (j % 2) * 256 + i * P:(j % 2) * 256 + (i + 1) * P],
                                             pr[:, (T_MV + i) * T + j * P:(T_MV + i) * T + (j + 1) * P], ident)
            mm.then_inc(S("vT"), 1)
            pe.wait_ge(S("lf"), 1)
            for d in range(2):
                for j in range(TILES):
                    out = ps[3 + d][0:4, j * P:(j + 1) * P]
                    for n, s in enumerate((*earlier(d, j), j)):
                        nc.tensor.matmul(out, lf[:, s * 8 + d * 4:s * 8 + d * 4 + 4], c(C_ONES) if s != j else c(C_TRI + d * P),
                                         start=(n == 0), stop=(s == j))
                for j in range(TILES):
                    nc.tensor.matmul(ps[5 + d][0:4, j * P:(j + 1) * P], gt[:, j, d * 4:d * 4 + 4], ident, start=True, stop=True)
            for d in range(2):
                for j in range(TILES):
                    out = ps[7][:, j * 8 + d * 4:j * 8 + d * 4 + 4]
                    for n, s in enumerate((*earlier(d, j), j)):
                        mm = nc.tensor.matmul(out, c(C_ONES) if s != j else c(C_TRI + d * P), lf[:, s * 8 + d * 4:s * 8 + d * 4 + 4],
                                              start=(n == 0), stop=(s == j))
            mm.then_inc(S("rows"), 1)
            pe.wait_ge(S("vT_out"), 1)

            def broadcasts(hd):
                if hd == 0:
                    pe.wait_ge(S("maxed"), 1)
                else:
                    pe.wait_ge(S("x"), 2 * TILES * hd)
                if hd == 2:
                    pe.wait_ge(S("pair_out"), 2)
                for d in range(2):
                    M = own(d, 0)[:, lo0 // SIDE:, :]
                    mm = nc.tensor.matmul(ps[d][:, lo0:], c(C_SELH + hd * P, P, 4), M, start=True, stop=True)
                mm.then_inc(S("mb"), 1)

            def qk(hd, s):
                n = TILES * hd + s
                if n >= 2:
                    pe.wait_ge(S("w"), 2 * (n - 1))
                r = (hd % 2) * HD
                i = hd // 2
                lo = lo0 if s < 2 else SIDE
                nc.tensor.matmul(ps[2 + s % 2][:, lo:], pr[r:r + HD, (T_MK + i) * T + s * P:(T_MK + i) * T + (s + 1) * P],
                                 pr[r:r + HD, (T_MQ + i) * T + lo:(T_MQ + i + 1) * T], start=True, stop=True).then_inc(S("qk"), 1)

            def values(hd):
                r = (hd % 2) * HD
                pe.wait_ge(S("w"), 2 * TILES * (hd + 1))
                pe.wait_ge(S("masked"), 1 + hd)
                if hd == 2:
                    pe.wait_ge(S("pair_out"), 2)
                for d in range(2):
                    for j in js:
                        seen = (*earlier(d, j), j)
                        for bank, lhs in ((4 + d, None), (6 + d, c(C_ONES, HD))):
                            for n, s in enumerate(seen):
                                l = lhs if lhs is not None else vT[:, s * 256 + hd * HD:s * 256 + (hd + 1) * HD]
                                mm = nc.tensor.matmul(ps[bank][r:r + HD, j * P:(j + 1) * P], l,
                                                      w[:, d * 2048 + s * T + j * P:d * 2048 + s * T + (j + 1) * P],
                                                      start=(n == 0), stop=(n == len(seen) - 1))
                mm.then_inc(S("values"), 1)

            for hd in range(HEADS):
                broadcasts(hd)
                for s in range(TILES):
                    qk(hd, s)
                values(hd)
                if hd % 2:
                    pe.wait_ge(S("floor"), 1)
                    for d in range(2):
                        mm = nc.tensor.matmul(ps[d][:, lo0:], c(C_SELP + (hd // 2) * P, P, 4), floor[:, d * T + lo0:(d + 1) * T],
                                              start=True, stop=True)
                    mm.then_inc(S("floor_b"), 1)
            pe.wait_ge(S("pair_out"), 4)
            head_sums(E, pe, y, (6, 7), layer).then_inc(S("mean"), 1)
            pe.wait_ge(S("sq"), 1)
            head_sums(E, pe, sq, (4, 5), layer).then_inc(S("ss"), 1)

        @block.gpsimd
        def _(pool):
            pool.memset(pad[:, :], 0.0).then_inc(S("pad0"), 1)
            for hd in range(HEADS):
                pool.wait_ge(S("w"), 2 * TILES * (hd + 1))
                for d in range(2):
                    for j in js:
                        b = w[:, d * 2048 + j * T + j * P:d * 2048 + j * T + (j + 1) * P]
                        ins = nc.gpsimd.tensor_tensor(b, b, c(C_TRI + d * P), ALU.mult)
                ins.then_inc(S("masked"), 1)

        @block.vector
        def _(dve):
            link = linker(dve, S("link"))
            dve.wait_ge(S("gates"), 1)
            gb = par[:, Q_GB:Q_GB + 16].rearrange("p (j g) -> p j g", j=1).to_broadcast([P, TILES, 16])
            g4 = small[:, 0:64].rearrange("p (j g) -> p j g", j=TILES)
            link(nc.vector.tensor_tensor(g4, ps[0][:, 0:256].rearrange("p (j g) -> p j g", j=TILES)[:, :, GATE_ROW:GATE_ROW + 16], gb, ALU.add))
            f = g4[:, :, 8:16]
            lf3, la3, lb3 = (v.rearrange("p (j g) -> p j g", j=TILES) for v in (lf, la, lb_))
            link(nc.vector.tensor_scalar(la3, f, -1.0, None, ALU.mult))
            link(nc.vector.tensor_tensor(la3, la3, f, ALU.min))
            nc.vector.tensor_scalar(lb3, f, 0.0, None, ALU.min).then_inc(S("absf"), 1)
            dve.wait_ge(S("lnf"), 1)
            nc.vector.tensor_tensor(lf3, lb3, la3, ALU.subtract).then_inc(S("lf"), 1)
            dve.wait_ge(S("pad0"), 1)
            dve.wait_ge(S("brow"), 1)
            for d in range(2):
                ins = nc.vector.tensor_tensor(own(d, 0), ps[5 + d][0:4, :].rearrange("p (s t) -> p s t", s=2),
                                              brow[:, d * T:(d + 1) * T].rearrange("p (s t) -> p s t", s=2), ALU.subtract)
            link(ins)
            nc.vector.tensor_tensor(gc.rearrange("p (j g) -> p j g", j=TILES), g4[:, :, 0:8],
                                    ps[7][:, 0:32].rearrange("p (j g) -> p j g", j=TILES), ALU.subtract)
            pp = 0
            for k in (1, 2, 4, 8, 16, 32, 64, 128):
                for d in range(2):
                    ins = nc.vector.tensor_tensor(own(d, 1 - pp), own(d, pp), own(d, pp, k), ALU.max)
                link(ins)
                pp = 1 - pp
            for d in range(2):
                end = own(d, 0)[:, 0, SIDE - 1:SIDE] if d == 0 else own(d, 0)[:, 0, 0:1]
                ins = nc.vector.tensor_scalar(own(d, 0)[:, 1, :], own(d, 0)[:, 1, :], end, 0.0, ALU.max, ALU.max)
            link(ins)
            for d in range(2):
                ins = nc.vector.tensor_scalar(own(d, 0)[:, 0, :], own(d, 0)[:, 0, :], 0.0, None, ALU.max)
            ins.then_inc(S("maxed"), 1)
            dve.wait_ge(S("maxed"), 1)
            for d in range(2):
                ins = nc.vector.tensor_tensor(floor[:, d * T:(d + 1) * T].rearrange("p (s t) -> p s t", s=2), own(d, 0),
                                              brow[:, d * T:(d + 1) * T].rearrange("p (s t) -> p s t", s=2), ALU.add)
            link(ins)
            nc.vector.tensor_scalar(floor, floor, -1.0, 60.0, ALU.mult, ALU.min).then_inc(S("floor_in"), 1)

            def exponents(hd, s):
                for d in range(2):
                    n = 2 * (TILES * hd + s) + d
                    if n >= 2:
                        dve.wait_ge(S("w"), n - 1)
                    a, b = reach(d, s)
                    nc.vector.tensor_scalar(x[:, d * T + a:d * T + b], ps[d][:, a:b], gc[:, s * 8 + d * 4 + hd:s * 8 + d * 4 + hd + 1],
                                            0.0, ALU.subtract, ALU.max).then_inc(S("x"), 1)

            def weights(hd, s):
                dve.wait_ge(S("qk"), TILES * hd + s + 1)
                if hd >= 1:
                    dve.wait_ge(S("values"), hd)
                for d in range(2):
                    dve.wait_ge(S("e"), 2 * (TILES * hd + s) + d + 1)
                    a, b = reach(d, s)
                    nc.vector.tensor_tensor(w[:, d * 2048 + s * T + a:d * 2048 + s * T + b], x[:, d * T + a:d * T + b],
                                            ps[2 + s % 2][:, a:b], ALU.mult).then_inc(S("w"), 1)

            for hd in range(HEADS):
                dve.wait_ge(S("mb"), hd + 1)
                for s in range(TILES):
                    exponents(hd, s)
                    weights(hd, s)
                if hd % 2:
                    i = hd // 2
                    dve.wait_ge(S("den"), 2 * (i + 1))
                    dve.wait_ge(S("floor_b"), i + 1)
                    for d in range(2):
                        yd = ys[:, d * T + lo0:(d + 1) * T]
                        link(nc.vector.tensor_tensor(yd, yd, ps[d][:, lo0:], ALU.max))
                        link(nc.vector.reciprocal(yd, yd))
                        ins = nc.vector.tensor_tensor(yd, yd, ps[4 + d][:, lo0:], ALU.mult)
                        ins.then_inc(S("pair_y"), 1)
                    dve.wait_ge(S("pair_y"), 2 * (i + 1))
                    nc.vector.tensor_tensor(y[:, i * T + lo0:(i + 1) * T], ys[:, lo0:T], ys[:, T + lo0:2 * T], ALU.add).then_inc(S("pair_out"), 2)
            dve.wait_ge(S("pair_out"), 4)
            dve.wait_ge(S("mean"), 1)
            for i in range(2):
                v = y[:, i * T + lo0:(i + 1) * T]
                ins = nc.vector.scalar_tensor_tensor(out=v, in0=ps[6 + i][:, lo0:], scalar=-1.0 / HD, in1=v, op0=ALU.mult, op1=ALU.add)
            link(ins)
            nc.vector.tensor_tensor(two(sq, layer), two(y, layer), two(y, layer), ALU.mult).then_inc(S("sq"), 1)
            dve.wait_ge(S("rn"), 1)
            link(nc.vector.tensor_tensor(two(y, layer), two(y, layer), two(sq, layer), ALU.mult))
            for i in range(2):
                v = y[:, i * T + lo0:(i + 1) * T]
                nc.vector.scalar_tensor_tensor(out=v, in0=v, scalar=par[:, Q_MN + i:Q_MN + i + 1],
                                               in1=pr[:, (T_MO + i) * T + lo0:(T_MO + i + 1) * T], op0=ALU.mult, op1=ALU.mult)

        @block.scalar
        def _(act):
            act.wait_ge(S("vT"), 1)
            nc.scalar.copy(vT[:, 0:512], ps[1][:, :])
            nc.scalar.copy(vT[:, 512:1024], ps[2][:, :]).then_inc(S("vT_out"), 1)
            act.wait_ge(S("absf"), 1)
            nc.scalar.activation(la, la, ACT.Exp).then_inc(S("link_act"), 1)
            act.wait_ge(S("link_act"), 1)
            nc.scalar.activation(la, la, ACT.Ln, bias=1.0).then_inc(S("lnf"), 1)
            act.wait_ge(S("rows"), 1)
            nc.scalar.copy(brow[:, 0:T], ps[3][0:4, :])
            nc.scalar.copy(brow[:, T:2 * T], ps[4][0:4, :]).then_inc(S("brow"), 1)
            act.wait_ge(S("floor_in"), 1)
            nc.scalar.activation(floor, floor, ACT.Exp).then_inc(S("floor"), 1)
            for hd in range(HEADS):
                for s in range(TILES):
                    for d in range(2):
                        act.wait_ge(S("x"), 2 * (TILES * hd + s) + d + 1)
                        a, b = reach(d, s)
                        nc.scalar.activation(x[:, d * T + a:d * T + b], x[:, d * T + a:d * T + b], ACT.Exp, scale=-1.0).then_inc(S("e"), 1)
                if hd % 2:
                    act.wait_ge(S("values"), hd + 1)
                    if hd == 3:
                        act.wait_ge(S("pair_out"), 2)
                    for d in range(2):
                        nc.scalar.activation(ys[:, d * T + lo0:(d + 1) * T], ps[6 + d][:, lo0:], ACT.Abs).then_inc(S("den"), 1)
            inverse_rms(E, S, act, (4, 5), sq, layer, 1.0 / HD, Q_EPS)


def hgrn(E, layer):
    nc, c, par, pr, work, mix, ps, ident, const = (E[k] for k in ("nc", "c", "par", "pr", "work", "mix", "ps", "ident", "const"))
    js = active(layer)
    lo0, n0 = span(layer)
    o = [0]

    def take(n):
        o[0] += n
        return work[:, o[0] - n:o[0]]

    cum = take(2048)
    lT = take(2048)
    vT = take(1024)
    at = take(4096)
    st = take(1024)
    A0 = take(3072)
    A1 = tiles(pr, T_DQ, 6)
    bufs = ((A0[:, 0:1024], A0[:, 1024:2048], A0[:, 2048:3072]), (A1[:, 0:1024], A1[:, 1024:2048], A1[:, 2048:3072]))
    qd = pr[:, T_MQ * T:(T_MQ + 4) * T]
    kd = pr[:, (T_MQ + 4) * T:(T_MQ + 8) * T]
    y = tiles(mix, 4, 2)
    sq = A0[:, 0:1024]
    col = tiles(mix, 0, 1)[:, 0:16]
    ecol = tiles(mix, 0, 1)[:, 16:32]
    nb = len(js) // 2
    steps = [(d, l) for l in range(LEVELS) for d in range(2)]

    with Stage(nc) as S, nc.Block() as block:
        for n in ("link", "at", "s_mm", "qf", "kf"):
            S(n)

        def end(d):
            return P - 1 if d == 0 else 0

        def blocks(t, l):
            return t.rearrange("p (i b t) -> p i b t", i=2, t=2 << l)[:, :, lo0 // (2 << l):, :]

        def half(t, l, second):
            h_ = 1 << l
            return blocks(t, l)[:, :, :, h_:] if second else blocks(t, l)[:, :, :, :h_]

        def later(t, d, l):
            return blocks(t, 0) if l == 0 else half(t, l, d == 0)

        def sooner(t, d, l):
            return blocks(t, 0) if l == 0 else half(t, l, d == 1)

        @block.tensor
        def _(pe):
            for j in range(TILES):
                for i in range(2):
                    mm = nc.tensor.transpose(ps[j // 2][:, (j % 2) * 256 + i * P:(j % 2) * 256 + (i + 1) * P],
                                             pr[:, (T_HI + i) * T + j * P:(T_HI + i) * T + (j + 1) * P], ident)
            mm.then_inc(S("vT"), 1)
            pe.wait_ge(S("logf"), 1)
            for d in range(2):
                for j in range(TILES):
                    for i in range(2):
                        mm = nc.tensor.transpose(ps[2 + 2 * d + j // 2][:, (j % 2) * 256 + i * P:(j % 2) * 256 + (i + 1) * P],
                                                 cum[:, (2 * d + i) * T + j * P:(2 * d + i) * T + (j + 1) * P], ident)
            mm.then_inc(S("lT"), 1)
            pe.wait_ge(S("lT_out"), 2)
            pe.wait_ge(S("vT_out"), 1)
            for d in range(2):
                for i in range(2):
                    for j in range(TILES):
                        mm = nc.tensor.matmul(ps[(6, 7, 0, 1)[2 * d + i]][:, j * P:(j + 1) * P],
                                              lT[:, (d * TILES + j) * 256 + i * P:(d * TILES + j) * 256 + (i + 1) * P],
                                              c(C_TRI + d * P), start=True, stop=True)
            mm.then_inc(S("cum"), 1)
            pe.wait_ge(S("kd"), 1)
            for d in range(2):
                for j in range(TILES):
                    for i in range(2):
                        mm = nc.tensor.transpose(ps[2 + 2 * d + j // 2][:, (j % 2) * 256 + i * P:(j % 2) * 256 + (i + 1) * P],
                                                 kd[:, (2 * d + i) * T + j * P:(2 * d + i) * T + (j + 1) * P], ident)
            mm.then_inc(S("kT"), 1)
            pe.wait_ge(S("kT_out"), 2)
            for d in range(2):
                for j in range(TILES):
                    for hd in range(HEADS):
                        r, i = (hd % 2) * HD, hd // 2
                        mm = nc.tensor.matmul(ps[6 + d][r:r + HD, (2 * j + i) * HD:(2 * j + i + 1) * HD],
                                              lT[:, (d * TILES + j) * 256 + hd * HD:(d * TILES + j) * 256 + (hd + 1) * HD],
                                              vT[:, j * 256 + hd * HD:j * 256 + (hd + 1) * HD], start=True, stop=True)
            mm.then_inc(S("kv"), 1)
            for n, (d, l) in enumerate(steps):
                pe.wait_ge(S("kf"), n + 1)
                for par_ in range(2):
                    if n >= 1:
                        pe.wait_ge(S("at"), nb * (2 * (n - 1) + par_ + 1))
                    for j in js:
                        for i in range(2):
                            r = par_ * HD
                            mm = nc.tensor.matmul(ps[2 * par_ + j // 2][:, (j % 2) * 256 + i * P:(j % 2) * 256 + (i + 1) * P],
                                                  bufs[d][2][r:r + HD, i * T + j * P:i * T + (j + 1) * P],
                                                  bufs[d][1][r:r + HD, i * T + j * P:i * T + (j + 1) * P], start=True, stop=True)
                    mm.then_inc(S("s_mm"), 1)
            pe.wait_ge(S("at"), 2 * nb * len(steps))
            for hd in range(HEADS):
                r, i = (hd % 2) * HD, hd // 2
                for j in js:
                    terms = []
                    for d in range(2):
                        terms.append((vT[:, j * 256 + hd * HD:j * 256 + (hd + 1) * HD],
                                      at[:, d * 2048 + (hd % 2) * 1024 + (2 * j + i) * P:d * 2048 + (hd % 2) * 1024 + (2 * j + i + 1) * P]))
                    for d in range(2):
                        if ORDER[d].index(j) > 0:
                            terms.append((st[r:r + HD, d * 512 + (2 * j + i) * HD:d * 512 + (2 * j + i + 1) * HD],
                                          qd[r:r + HD, (2 * d + i) * T + j * P:(2 * d + i) * T + (j + 1) * P]))
                    for n, (l, rh) in enumerate(terms):
                        mm = nc.tensor.matmul(ps[4 + i][r:r + HD, j * P:(j + 1) * P], l, rh, start=(n == 0), stop=(n == len(terms) - 1))
            mm.then_inc(S("y"), 1)
            pe.wait_ge(S("sq"), 1)
            head_sums(E, pe, sq, (6, 7), layer).then_inc(S("ss"), 1)

        @block.gpsimd
        def _(pool):
            nc.gpsimd.memset(at[:, :], 0.0).then_inc(S("at0"), 1)

        @block.vector
        def _(dve):
            link = linker(dve, S("link"))
            if layer == 0:
                link(nc.vector.memset(col[:, 0:2], 0.0))
            else:
                nc.vector.tensor_tensor(col[:, 4:6], par[:, Q_LB:Q_LB + 2], par[:, Q_LB + 2:Q_LB + 4], ALU.max).then_inc(S("lb_max"), 1)
                dve.wait_ge(S("lb_max"), 1)
                link(nc.vector.tensor_tensor(col[:, 6:8], par[:, Q_LB:Q_LB + 2], col[:, 4:6], ALU.subtract))
                nc.vector.tensor_tensor(col[:, 8:10], par[:, Q_LB + 2:Q_LB + 4], col[:, 4:6], ALU.subtract).then_inc(S("lb_in"), 1)
                dve.wait_ge(S("lb_exp"), 1)
                link(nc.vector.tensor_tensor(col[:, 10:12], col[:, 6:8], col[:, 8:10], ALU.add))
                link(nc.vector.reciprocal(col[:, 10:12], col[:, 10:12]))
                link(nc.vector.tensor_tensor(col[:, 0:2], col[:, 8:10], col[:, 10:12], ALU.mult))
            nc.vector.tensor_scalar(col[:, 2:4], col[:, 0:2], -1.0, 1.0, ALU.mult, ALU.add)
            nc.vector.tensor_scalar(col[:, 12:14], col[:, 0:2], 1e-30, None, ALU.max).then_inc(S("lb"), 1)
            dve.wait_ge(S("lb"), 1)
            for d in range(2):
                for i in range(2):
                    t = tiles(pr, T_HF + 2 * d + i, 1)
                    ins = nc.vector.tensor_scalar(t, t, col[:, 2 + i:3 + i], None, ALU.mult)
            link(ins)
            dve.wait_ge(S("lT"), 1)
            nc.vector.tensor_copy(lT[:, 0:512], ps[2][:, :])
            nc.vector.tensor_copy(lT[:, 512:1024], ps[3][:, :]).then_inc(S("lT_out"), 1)
            dve.wait_ge(S("cum"), 1)
            for n, b in enumerate((6, 7, 0, 1)):
                ins = nc.vector.tensor_copy(cum[:, n * T:(n + 1) * T], ps[b][:, :])
            ins.then_inc(S("cum_out"), 1)
            dve.wait_ge(S("cum_out"), 1)
            for d in range(2):
                cv = tiles(cum, 2 * d, 2).rearrange("p (b t) -> p b t", t=P)
                ev = cv[:, :, end(d):end(d) + 1].to_broadcast([P, 2 * TILES, P])
                ins = nc.vector.tensor_tensor(tiles(kd, 2 * d, 2).rearrange("p (b t) -> p b t", t=P), ev, cv, ALU.subtract)
            ins.then_inc(S("rest"), 1)

            def exponents(n):
                d, l = steps[n]
                cv, dv = blocks(tiles(cum, 2 * d, 2), l), blocks(bufs[d][0], l)
                ref = (1 << l) - 1 if d == 0 else 1 << l
                if n >= 2:
                    dve.wait_ge(S("exps"), n - 1)
                nc.vector.tensor_tensor(dv, cv, cv[:, :, :, ref:ref + 1].to_broadcast(list(cv.shape)),
                                        ALU.subtract).then_inc(S("dv"), 1)

            def factors(n):
                d, l = steps[n]
                dve.wait_ge(S("exps"), n + 1)
                nc.vector.tensor_tensor(later(bufs[d][1], d, l), later(bufs[d][1], d, l), later(tiles(pr, T_HQ, 2), d, l), ALU.mult)
                nc.vector.tensor_tensor(sooner(bufs[d][2], d, l), sooner(bufs[d][2], d, l), sooner(tiles(pr, T_HF + 2 * d, 2), d, l),
                                        ALU.mult).then_inc(S("kf"), 1)

            def collect(n):
                d, l = steps[n]
                m0 = C_BASE + d * P if l == 0 else C_LEVEL + (d * LEVELS + l) * P
                mask = c(m0).bitcast(I32).rearrange("p (b t) -> p b t", b=1).to_broadcast([P, 4, P])
                for q in range(2):
                    dve.wait_ge(S("s_mm"), 2 * n + q + 1)
                    for b in range(js[0] // 2, 2):
                        o_ = d * 2048 + q * 1024 + b * 512
                        nc.vector.copy_predicated(at[:, o_:o_ + 512].rearrange("p (b t) -> p b t", b=4), mask,
                                                  ps[2 * q + b][:, :].rearrange("p (b t) -> p b t", b=4)).then_inc(S("at"), 1)

            dve.wait_ge(S("kd_exp"), 1)
            nc.vector.tensor_tensor(kd, kd, tiles(pr, T_HF, 4), ALU.mult).then_inc(S("kd"), 1)
            for d in range(2):
                ins = nc.vector.tensor_tensor(tiles(qd, 2 * d, 2), tiles(qd, 2 * d, 2), tiles(pr, T_HQ, 2), ALU.mult)
            link(ins)
            dve.wait_ge(S("kT"), 1)
            nc.vector.tensor_copy(lT[:, 0:512], ps[2][:, :])
            nc.vector.tensor_copy(lT[:, 512:1024], ps[3][:, :]).then_inc(S("kT_out"), 1)
            dve.wait_ge(S("kv"), 1)
            for m in range(1, TILES):
                for d in range(2):
                    j0, j1 = ORDER[d][m - 1], ORDER[d][m]
                    for i in range(2):
                        new = st[:, d * 512 + (2 * j1 + i) * HD:d * 512 + (2 * j1 + i + 1) * HD]
                        old = st[:, d * 512 + (2 * j0 + i) * HD:d * 512 + (2 * j0 + i + 1) * HD]
                        kv = ps[6 + d][:, (2 * j0 + i) * HD:(2 * j0 + i + 1) * HD]
                        if m == 1:
                            ins = nc.vector.tensor_copy(new, kv)
                        else:
                            e_ = ecol[:, (2 * d + i) * TILES + j0:(2 * d + i) * TILES + j0 + 1]
                            ins = nc.vector.scalar_tensor_tensor(out=new, in0=old, scalar=e_, in1=kv, op0=ALU.mult, op1=ALU.add)
                link(ins)
            dve.wait_ge(S("at0"), 1)
            exponents(0)
            exponents(1)
            for n in range(len(steps)):
                factors(n)
                if n + 2 < len(steps):
                    exponents(n + 2)
                if n >= 1:
                    collect(n - 1)
            collect(len(steps) - 1)
            dve.wait_ge(S("y"), 1)
            for i in range(2):
                ins = nc.vector.tensor_copy(y[:, i * T + lo0:(i + 1) * T], ps[4 + i][:, lo0:])
            link(ins)
            nc.vector.tensor_tensor(two(sq, layer), two(y, layer), two(y, layer), ALU.mult).then_inc(S("sq"), 1)
            dve.wait_ge(S("rn"), 1)
            link(nc.vector.tensor_tensor(two(y, layer), two(y, layer), two(sq, layer), ALU.mult))
            for i in range(2):
                v = y[:, i * T + lo0:(i + 1) * T]
                nc.vector.scalar_tensor_tensor(out=v, in0=v, scalar=par[:, Q_HN:Q_HN + 1],
                                               in1=pr[:, (T_HG + i) * T + lo0:(T_HG + i + 1) * T], op0=ALU.mult, op1=ALU.mult)

        @block.scalar
        def _(act):
            if layer:
                act.wait_ge(S("lb_in"), 1)
                nc.scalar.activation(col[:, 6:10], col[:, 6:10], ACT.Exp).then_inc(S("lb_exp"), 1)
            act.wait_ge(S("vT"), 1)
            nc.scalar.copy(vT[:, 0:512], ps[0][:, :])
            nc.scalar.copy(vT[:, 512:1024], ps[1][:, :]).then_inc(S("vT_out"), 1)
            act.wait_ge(S("lb"), 1)
            for n in range(4):
                i = n % 2
                ins = nc.scalar.activation(tiles(cum, n, 1), tiles(cum, n, 1), ACT.Ln, bias=col[:, 12 + i:13 + i], scale=col[:, 2 + i:3 + i])
            ins.then_inc(S("logf"), 1)
            act.wait_ge(S("lT"), 1)
            nc.scalar.copy(lT[:, 1024:1536], ps[4][:, :])
            nc.scalar.copy(lT[:, 1536:2048], ps[5][:, :]).then_inc(S("lT_out"), 1)
            act.wait_ge(S("cum_out"), 1)
            nc.scalar.activation(qd, cum, ACT.Exp)
            for d in range(2):
                cv = tiles(cum, 2 * d, 2).rearrange("p (b t) -> p b t", t=P)
                nc.scalar.activation(ecol[:, 8 * d:8 * d + 8].rearrange("p (b t) -> p b t", t=1), cv[:, :, end(d):end(d) + 1], ACT.Exp)
            act.wait_ge(S("rest"), 1)
            nc.scalar.activation(kd, kd, ACT.Exp).then_inc(S("kd_exp"), 1)
            act.wait_ge(S("kT"), 1)
            nc.scalar.copy(lT[:, 1024:1536], ps[4][:, :])
            nc.scalar.copy(lT[:, 1536:2048], ps[5][:, :]).then_inc(S("kT_out"), 1)
            for n, (d, l) in enumerate(steps):
                act.wait_ge(S("dv"), n + 1)
                if n >= 2:
                    act.wait_ge(S("s_mm"), 2 * (n - 1))
                nc.scalar.activation(later(bufs[d][1], d, l), later(bufs[d][0], d, l), ACT.Exp)
                nc.scalar.activation(sooner(bufs[d][2], d, l), sooner(bufs[d][0], d, l), ACT.Exp, scale=-1.0).then_inc(S("exps"), 1)
            inverse_rms(E, S, act, (6, 7), sq, layer, 1.0 / HD, Q_EPS)


def rwkv(E, layer):
    nc, c, par, pr, work, mix, ring, ps, ident = (E[k] for k in ("nc", "c", "par", "pr", "work", "mix", "ring", "ps", "ident"))
    js = active(layer)
    lo0, n0 = span(layer)
    KAPPA = float(np.exp(-0.5))
    MID = P // 2
    o = [0]

    def take(n):
        o[0] += n
        return work[:, o[0] - n:o[0]]

    sg, sa, cum, tm = take(2048), take(2048), take(2048), take(2048)
    vT, kk, kT, Q, ct = take(1024), take(1024), take(1024), take(1024), take(1024)
    al, rr, be, ks = (ring[:, n * 1024:(n + 1) * 1024] for n in range(4))
    alT, beT = tm[:, 0:1024], tm[:, 1024:2048]
    free = tiles(pr, 10, 24)
    NT, AkT, RbT, RkT = (free[:, n * 2048:(n + 1) * 2048] for n in range(4))
    X, XT = free[:, 8192:10240], free[:, 10240:12288]
    t1 = tiles(pr, T_WD, 2)
    PT, Qp = t1, ct
    U, st = NT[:, 0:1024], NT[:, 1024:1536]
    y = tiles(mix, 0, 2)
    sq = al
    units = [(l, j) for l in range(1, LEVELS) for j in range(TILES)]
    NU = len(units)

    def mat(m, j, hd):
        return m[:, (j * HEADS + hd) * P:(j * HEADS + hd + 1) * P]

    def four(m, j):
        return m[:, j * 512:(j + 1) * 512]

    with Stage(nc) as S, nc.Block() as block:
        for n in ("link", "tT", "raw", "raw_out", "ct", "t1", "t1_out", "x_up", "d_mm", "u_mm", "s_mm", "u", "s"):
            S(n)
        fcol = E["fcol"]

        def turns(src, dst_banks, n=2):
            for j in range(TILES):
                for i in range(n):
                    mm = nc.tensor.transpose(ps[dst_banks[j // 2]][:, (j % 2) * 256 + i * P:(j % 2) * 256 + (i + 1) * P],
                                             src[:, i * T + j * P:i * T + (j + 1) * P], ident)
            return mm

        @block.tensor
        def _(pe):
            for d in range(2):
                for i in range(2):
                    for n, t in ((0, T_WD), (1, T_AD)):
                        mm = nc.tensor.matmul(ps[4 * n + 2 * d + i][:, :], par[d * 64:(d + 1) * 64, Q_LORA + n * 256 + i * P:Q_LORA + n * 256 + (i + 1) * P],
                                              pr[d * 64:(d + 1) * 64, t * T:(t + 1) * T], start=True, stop=True)
            mm.then_inc(S("lora"), 1)
            pe.wait_ge(S("sig"), 1)
            turns(sg[:, 0:1024], (0, 1))
            turns(sg[:, 1024:2048], (2, 3))
            turns(tiles(pr, T_V, 2), (4, 5)).then_inc(S("sT"), 1)
            pe.wait_ge(S("kk"), 1)
            for i in range(2):
                mm = nc.tensor.matmul(ps[6 + i][:, :], c(C_HONES), al[:, i * T:(i + 1) * T], start=True, stop=True)
            mm.then_inc(S("kk_ss"), 1)
            pe.wait_ge(S("sT_out"), 1)
            for d in range(2):
                for i in range(2):
                    for j in range(TILES):
                        mm = nc.tensor.matmul(ps[2 * d + i][:, j * P:(j + 1) * P], tm[:, (d * TILES + j) * 256 + i * P:(d * TILES + j) * 256 + (i + 1) * P],
                                              c(C_TRI + d * P), start=True, stop=True)
            mm.then_inc(S("cum"), 1)
            for d in range(2):
                pe.wait_ge(S("scaled"), d + 1)
                turns(al, (0, 1))
                turns(be, (2, 3))
                turns(ks, (4, 5)).then_inc(S("tT"), 1)
                pe.wait_ge(S("tT_out"), 2 * (d + 1))
                for j in range(TILES):
                    b0 = 4 * (j % 2)
                    if j >= 2:
                        pe.wait_ge(S("raw_out"), 2 * (TILES * d + j - 1))
                    for n, rh in enumerate((al, rr)):
                        for q in range(2):
                            for i in range(2):
                                for m, lh in enumerate((be, ks)):
                                    mm = nc.tensor.matmul(ps[b0 + 2 * n + q][:, (2 * m + i) * P:(2 * m + i + 1) * P],
                                                          lh[q * HD:(q + 1) * HD, i * T + j * P:i * T + (j + 1) * P],
                                                          rh[q * HD:(q + 1) * HD, i * T + j * P:i * T + (j + 1) * P], start=True, stop=True)
                        mm.then_inc(S("raw"), 1)
                pe.wait_ge(S("raw_out"), 2 * TILES * (d + 1))
                for j in range(TILES):
                    pe.wait_ge(S("x0T"), TILES * d + j + 1)
                    for hd in range(HEADS):
                        mm = nc.tensor.transpose(ps[j][:, hd * P:(hd + 1) * P], mat(X, j, hd), ident)
                    mm.then_inc(S("x0"), 1)

                def first(u):
                    l, j = units[u]
                    pe.wait_ge(S("ct"), NU * d + u + 1)
                    pe.wait_ge(S("x_up"), (NU + TILES) * d + u + 1)
                    if u >= 2:
                        pe.wait_ge(S("t1_out"), NU * d + u - 1)
                    else:
                        pe.wait_ge(S("x_up"), (NU + TILES) * d + TILES)
                    for hd in range(HEADS):
                        mm = nc.tensor.matmul(ps[u % 2][:, hd * P:(hd + 1) * P], ct[:, (u % 2) * 512 + hd * P:(u % 2) * 512 + (hd + 1) * P],
                                              mat(X, j, hd), start=True, stop=True)
                    mm.then_inc(S("t1"), 1)

                def second(u):
                    l, j = units[u]
                    pe.wait_ge(S("t1_out"), NU * d + u + 1)
                    if u >= 2:
                        pe.wait_ge(S("x_up"), (NU + TILES) * d + TILES + u - 1)
                    for hd in range(HEADS):
                        t = t1[:, (u % 2) * 512 + hd * P:(u % 2) * 512 + (hd + 1) * P]
                        nc.tensor.matmul(ps[4 + u % 2][:, hd * P:(hd + 1) * P], t, mat(XT, j, hd), start=True, stop=True)
                    for hd in range(HEADS):
                        t = t1[:, (u % 2) * 512 + hd * P:(u % 2) * 512 + (hd + 1) * P]
                        mm = nc.tensor.matmul(ps[2 + u % 2][:, hd * P:(hd + 1) * P], mat(XT, j, hd), t, start=True, stop=True)
                    mm.then_inc(S("d_mm"), 1)

                for u in range(NU + 1):
                    if u < NU:
                        first(u)
                    if u >= 1:
                        second(u - 1)
                pe.wait_ge(S("x_up"), (NU + TILES) * (d + 1))
                for i in range(2):
                    for j in range(TILES):
                        for q in range(2):
                            hd = 2 * i + q
                            nc.tensor.matmul(ps[6 + i][q * HD:(q + 1) * HD, j * P:(j + 1) * P],
                                             alT[:, j * 256 + hd * HD:j * 256 + (hd + 1) * HD], mat(XT, j, hd), start=True, stop=True)
                for j in range(TILES):
                    for hd in range(HEADS):
                        mm = nc.tensor.matmul(ps[j // 2][:, (j % 2) * 256 + hd * HD:(j % 2) * 256 + (hd + 1) * HD], mat(AkT, j, hd),
                                              vT[:, j * 256 + hd * HD:j * 256 + (hd + 1) * HD], start=True, stop=True)
                mm.then_inc(S("pq"), 1)
                pe.wait_ge(S("qp_out"), d + 1)
                for j in range(TILES):
                    for hd in range(HEADS):
                        mm = nc.tensor.matmul(ps[2 + j // 2][:, (j % 2) * 256 + hd * HD:(j % 2) * 256 + (hd + 1) * HD], mat(XT, j, hd),
                                              Qp[:, j * 256 + hd * HD:j * 256 + (hd + 1) * HD], start=True, stop=True)
                mm.then_inc(S("q"), 1)
                pe.wait_ge(S("q_out"), d + 1)
                for m, j in enumerate(ORDER[d]):
                    if m:
                        pe.wait_ge(S("s"), (TILES - 1) * d + m)
                        for q in range(2):
                            for i in range(2):
                                mm = nc.tensor.matmul(ps[q][:, i * HD:(i + 1) * HD], PT[q * HD:(q + 1) * HD, i * T + j * P:i * T + (j + 1) * P],
                                                      st[q * HD:(q + 1) * HD, (2 * j + i) * HD:(2 * j + i + 1) * HD], start=True, stop=True)
                        mm.then_inc(S("u_mm"), 1)
                        pe.wait_ge(S("u"), (TILES - 1) * d + m)
                    if m < TILES - 1:
                        for hd in range(HEADS):
                            q, i = hd % 2, hd // 2
                            out = ps[2][q * HD:(q + 1) * HD, i * HD:(i + 1) * HD]
                            a = j * 256 + hd * HD
                            nc.tensor.matmul(out, beT[:, a:a + HD], (U if m else Q)[:, a:a + HD], start=True, stop=False)
                            mm = nc.tensor.matmul(out, kT[:, a:a + HD], vT[:, a:a + HD], start=False, stop=True)
                        mm.then_inc(S("s_mm"), 1)
                for hd in range(HEADS):
                    q, i = hd % 2, hd // 2
                    for j in js:
                        out = ps[4 + i][q * HD:(q + 1) * HD, j * P:(j + 1) * P]
                        a = j * 256 + hd * HD
                        first_ = ORDER[d][0] == j
                        nc.tensor.matmul(out, (Q if first_ else U)[:, a:a + HD], mat(RbT, j, hd), start=True, stop=False)
                        mm = nc.tensor.matmul(out, vT[:, a:a + HD], mat(RkT, j, hd), start=False, stop=first_)
                        if not first_:
                            mm = nc.tensor.matmul(out, st[q * HD:(q + 1) * HD, (2 * j + i) * HD:(2 * j + i + 1) * HD],
                                                  rr[q * HD:(q + 1) * HD, i * T + j * P:i * T + (j + 1) * P], start=False, stop=True)
                mm.then_inc(S("y"), 1)
            for i in range(2):
                nc.tensor.matmul(ps[i][:, lo0:], par[:, Q_LORA + 512 + i * P:Q_LORA + 512 + (i + 1) * P], pr[:, T_GD * T + lo0:(T_GD + 1) * T],
                                 start=True, stop=False)
                nc.tensor.matmul(ps[i][:, lo0:], par[0:32, Q_LORA + 768 + i * P:Q_LORA + 768 + (i + 1) * P],
                                 pr[0:32, T_GD2 * T + lo0:(T_GD2 + 1) * T], start=False, stop=True)
            pe.wait_ge(S("bonus"), 1)
            head_sums(E, pe, rr, (2, 3), layer)
            head_sums(E, pe, y, (6, 7), layer).then_inc(S("mean"), 1)
            pe.wait_ge(S("sq"), 1)
            head_sums(E, pe, sq, (4, 5), layer).then_inc(S("ss"), 1)

        @block.gpsimd
        def _(pool):
            for d in range(2):
                for u, (l, j) in enumerate(units):
                    if u == 0:
                        pool.wait_ge(S("raw_out"), 2 * TILES * (d + 1))
                        if d:
                            pool.wait_ge(S("x0T"), TILES * d + 1)
                    if u >= 2:
                        pool.wait_ge(S("t1"), NU * d + u - 1)
                    mask = c(C_LEVEL + (d * LEVELS + l) * P).rearrange("p (b t) -> p b t", b=1).to_broadcast([P, HEADS, P])
                    nc.gpsimd.tensor_tensor(ct[:, (u % 2) * 512:(u % 2 + 1) * 512].rearrange("p (b t) -> p b t", b=HEADS),
                                            four(NT, j).rearrange("p (b t) -> p b t", b=HEADS), mask, ALU.mult).then_inc(S("ct"), 1)

        def tile_view(t):
            return t.rearrange("p (b t) -> p b t", t=P)

        @block.vector
        def _(dve):
            link = linker(dve, S("link"))
            for i in range(2):
                ins = nc.vector.tensor_scalar(tiles(kk, i, 1), tiles(pr, T_K + i, 1), par[:, Q_KK + i:Q_KK + i + 1], None, ALU.mult)
            link(ins)
            nc.vector.tensor_tensor(al, kk, kk, ALU.mult).then_inc(S("kk"), 1)
            dve.wait_ge(S("sT"), 1)
            nc.vector.tensor_copy(vT[:, 0:512], ps[4][:, :])
            nc.vector.tensor_copy(vT[:, 512:1024], ps[5][:, :])
            dve.wait_ge(S("kk_ss"), 1)
            for i in range(2):
                ins = nc.vector.tensor_scalar(tiles(al, i, 1), ps[6 + i][:, :], 1e-24, None, ALU.max)
            ins.then_inc(S("kk_max"), 1)
            dve.wait_ge(S("cum"), 1)
            for n in range(4):
                ins = nc.vector.tensor_copy(tiles(cum, n, 1), ps[n][:, :])
            link(ins)
            dve.wait_ge(S("kk_norm"), 1)
            link(nc.vector.reciprocal(al, al))
            link(nc.vector.tensor_tensor(kk, kk, al, ALU.mult))
            for d in range(2):
                end = P - 1 if d == 0 else 0
                if d:
                    dve.wait_ge(S("y"), d)
                    for i in range(2):
                        ins = nc.vector.tensor_copy(y[:, i * T + lo0:(i + 1) * T], ps[4 + i][:, lo0:])
                    link(ins)
                cv = tile_view(tiles(cum, 2 * d, 2))
                mid = cv[:, :, MID:MID + 1]
                link(nc.vector.tensor_tensor(tile_view(rr), cv, mid.to_broadcast([P, 2 * TILES, P]), ALU.subtract))
                nc.vector.tensor_tensor(al, rr, tiles(sg, 2 * d, 2), ALU.subtract)
                fc = fcol[:, 0:8].rearrange("p (i j) -> p i j", i=2)
                c4 = tiles(cum, 2 * d, 2).rearrange("p (i j t) -> p i j t", i=2, t=P)
                for m in range(TILES - 1):
                    j0, j1 = ORDER[d][m], ORDER[d][m + 1]
                    ins = nc.vector.tensor_tensor(fc[:, :, j0:j0 + 1], c4[:, :, j0, end:end + 1], c4[:, :, j0, MID:MID + 1], ALU.subtract)
                link(ins)
                for m in range(TILES - 1):
                    j0, j1 = ORDER[d][m], ORDER[d][m + 1]
                    ins = nc.vector.tensor_tensor(fc[:, :, j0:j0 + 1], fc[:, :, j0:j0 + 1], c4[:, :, j1, MID:MID + 1], ALU.add)
                ins.then_inc(S("dv"), 1)
                for i in range(2):
                    ins = nc.vector.tensor_scalar(tiles(ct, i, 1), tiles(sa, 2 * d + i, 1), -1.0, par[:, Q_KA + i:Q_KA + i + 1], ALU.add, ALU.mult)
                link(ins)
                link(nc.vector.scalar_tensor_tensor(out=ct, in0=ct, scalar=1.0, in1=tiles(pr, T_K, 2), op0=ALU.add, op1=ALU.mult))
                dve.wait_ge(S("exp"), d + 1)
                link(nc.vector.tensor_tensor(ks, ct, be, ALU.mult))
                link(nc.vector.tensor_tensor(ct, kk, tiles(sa, 2 * d, 2), ALU.mult))
                nc.vector.scalar_tensor_tensor(out=be, in0=be, scalar=-1.0, in1=ct, op0=ALU.mult, op1=ALU.mult)
                nc.vector.tensor_tensor(al, al, kk, ALU.mult)
                nc.vector.tensor_tensor(rr, rr, tiles(pr, T_R, 2), ALU.mult).then_inc(S("scaled"), 1)
                dve.wait_ge(S("scaled"), d + 1)
                dve.wait_ge(S("tT"), d + 1)
                for n, (dst, b) in enumerate(((alT, 0), (alT, 1), (beT, 2))):
                    ins = nc.vector.tensor_copy(dst[:, (b % 2) * 512:(b % 2 + 1) * 512], ps[b][:, :])
                ins.then_inc(S("tT_out"), 1)
                for j in range(TILES):
                    for n, (m0, msk) in enumerate(((0, C_STRICT), (4096, C_TRI))):
                        dve.wait_ge(S("raw"), 2 * (TILES * d + j) + n + 1)
                        mask = c(msk + d * P).rearrange("p (a b t) -> p a b t", a=1, b=1).to_broadcast([P, 2, 2, P])
                        for q in range(2):
                            dst = free[:, m0:m0 + 4096].rearrange("p (k j i q t) -> p k j i q t", k=2, j=TILES, i=2, q=2)[:, :, j, :, q, :]
                            src = ps[4 * (j % 2) + 2 * n + q][:, :].rearrange("p (k i t) -> p k i t", k=2, i=2)
                            ins = nc.vector.tensor_tensor(dst, src, mask, ALU.mult)
                        ins.then_inc(S("raw_out"), 1)
                dve.wait_ge(S("raw_out"), 2 * TILES * (d + 1))
                idb = ident.rearrange("p (b t) -> p b t", b=1).to_broadcast([P, HEADS, P])
                mask = c(C_LEVEL + d * LEVELS * P).rearrange("p (b t) -> p b t", b=1).to_broadcast([P, HEADS, P])
                for j in range(TILES):
                    nc.vector.tensor_tensor(four(X, j).rearrange("p (b t) -> p b t", b=HEADS), four(NT, j).rearrange("p (b t) -> p b t", b=HEADS),
                                            mask, ALU.mult).then_inc(S("x0T"), 1)
                dve.wait_ge(S("x0T"), TILES * (d + 1))
                for j in range(TILES):
                    ins = nc.vector.tensor_tensor(four(XT, j).rearrange("p (b t) -> p b t", b=HEADS),
                                                  four(X, j).rearrange("p (b t) -> p b t", b=HEADS), idb, ALU.add)
                link(ins)
                for j in range(TILES):
                    dve.wait_ge(S("x0"), TILES * d + j + 1)
                    nc.vector.tensor_tensor(four(X, j).rearrange("p (b t) -> p b t", b=HEADS), ps[j][:, :].rearrange("p (b t) -> p b t", b=HEADS),
                                            idb, ALU.add).then_inc(S("x_up"), 1)
                for u, (l, j) in enumerate(units):
                    dve.wait_ge(S("d_mm"), NU * d + u + 1)
                    dve.wait_ge(S("x_up"), (NU + TILES) * d + u + 1)
                    nc.vector.tensor_tensor(four(XT, j), four(XT, j), ps[4 + u % 2][:, :], ALU.add)
                    nc.vector.tensor_tensor(four(X, j), four(X, j), ps[2 + u % 2][:, :], ALU.add).then_inc(S("x_up"), 1)
                dve.wait_ge(S("x_up"), (NU + TILES) * (d + 1))
                dve.wait_ge(S("pq"), d + 1)
                nc.vector.tensor_copy(Qp[:, 0:512], ps[0][:, :])
                nc.vector.tensor_copy(Qp[:, 512:1024], ps[1][:, :]).then_inc(S("qp_out"), 1)
                dve.wait_ge(S("q"), d + 1)
                dve.wait_ge(S("pt_out"), d + 1)
                nc.vector.tensor_copy(Q[:, 0:512], ps[2][:, :])
                nc.vector.tensor_copy(Q[:, 512:1024], ps[3][:, :]).then_inc(S("q_out"), 1)
                dve.wait_ge(S("q_out"), d + 1)
                for m, j in enumerate(ORDER[d]):
                    if m:
                        dve.wait_ge(S("u_mm"), (TILES - 1) * d + m)
                        for q in range(2):
                            uv, qv = (t[:, j * 256:(j + 1) * 256].rearrange("p (i q v) -> p i q v", i=2, q=2)[:, :, q, :] for t in (U, Q))
                            ins = nc.vector.tensor_tensor(uv, qv, ps[q][:, 0:P].rearrange("p (i v) -> p i v", i=2), ALU.add)
                        ins.then_inc(S("u"), 1)
                    if m < TILES - 1:
                        dve.wait_ge(S("s_mm"), (TILES - 1) * d + m + 1)
                        j1 = ORDER[d][m + 1]
                        new, old = st[:, j1 * P:(j1 + 1) * P], st[:, j * P:(j + 1) * P]
                        if m:
                            link(nc.vector.tensor_tensor(new, old, ps[2][:, 0:P], ALU.add))
                        for i in range(2):
                            ins = nc.vector.tensor_scalar(new[:, i * HD:(i + 1) * HD], (new if m else ps[2][:, 0:P])[:, i * HD:(i + 1) * HD],
                                                          fcol[:, 8 + i * TILES + j:9 + i * TILES + j], None, ALU.mult)
                        ins.then_inc(S("s"), 1)
                        dve.wait_ge(S("s"), (TILES - 1) * d + m + 1)
            dve.wait_ge(S("y"), 2)
            for i in range(2):
                v = y[:, i * T + lo0:(i + 1) * T]
                ins = nc.vector.tensor_tensor(v, v, ps[4 + i][:, lo0:], ALU.add)
            link(nc.vector.tensor_tensor(ks, tiles(sa, 0, 2), tiles(sa, 2, 2), ALU.add))
            for i in range(2):
                ins = nc.vector.tensor_scalar(tiles(ks, i, 1), tiles(ks, i, 1), -2.0, par[:, Q_KA + i:Q_KA + i + 1], ALU.add, ALU.mult)
            link(ins)
            link(nc.vector.scalar_tensor_tensor(out=ks, in0=ks, scalar=2.0, in1=tiles(pr, T_K, 2), op0=ALU.add, op1=ALU.mult))
            for i in range(2):
                ins = nc.vector.scalar_tensor_tensor(out=tiles(rr, i, 1), in0=tiles(pr, T_R + i, 1), scalar=par[:, Q_RK + i:Q_RK + i + 1],
                                                     in1=tiles(ks, i, 1), op0=ALU.mult, op1=ALU.mult)
            ins.then_inc(S("bonus"), 1)
            dve.wait_ge(S("mean"), 1)
            for i in range(2):
                v = y[:, i * T + lo0:(i + 1) * T]
                ins = nc.vector.scalar_tensor_tensor(out=v, in0=ps[6 + i][:, lo0:], scalar=-1.0 / HD, in1=v, op0=ALU.mult, op1=ALU.add)
            link(ins)
            nc.vector.tensor_tensor(two(sq, layer), two(y, layer), two(y, layer), ALU.mult).then_inc(S("sq"), 1)
            for i in range(2):
                ins = nc.vector.tensor_tensor(be[:, i * T + lo0:(i + 1) * T], pr[:, (T_V + i) * T + lo0:(T_V + i + 1) * T], ps[2 + i][:, lo0:], ALU.mult)
            dve.wait_ge(S("rn"), 1)
            link(nc.vector.tensor_tensor(two(y, layer), two(y, layer), two(sq, layer), ALU.mult))
            for i in range(2):
                v = y[:, i * T + lo0:(i + 1) * T]
                ins = nc.vector.tensor_scalar(v, v, par[:, Q_XG + i:Q_XG + i + 1], par[:, Q_XB + i:Q_XB + i + 1], ALU.mult, ALU.add)
            link(ins)
            link(nc.vector.tensor_tensor(two(y, layer), two(y, layer), two(be, layer), ALU.add))
            for i in range(2):
                v = y[:, i * T + lo0:(i + 1) * T]
                nc.vector.tensor_tensor(v, v, ps[i][:, lo0:], ALU.mult)

        @block.scalar
        def _(act):
            act.wait_ge(S("lora"), 1)
            for d in range(2):
                for i in range(2):
                    n = 2 * d + i
                    nc.scalar.activation(tiles(sg, n, 1), ps[n][:, :], ACT.Sigmoid, bias=par[:, Q_W0 + n:Q_W0 + n + 1])
                    ins = nc.scalar.activation(tiles(sa, n, 1), ps[4 + n][:, :], ACT.Sigmoid, bias=par[:, Q_A0 + n:Q_A0 + n + 1])
            ins.then_inc(S("sig"), 1)
            act.wait_ge(S("sT"), 1)
            for n in range(4):
                ins = nc.scalar.copy(tm[:, n * 512:(n + 1) * 512], ps[n][:, :])
            ins.then_inc(S("sT_out"), 1)
            act.wait_ge(S("kk_max"), 1)
            nc.scalar.activation(al, al, ACT.Sqrt).then_inc(S("kk_norm"), 1)
            for d in range(2):
                act.wait_ge(S("dv"), d + 1)
                nc.scalar.activation(be, rr, ACT.Exp, scale=KAPPA).then_inc(S("be_exp"), 1)
                act.wait_ge(S("be_exp"), d + 1)
                nc.scalar.activation(rr, rr, ACT.Exp, scale=-KAPPA)
                nc.scalar.activation(al, al, ACT.Exp, scale=-KAPPA)
                fc = fcol[:, 0:8].rearrange("p (i j) -> p i j", i=2)
                fo = fcol[:, 8:16].rearrange("p (i j) -> p i j", i=2)
                last = ORDER[d][-1]
                a, b = (0, 3) if d == 0 else (0, 4)
                if d == 0:
                    nc.scalar.activation(fo[:, :, 0:3], fc[:, :, 0:3], ACT.Exp, scale=-KAPPA).then_inc(S("exp"), 1)
                else:
                    nc.scalar.activation(fo[:, :, 0:2], fc[:, :, 0:2], ACT.Exp, scale=-KAPPA)
                    nc.scalar.activation(fo[:, :, 3:4], fc[:, :, 3:4], ACT.Exp, scale=-KAPPA).then_inc(S("exp"), 1)
                act.wait_ge(S("tT"), d + 1)
                nc.scalar.copy(beT[:, 512:1024], ps[3][:, :])
                nc.scalar.copy(kT[:, 0:512], ps[4][:, :])
                nc.scalar.copy(kT[:, 512:1024], ps[5][:, :]).then_inc(S("tT_out"), 1)
                for u in range(NU):
                    act.wait_ge(S("t1"), NU * d + u + 1)
                    if u >= 2:
                        act.wait_ge(S("d_mm"), NU * d + u - 1)
                    nc.scalar.copy(t1[:, (u % 2) * 512:(u % 2 + 1) * 512], ps[u % 2][:, :]).then_inc(S("t1_out"), 1)
                act.wait_ge(S("pq"), d + 1)
                nc.scalar.copy(PT[:, 0:512], ps[6][:, :])
                nc.scalar.copy(PT[:, 512:1024], ps[7][:, :]).then_inc(S("pt_out"), 1)
            inverse_rms(E, S, act, (4, 5), sq, layer, 1.0 / HD, Q_EPS + 1)


def residual_norm(E, S, dve, act, layer, which, lnp):
    nc, h, gate, ps, par = (E[k] for k in ("nc", "h", "gate", "ps", "par"))
    js = active(layer)
    g0 = 2 * which
    tmp, stats = E["pr"][:, 30 * T:32 * T], E["pr"][:, 29 * T:29 * T + 128]
    if dve:
        link = linker(dve, S("link"))
        dve.wait_ge(S("y"), 1)
        for m, j in enumerate(js):
            side = j // 2
            hj = h[:, j * D:(j + 1) * D]
            for b in range(2):
                ins = nc.vector.tensor_tensor(tmp[:, b * 512:(b + 1) * 512], ps[2 * j + b][:, :],
                                              gate[:, (g0 + side) * D + b * 512:(g0 + side) * D + (b + 1) * 512], ALU.mult)
            link(ins)
            link(nc.vector.scalar_tensor_tensor(out=hj, in0=hj, scalar=ALPHA, in1=tmp, op0=ALU.mult, op1=ALU.add))
            s = stats[:, 32 * m:32 * m + 32]
            for b in range(2):
                ins = nc.vector.bn_stats(s[:, 6 * b:6 * b + 6], hj[:, b * 512:(b + 1) * 512])
            link(ins)
            nc.vector.bn_aggr(s[:, 12:14], s[:, 0:12]).then_inc(S("var"), 1)
        dve.wait_ge(S("ln_par"), 16)
        for m, j in enumerate(js):
            hj, s = h[:, j * D:(j + 1) * D], stats[:, 32 * m:32 * m + 32]
            dve.wait_ge(S("rstd"), m + 1)
            link(nc.vector.tensor_scalar(hj, hj, s[:, 12:13], s[:, 15:16], ALU.subtract, ALU.mult))
            link(nc.vector.tensor_tensor(hj, hj, lnp[:, 0:D], ALU.mult))
            nc.vector.tensor_tensor(hj, hj, lnp[:, D:2 * D], ALU.add).then_inc(S("normed"), 1)
    if act:
        for m, j in enumerate(js):
            s = stats[:, 32 * m:32 * m + 32]
            act.wait_ge(S("var"), m + 1)
            nc.scalar.activation(s[:, 14:15], s[:, 13:14], ACT.Ln, bias=par[:, Q_EPS:Q_EPS + 1]).then_inc(S("lnv"), 1)
            act.wait_ge(S("lnv"), m + 1)
            nc.scalar.activation(s[:, 15:16], s[:, 14:15], ACT.Exp, scale=-0.5).then_inc(S("rstd"), 1)


def output_projection(E, layer):
    nc, A, mix, ring, ps = (E[k] for k in ("nc", "A", "mix", "ring", "ps"))
    js = active(layer)
    lnp = E["pr"][:, 24 * T:28 * T]
    with Stage(nc) as S, nc.Block() as block:
        for n in ("link", "y", "var", "lnv", "rstd", "ln_par"):
            S(n)

        @block.sync
        def _(sp):
            for k in range(KD):
                if k >= 4:
                    sp.wait_ge(S("mm"), k - 3)
                sp.dma_start(ring[:, (k % 4) * D:(k % 4 + 1) * D], A["w_out"][layer, k]).then_inc(S(f"w{k % 4}"), 16)
            sp.dma_start(lnp, A["ln"][layer, 0]).then_inc(S("ln_par"), 16)

        @block.tensor
        def _(pe):
            for k in range(KD):
                pe.wait_ge(S(f"w{k % 4}"), 16 * (k // 4 + 1))
                for j in js:
                    for b in range(2):
                        mm = nc.tensor.matmul(ps[2 * j + b][:, :], mix[:, k * T + j * P:k * T + (j + 1) * P],
                                              ring[:, (k % 4) * D + b * 512:(k % 4) * D + (b + 1) * 512], start=(k == 0), stop=(k == KD - 1))
                mm.then_inc(S("mm"), 1)
            pe.wait_ge(S("mm"), KD)
            pe.sem_inc(S("y"), 1)

        @block.vector
        def _(dve):
            residual_norm(E, S, dve, None, layer, 0, lnp)

        @block.scalar
        def _(act):
            residual_norm(E, S, None, act, layer, 0, lnp)


def ffn(E, layer):
    nc, A, par, pr, work, ring, ps = (E[k] for k in ("nc", "A", "par", "pr", "work", "ring", "ps"))
    js = active(layer)
    lo0, n0 = span(layer)
    ns = n0 // SIDE
    lnp = pr[:, 24 * T:28 * T]
    tb = work[:, 4096:4096 + 1024]
    wup = (ring[:, 0:2048], ring[:, 2048:4096], work[:, 5120:7168], work[:, 7168:9216], work[:, 9216:11264], work[:, 11264:13312])
    NW = len(wup)
    with Stage(nc) as S, nc.Block() as block:
        for n in ("link", "y", "var", "lnv", "rstd", "ln_par", "turned", "dd"):
            S(n)

        @block.sync
        def _(sp):
            for f in range(KF):
                if f >= NW:
                    sp.wait_ge(S("up"), f - NW + 1)
                sp.dma_start(wup[f % NW], A["w_up"][layer, f]).then_inc(S(f"w{f % NW}"), 16)
            for k in range(0, KF, 2):
                f = KF + k // 2
                sp.wait_ge(S("up"), min(f - NW + 1, KF)) if f - NW < KF else sp.wait_ge(S("down"), f - NW - KF + 1)
                sp.dma_start(wup[f % NW].rearrange("p (a n) -> p a n", a=2), A["w_down"][layer, k:k + 2].rearrange("a p n -> p a n"))\
                    .then_inc(S(f"w{f % NW}"), 16)
            sp.dma_start(lnp, A["ln"][layer, 1]).then_inc(S("ln_par"), 16)

        @block.tensor
        def _(pe):
            transpose_modulate(E, S, pe=pe)
            pe.wait_ge(S("hT0"), KD)
            pe.wait_ge(S("hT1"), KD)
            for f in range(KF):
                pe.wait_ge(S(f"w{f % NW}"), 16 * (f // NW + 1))
                if f >= 2:
                    pe.wait_ge(S("acts"), f - 1)
                for v in range(2):
                    for k in range(KD):
                        mm = nc.tensor.matmul(ps[2 * (f % 2) + v][:, lo0:], wup[f % NW][:, v * 1024 + k * P:v * 1024 + (k + 1) * P],
                                              work[:, k * T + lo0:(k + 1) * T], start=(k == 0), stop=(k == KD - 1))
                mm.then_inc(S("up"), 1)
            pe.wait_ge(S("acts"), KF)
            for k in range(KF):
                f = KF + k // 2
                if k % 2 == 0:
                    pe.wait_ge(S(f"w{f % NW}"), 16 * (f // NW + 1))
                for j in js:
                    for b in range(2):
                        mm = nc.tensor.matmul(ps[2 * j + b][:, :], pr[:, k * T + j * P:k * T + (j + 1) * P],
                                              wup[f % NW][:, (k % 2) * D + b * 512:(k % 2) * D + (b + 1) * 512], start=(k == 0), stop=(k == KF - 1))
                if k % 2:
                    mm.then_inc(S("down"), 1)
            pe.wait_ge(S("down"), KF // 2)
            pe.sem_inc(S("y"), 1)

        @block.vector
        def _(dve):
            transpose_modulate(E, S, dve=dve, shift=3, scale=4)
            link = linker(dve, S("dd"))
            for f in range(KF + 1):
                if f < KF:
                    dve.wait_ge(S("up"), f + 1)
                    if f >= 2:
                        dve.wait_ge(S("gelu"), f - 1)
                    z = ps[2 * (f % 2)][:, lo0:]
                    t = tb[:, (f % 2) * T + lo0:(f % 2 + 1) * T]
                    z3, t3 = (v.rearrange("p (s t) -> p s t", s=ns) for v in (z, t))
                    a = Q_FCW + 3 * f
                    link(nc.vector.tensor_scalar(t, z, par[:, a + 1:a + 2], par[:, Q_FCB + f:Q_FCB + f + 1], ALU.mult, ALU.add))
                    link(nc.vector.scalar_tensor_tensor(out=t3[:, :, 1:], in0=z3[:, :, :-1], scalar=par[:, a:a + 1], in1=t3[:, :, 1:],
                                                        op0=ALU.mult, op1=ALU.add))
                    nc.vector.scalar_tensor_tensor(out=t3[:, :, :-1], in0=z3[:, :, 1:], scalar=par[:, a + 2:a + 3], in1=t3[:, :, :-1],
                                                   op0=ALU.mult, op1=ALU.add).then_inc(S("conv"), 1)
                if f >= 1:
                    g = f - 1
                    dve.wait_ge(S("gelu"), g + 1)
                    o = pr[:, g * T + lo0:(g + 1) * T]
                    nc.vector.tensor_tensor(o, o, ps[2 * (g % 2) + 1][:, lo0:], ALU.mult).then_inc(S("acts"), 1)
            residual_norm(E, S, dve, None, layer, 1, lnp)

        @block.scalar
        def _(act):
            transpose_modulate(E, S, act=act, shift=3, scale=4)
            for f in range(KF):
                act.wait_ge(S("conv"), f + 1)
                nc.scalar.activation(pr[:, f * T + lo0:(f + 1) * T], tb[:, (f % 2) * T + lo0:(f % 2 + 1) * T],
                                     ACT.Gelu_apprx_tanh).then_inc(S("gelu"), 1)
            residual_norm(E, S, None, act, layer, 1, lnp)


def store_output(E):
    nc, h, out = (E[k] for k in ("nc", "h", "out"))
    with Stage(nc) as S, nc.Block() as block:
        @block.sync
        def _(sp):
            sp.dma_start(out.rearrange("(j p) d -> p j d", p=P), h[:, :].rearrange("p (j d) -> p j d", j=TILES)[:, 2:4, :])\
                .then_inc(E["stored"], 16)
            sp.wait_ge(E["stored"], 16)


def constants():
    t = np.zeros((P, N_CONST), np.float32)
    s, q = np.arange(P)[:, None], np.arange(P)[None, :]
    t[:, C_ID:C_ID + P] = s == q
    for d in range(2):
        before = (s <= q) if d == 0 else (s >= q)
        t[:, C_TRI + d * P:C_TRI + (d + 1) * P] = before
        t[:, C_STRICT + d * P:C_STRICT + (d + 1) * P] = before & (s != q)
        t[:, C_BASE + d * P:C_BASE + (d + 1) * P] = before & (s // 2 == q // 2)
        for l in range(LEVELS):
            a = C_LEVEL + (d * LEVELS + l) * P
            t[:, a:a + P] = (s // (2 << l) == q // (2 << l)) & (s // (1 << l) != q // (1 << l)) & before
    t[:, C_ONES:C_ONES + P] = 1
    t[:, C_HONES:C_HONES + P] = s // HD == q // HD
    t[:, C_ROT:C_ROT + P] = np.where(s // 32 == q // 32, np.where((q % 32 < 16) & (s == q + 16), -1.0, 0.0) + ((q % 32 >= 16) & (s == q - 16)), 0.0)
    tok = np.arange(SIDE)
    n_freq = HD // 8
    inv = (np.float32(10000.0) ** (-np.arange(n_freq, dtype=np.float32) / np.float32(n_freq))).astype(np.float32)
    ang = np.concatenate([(tok // 64).astype(np.float32)[:, None] * inv, (tok % 64).astype(np.float32)[:, None] * inv], axis=1)
    ch = np.arange(P) % 16
    t[:, C_COS:C_COS + SIDE] = np.cos(ang)[:, ch].T
    t[:, C_SIN:C_SIN + SIDE] = np.sin(ang)[:, ch].T
    for hd in range(HEADS):
        t[hd, C_SELH + hd * P:C_SELH + (hd + 1) * P] = 1
        t[hd, C_SELP + (hd // 2) * P + (hd % 2) * HD:C_SELP + (hd // 2) * P + (hd % 2 + 1) * HD] = 1
    for side in range(2):
        t[side, C_SEL2 + side * P:C_SEL2 + (side + 1) * P] = 1
    return t


def lay_out(x, c, ctx, c_ctx, ada_w, ada_b, w_in, rwkv_mu, rwkv_w0, rwkv_w2, rwkv_a0, rwkv_a2, rwkv_g2, rwkv_k_k, rwkv_k_a,
            rwkv_r_k, rwkv_lnx_g, rwkv_lnx_b, diff_lambda, diff_norm_g, hgrn_lb_logits, hgrn_norm_g, mlstm_conv_w, mlstm_conv_b,
            mlstm_gate_b, mlstm_norm_g, w_out, ffn_w_up, ffn_conv_w, ffn_conv_b, ffn_w_down, ln_g, ln_b):
    L = DEPTH
    w = np.zeros((L, D, IN_TILES * P), np.float32)
    w[:, :, 0:1184] = w_in[:, :, 0:1184]
    w[:, :, 1184:1200] = w_in[:, :, 4256:4272]
    w[:, :, 10 * P:] = w_in[:, :, 1184:4256]
    w = w.reshape(L, KD, P, IN_TILES, P).transpose(0, 3, 2, 1, 4).reshape(L, IN_TILES, P, KD * P)
    up = ffn_w_up.reshape(L, KD, P, 2, KF, P).transpose(0, 4, 2, 3, 1, 5).reshape(L, KF, P, 2 * KD * P)
    ada = ada_w.reshape(L, KD, P, 12, 512).transpose(0, 3, 2, 1, 4).reshape(L, 12, P, KD * 512)
    par = np.zeros((L, P, N_PAR), np.float32)

    def put(o, a, n):
        par[:, :, o:o + n] = a.reshape(L, n, P).transpose(0, 2, 1)

    mu = np.zeros((L, 10 * P), np.float32)
    mu[:, 0:1184] = rwkv_mu
    put(Q_MU, mu, 10)
    put(Q_W0, rwkv_w0, 4)
    put(Q_A0, rwkv_a0, 4)
    for o, a in ((Q_KK, rwkv_k_k), (Q_KA, rwkv_k_a), (Q_RK, rwkv_r_k), (Q_XG, rwkv_lnx_g), (Q_XB, rwkv_lnx_b), (Q_MN, mlstm_norm_g)):
        put(o, a, 2)
    put(Q_DN, np.tile(diff_norm_g, (1, 2)), 1)
    put(Q_HN, np.tile(hgrn_norm_g, (1, 2)), 1)
    for l in range(L):
        put(Q_LB + 2 * l, np.broadcast_to(hgrn_lb_logits[l], (L, 256)), 2)
    par[:, :, Q_MCW:Q_MCW + 12] = mlstm_conv_w.reshape(L, 3, 4, P).transpose(0, 3, 2, 1).reshape(L, P, 12)
    put(Q_MCB, mlstm_conv_b, 4)
    par[:, :, Q_FCW:Q_FCW + 3 * KF] = ffn_conv_w.reshape(L, 3, KF, P).transpose(0, 3, 2, 1).reshape(L, P, 3 * KF)
    put(Q_FCB, ffn_conv_b, KF)
    par[:, :, Q_GB:Q_GB + 16] = mlstm_gate_b.reshape(L, 1, 16)
    par[:, :, Q_LAM:Q_LAM + 128] = diff_lambda.reshape(L, 1, 128)
    par[:, :, Q_EPS] = LN_EPS
    par[:, :, Q_EPS + 1] = LNX_EPS
    par[:, :, Q_LORA:Q_LORA + 256] = rwkv_w2.reshape(L, P, 256)
    par[:, :, Q_LORA + 256:Q_LORA + 512] = rwkv_a2.reshape(L, P, 256)
    par[:, :, Q_LORA + 512:Q_LORA + 768] = rwkv_g2[:, 0:P]
    par[:, 0:32, Q_LORA + 768:Q_LORA + 1024] = rwkv_g2[:, P:160]
    ln = np.stack([ln_g, ln_b], axis=2).reshape(L, 2, 1, 2 * D)
    return {
        "x": x[0], "ctx": ctx[0], "const": constants(), "par": par,
        "cond": np.stack([c_ctx.reshape(KD, P), c.reshape(KD, P)], axis=0).transpose(2, 1, 0).reshape(P, 2 * KD),
        "ada_w": ada, "ada_b": np.broadcast_to(ada_b[:, None, :], (L, 2, 6 * D)), "w_in": w, "w_out": w_out.reshape(L, KD, P, D),
        "w_up": up, "w_down": ffn_w_down.reshape(L, KF, P, D), "ln": np.broadcast_to(ln, (L, 2, P, 2 * D)),
    }


def kernel(**inputs):
    import concourse.bacc as bacc
    from concourse.bass_utils import run_bass_kernel_spmd

    nc = bacc.Bacc("TRN2", target_bir_lowering=False, num_devices=1)
    arrays = {k: np.ascontiguousarray(v) for k, v in lay_out(**{k: np.asarray(v) for k, v in inputs.items()}).items()}
    A = {k: nc.dram_tensor(f"in_{k}", v.shape, F32, kind="ExternalInput").ap() for k, v in arrays.items()}
    out = nc.dram_tensor("out", (SIDE, D), F32, kind="ExternalOutput").ap()
    build(nc, A, out)
    r = run_bass_kernel_spmd(nc, [{f"in_{k}": v for k, v in arrays.items()}], core_ids=[0])
    return r.results[0]["out"].reshape(1, SIDE, D)
```

```python
from contextlib import ExitStack

import numpy as np
import concourse.bass as bass
from concourse import mybir

F32 = mybir.dt.float32
F32R = mybir.dt.float32r
I32 = mybir.dt.int32
ALU = mybir.AluOpType
ACT = mybir.ActivationFunctionType
AX_X = mybir.AxisListType.X

P = 128
D = 1024
KD = D // P
SIDE = 256
T = 2 * SIDE
TILES = T // P
DEPTH = 2
HEADS = 4
HD = 64
FF = 2816
KF = FF // P
ALPHA = (2.0 * DEPTH) ** 0.25
LN_EPS = 1e-5
LNX_EPS = 64e-5
ORDER = ((0, 1, 2, 3), (1, 0, 3, 2))
LEVELS = 7

T_R, T_K, T_V, T_WD, T_AD, T_GD, T_GD2 = 0, 2, 4, 6, 7, 8, 9
GATE_ROW = 32
T_DQ, T_DK, T_DV = 10, 12, 14
T_HQ, T_HF, T_HB, T_HI, T_HG = 16, 18, 20, 22, 24
T_MQ, T_MK, T_MV, T_MO = 26, 28, 30, 32
IN_TILES = 34

C_ID = 0
C_TRI = C_ID + P
C_STRICT = C_TRI + 2 * P
C_BASE = C_STRICT + 2 * P
C_ONES = C_BASE + 2 * P
C_HONES = C_ONES + P
C_ROT = C_HONES + P
C_COS = C_ROT + P
C_SIN = C_COS + SIDE
C_LEVEL = C_SIN + SIDE
C_SELH = C_LEVEL + 2 * LEVELS * P
C_SELP = C_SELH + HEADS * P
C_SEL2 = C_SELP + 2 * P
N_CONST = C_SEL2 + 2 * P

_o = 0


def _cols(n):
    global _o
    _o += n
    return _o - n


Q_MU, Q_W0, Q_A0, Q_KK, Q_KA, Q_RK, Q_XG, Q_XB = (_cols(n) for n in (10, 4, 4, 2, 2, 2, 2, 2))
Q_DN, Q_HN, Q_LB, Q_MCW, Q_MCB, Q_MN = (_cols(n) for n in (1, 1, 4, 12, 4, 2))
Q_FCW, Q_FCB, Q_GB, Q_LAM, Q_EPS, Q_LORA = (_cols(n) for n in (3 * KF, KF, 16, 128, 4, 1024))
N_PAR = _o


class Stage:

    zeroed, made = [], 0

    def __init__(self, nc):
        Stage.made += 1
        self.nc, self.sems, self.tag, self.memory = nc, {}, Stage.made, ExitStack()

    def sb(self, name, cols, dtype=F32):
        return self.memory.enter_context(self.nc.sbuf_tensor(f"{name}_{self.tag}", [P, cols], dtype))

    def __enter__(self):
        return self

    def __call__(self, name):
        if name not in self.sems:
            self.sems[name] = self.nc.alloc_semaphore(f"{name}_{self.tag}")
        return self.sems[name]

    def __exit__(self, *exc):
        self.memory.close()
        if exc[0] is None:
            for sem in Stage.zeroed:
                self.nc.release_semaphore(sem)
            for sem in self.sems.values():
                self.nc.sync.sem_clear(sem)
            Stage.zeroed = list(self.sems.values())


def linker(eng, sem):
    count = [0]

    def link(ins):
        count[0] += 1
        ins.then_inc(sem, 1)
        eng.wait_ge(sem, count[0])

    return link


def build(nc, A, out):
    Stage.zeroed, Stage.made = [], 0
    with ExitStack() as ctx:
        def sb(name, cols):
            return ctx.enter_context(nc.sbuf_tensor(name, [P, cols], F32))

        const = sb("const", N_CONST)
        par = sb("par", N_PAR)
        h = sb("h", TILES * D)
        pr = sb("pr", IN_TILES * T)
        mix = sb("mix", KD * T)
        gate = sb("gate", 4 * D)
        modc = sb("modc", 48 * 2)
        cond = sb("cond", KD * 2)
        fcol = sb("fcol", 16)
        ps = [ctx.enter_context(nc.psum_tensor(f"ps{i}", [P, 512], F32)) for i in range(8)]

        def c(o, n=P, rows=P):
            return const[0:rows, o:o + n]

        ident = c(C_ID)
        stored = ctx.enter_context(nc.semaphore("stored"))
        E = dict(stored=stored, nc=nc, A=A, out=out, c=c, const=const, ident=ident, par=par, h=h, pr=pr, mix=mix, gate=gate, modc=modc, cond=cond, fcol=fcol, ps=ps)
        load_inputs(E)
        for layer in range(DEPTH):
            adaln(E, layer)
            input_projection(E, layer)
            with nc.sbuf_tensor(f"work{layer}", [P, 13312], F32) as E["work"], nc.sbuf_tensor(f"more{layer}", [P, 4096], F32) as E["ring"]:
                conv_and_sigmoids(E, layer)
                diff_attention(E, layer)
                mlstm(E, layer)
                hgrn(E, layer)
                rwkv(E, layer)
            output_projection(E, layer)
            ffn(E, layer)
        store_output(E)


def load_inputs(E):
    nc, A, par, const, h, cond, ps = (E[k] for k in ("nc", "A", "par", "const", "h", "cond", "ps"))
    with Stage(nc) as S, nc.Block() as block:
        work = S.sb("sigmoid", 16)

        @block.sync
        def _(sp):
            sp.dma_start(cond[:, :], A["cond"]).then_inc(S("c"), 16)
            sp.dma_start(const[:, :], A["const"]).then_inc(S("in"), 16)
            sp.dma_start(h[:, :].rearrange("p (j d) -> p j d", j=TILES)[:, 0:2, :],
                         A["ctx"].rearrange("(j p) d -> p j d", p=P)).then_inc(S("in"), 16)
            sp.dma_start(h[:, :].rearrange("p (j d) -> p j d", j=TILES)[:, 2:4, :],
                         A["x"].rearrange("(j p) d -> p j d", p=P)).then_inc(S("in"), 16)
            sp.wait_ge(S("in"), 48)

        @block.scalar
        def _(act):
            act.wait_ge(S("c"), 16)
            nc.scalar.activation(work[:, 0:16], cond[:, :], ACT.Sigmoid).then_inc(S("sig"), 1)

        @block.vector
        def _(dve):
            dve.wait_ge(S("sig"), 1)
            nc.vector.tensor_tensor(cond[:, :], cond[:, :], work[:, 0:16], ALU.mult)


def split_high(nc, act, raw, high):
    return nc.scalar.copy(high, raw)


def split_low(nc, dve, raw, high, low):
    return nc.vector.tensor_tensor(low, raw, high.bitcast(F32), ALU.subtract)


def product(nc, out, stationary, moving, first, last):
    (sh, sl), (mh, ml) = stationary, moving
    nc.tensor.matmul(out, sh, mh, start=first, stop=False)
    nc.tensor.matmul(out, sh, ml, start=False, stop=False)
    return nc.tensor.matmul(out, sl, mh, start=False, stop=last)


def adaln(E, layer):
    nc, A, c, par, pr, mix, gate, modc, cond, ps = (
        E[k] for k in ("nc", "A", "c", "par", "pr", "mix", "gate", "modc", "cond", "ps"))
    NB, W = 12, KD * 512
    raw = (pr[:, 0:W], pr[:, W:2 * W], mix[:, :])
    SLOTS = len(raw)
    bias = pr[0:2, 2 * W:2 * W + NB * 512]
    rows = pr[0:2, 2 * W + NB * 512:2 * W + NB * 512 + 1024]
    with Stage(nc) as S, nc.Block() as block:
        condr = S.sb("condr", 2 * (2 * KD + P), F32R)
        wr = S.sb("wr", 4 * W, F32R)

        def high(n):
            return wr[:, (n % 2) * 2 * W:(n % 2) * 2 * W + W]

        def low(n):
            return wr[:, (n % 2) * 2 * W + W:(n % 2 + 1) * 2 * W]

        def cpart(p):
            return condr[:, p * (2 * KD + P):(p + 1) * (2 * KD + P)]

        @block.sync
        def _(sp):
            for n in range(NB):
                if n >= SLOTS:
                    sp.wait_ge(S("low"), n - SLOTS + 1)
                sp.dma_start(raw[n % SLOTS], A["ada_w"][layer, n]).then_inc(S(f"w{n % SLOTS}"), 16)
                if n == 0:
                    sp.dma_start(bias, A["ada_b"][layer]).then_inc(S("bias"), 16)
                    sp.dma_start(par[:, :], A["par"][layer]).then_inc(S("par"), 16)
            sp.wait_ge(S("par"), 16)

        @block.tensor
        def _(pe):
            def products(n):
                pe.wait_ge(S("high"), n + 1)
                pe.wait_ge(S("low"), n + 1)
                if n >= 2:
                    pe.wait_ge(S("row"), n - 1)
                for k in range(KD):
                    mm = product(nc, ps[n % 2][:, :], [cpart(p)[:, 2 * k:2 * k + P] for p in (0, 1)],
                                 [w[:, k * 512:(k + 1) * 512] for w in (high(n), low(n))], k == 0, k == KD - 1)
                mm.then_inc(S("mm"), 1)

            def spread(n):
                pe.wait_ge(S("row"), n + 1)
                if n >= 1:
                    pe.wait_ge(S("spread_out"), n)
                row = rows[:, (n % 2) * 512:(n % 2 + 1) * 512]
                if n // 2 in (2, 5):
                    for side in range(2):
                        mm = nc.tensor.matmul(ps[2 + side][:, :], c(C_SEL2 + side * P, P, 2), row, start=True, stop=True)
                else:
                    for b in range(4):
                        mm = nc.tensor.matmul(ps[2][:, 2 * b:2 * b + 2], row[:, b * P:(b + 1) * P],
                                              c(C_ID, 2, 2), start=True, stop=True)
                mm.then_inc(S("spread"), 1)

            pe.wait_ge(S("condr"), 2)
            for n in range(NB):
                products(n)
                if n >= 1:
                    spread(n - 1)
            spread(NB - 1)

        @block.scalar
        def _(act):
            act.wait_ge(S("condr0"), 1)
            nc.scalar.copy(cpart(0)[:, 0:2 * KD], cond[:, :]).then_inc(S("condr"), 1)
            for n in range(NB):
                act.wait_ge(S(f"w{n % SLOTS}"), 16 * (n // SLOTS + 1))
                if n >= 2:
                    act.wait_ge(S("mm"), n - 1)
                split_high(nc, act, raw[n % SLOTS], high(n)).then_inc(S("high"), 1)

        @block.vector
        def _(dve):
            nc.vector.memset(condr[:, :].bitcast(F32), 0.0).then_inc(S("condr0"), 1)
            dve.wait_ge(S("condr"), 1)
            split_low(nc, dve, cond[:, :], cpart(0)[:, 0:2 * KD], cpart(1)[:, 0:2 * KD]).then_inc(S("condr"), 1)
            dve.wait_ge(S("bias"), 16)
            for n in range(NB + 2):
                if n < NB:
                    dve.wait_ge(S("high"), n + 1)
                    if n >= 2:
                        dve.wait_ge(S("mm"), n - 1)
                    split_low(nc, dve, raw[n % SLOTS], high(n), low(n)).then_inc(S("low"), 1)
                if 1 <= n <= NB:
                    m = n - 1
                    dve.wait_ge(S("mm"), m + 1)
                    if m >= 2:
                        dve.wait_ge(S("spread"), m - 1)
                    nc.vector.tensor_tensor(rows[:, (m % 2) * 512:(m % 2 + 1) * 512], ps[m % 2][0:2, :],
                                            bias[:, m * 512:(m + 1) * 512], ALU.add).then_inc(S("row"), 1)
                if n >= 2:
                    m = n - 2
                    dve.wait_ge(S("spread"), m + 1)
                    if m // 2 in (2, 5):
                        g = m // 2 // 3
                        for side in range(2):
                            o = (2 * g + side) * D + (m % 2) * 512
                            ins = nc.vector.tensor_copy(gate[:, o:o + 512], ps[2 + side][:, :])
                    else:
                        ins = nc.vector.tensor_scalar(modc[:, 8 * m:8 * m + 8], ps[2][:, 0:8],
                                                      1.0 if m // 2 in (1, 4) else 0.0, None, ALU.add)
                    ins.then_inc(S("spread_out"), 1)


def transpose_modulate(E, S, hr, layer_tiles, tmp, pe=None, dve=None, act=None, shift=0, scale=1):
    nc, h, ps, modc, ident = (E[k] for k in ("nc", "h", "ps", "modc", "ident"))
    lo = layer_tiles[0] * P
    for k in range(KD):
        buf = tmp[:, (k % 2) * T:(k % 2 + 1) * T]
        if pe:
            if k >= 4:
                pe.wait_ge(S("modulated"), k - 3)
            for j in layer_tiles:
                mm = nc.tensor.transpose(ps[4 + k % 4][:, j * P:(j + 1) * P],
                                         h[:, j * D + k * P:j * D + (k + 1) * P], ident)
            mm.then_inc(S("turned"), 1)
        if act:
            act.wait_ge(S("turned"), k + 1)
            if k >= 2:
                act.wait_ge(S("hT"), k - 1)
            for side in range(layer_tiles[0] // 2, 2):
                a = modc[:, (scale * KD + k) * 2 + side:(scale * KD + k) * 2 + side + 1]
                b = modc[:, (shift * KD + k) * 2 + side:(shift * KD + k) * 2 + side + 1]
                ins = nc.scalar.activation(buf[:, side * SIDE:(side + 1) * SIDE], ps[4 + k % 4][:, side * SIDE:(side + 1) * SIDE],
                                           ACT.Identity, bias=b, scale=a)
            ins.then_inc(S("modulated"), 1)
            act.wait_ge(S("modulated"), k + 1)
            split_high(nc, act, buf[:, lo:], hr[0][:, k * T + lo:(k + 1) * T]).then_inc(S("hT_high"), 1)
        if dve:
            dve.wait_ge(S("hT_high"), k + 1)
            split_low(nc, dve, buf[:, lo:], hr[0][:, k * T + lo:(k + 1) * T], hr[1][:, k * T + lo:(k + 1) * T]).then_inc(S("hT"), 1)


def input_projection(E, layer):
    nc, A, ps, pr, mix = (E[k] for k in ("nc", "A", "ps", "pr", "mix"))
    RAW, SLOTS, W = 4, 3, KD * P
    with Stage(nc) as S, nc.Block() as block:
        hr = [S.sb(f"hr{p}", KD * T, F32R) for p in range(2)]
        wr = S.sb("wr", SLOTS * 2 * W, F32R)
        tmp = S.sb("tmp", 2 * T)

        def raw(m):
            return mix[:, (m % RAW) * W:(m % RAW + 1) * W]

        def part(m, p):
            return wr[:, (2 * (m % SLOTS) + p) * W:(2 * (m % SLOTS) + p + 1) * W]

        @block.sync
        def _(sp):
            for m in range(IN_TILES):
                if m >= RAW:
                    sp.wait_ge(S("low"), m - RAW + 1)
                sp.dma_start(raw(m), A["w_in"][layer, m]).then_inc(S(f"w{m % RAW}"), 16)

        @block.tensor
        def _(pe):
            transpose_modulate(E, S, hr, range(TILES), tmp, pe=pe)
            for m in range(IN_TILES):
                pe.wait_ge(S("high"), m + 1)
                pe.wait_ge(S("low"), m + 1)
                if m >= 4:
                    pe.wait_ge(S(f"out{m % 2}"), m // 2 - 1)
                for k in range(KD):
                    if m == 0:
                        pe.wait_ge(S("hT"), k + 1)
                    mm = product(nc, ps[m % 4][:, :], [part(m, p)[:, k * P:(k + 1) * P] for p in (0, 1)],
                                 [x[:, k * T:(k + 1) * T] for x in hr], k == 0, k == KD - 1)
                mm.then_inc(S("mm"), 1)

        @block.vector
        def _(dve):
            def low(m):
                dve.wait_ge(S("high"), m + 1)
                if m >= SLOTS:
                    dve.wait_ge(S("mm"), m - SLOTS + 1)
                split_low(nc, dve, raw(m), part(m, 0), part(m, 1)).then_inc(S("low"), 1)

            low(0)
            low(1)
            transpose_modulate(E, S, hr, range(TILES), tmp, dve=dve)
            for n in range(IN_TILES):
                if n + 2 < IN_TILES:
                    low(n + 2)
                if n % 2 == 0:
                    dve.wait_ge(S("mm"), n + 1)
                    nc.vector.tensor_copy(pr[:, n * T:(n + 1) * T], ps[n % 4][:, :]).then_inc(S("out0"), 1)

        @block.scalar
        def _(act):
            def high(m):
                act.wait_ge(S(f"w{m % RAW}"), 16 * (m // RAW + 1))
                if m >= SLOTS:
                    act.wait_ge(S("mm"), m - SLOTS + 1)
                split_high(nc, act, raw(m), part(m, 0)).then_inc(S("high"), 1)

            high(0)
            high(1)
            transpose_modulate(E, S, hr, range(TILES), tmp, act=act, shift=0, scale=1)
            for n in range(IN_TILES):
                if n + 2 < IN_TILES:
                    high(n + 2)
                if n % 2 == 1:
                    act.wait_ge(S("mm"), n + 1)
                    nc.scalar.copy(pr[:, n * T:(n + 1) * T], ps[n % 4][:, :]).then_inc(S("out1"), 1)


def tiles(t, first, n):
    return t[:, first * T:(first + n) * T]


def sides(ap, n):
    return ap.rearrange("p (n s t) -> p n s t", n=n, s=2)


def conv_and_sigmoids(E, layer):
    nc, par, pr, work = (E[k] for k in ("nc", "par", "pr", "work"))
    with Stage(nc) as S, nc.Block() as block:
        S("link")
        sf = work[:, 0:4 * T]
        tmp = work[:, 4 * T:4 * T + 10 * T]

        @block.vector
        def _(dve):
            link = linker(dve, S("link"))

            def pc(o, i=0, rows=P):
                return par[0:rows, o + i:o + i + 1]

            t = tmp[:, 0:4 * T]
            z = tiles(pr, T_MQ, 4)
            for i in range(4):
                ins = nc.vector.tensor_scalar(tiles(t, i, 1), tiles(z, i, 1), pc(Q_MCW, 3 * i + 1), pc(Q_MCB, i), ALU.mult, ALU.add)
            link(ins)
            for i in range(4):
                zi, ti = sides(tiles(z, i, 1), 1)[:, 0], sides(tiles(t, i, 1), 1)[:, 0]
                ins = nc.vector.scalar_tensor_tensor(out=ti[:, :, 1:], in0=zi[:, :, :-1], scalar=pc(Q_MCW, 3 * i), in1=ti[:, :, 1:],
                                                     op0=ALU.mult, op1=ALU.add)
            link(ins)
            for i in range(4):
                zi, ti = sides(tiles(z, i, 1), 1)[:, 0], sides(tiles(t, i, 1), 1)[:, 0]
                ins = nc.vector.scalar_tensor_tensor(out=ti[:, :, :-1], in0=zi[:, :, 1:], scalar=pc(Q_MCW, 3 * i + 2), in1=ti[:, :, :-1],
                                                     op0=ALU.mult, op1=ALU.add)
            ins.then_inc(S("conv"), 1)
            dve.wait_ge(S("conv_sig"), 1)
            link(nc.vector.tensor_tensor(tiles(pr, T_MQ, 2), tiles(t, 0, 2), tiles(pr, T_MQ, 2), ALU.mult))
            link(nc.vector.scalar_tensor_tensor(out=tiles(pr, T_MK, 2), in0=tiles(t, 2, 2), scalar=HD ** -0.5, in1=tiles(pr, T_MK, 2),
                                                op0=ALU.mult, op1=ALU.mult))

            for first, n, rows in ((0, 9, P), (9, 1, 32)):
                z = sides(pr[0:rows, first * T:(first + n) * T], n)
                u = sides(tmp[0:rows, first * T:(first + n) * T], n)
                nc.vector.tensor_tensor(u[:, :, :, 1:-1], z[:, :, :, :-2], z[:, :, :, 2:], ALU.add)
                nc.vector.tensor_copy(u[:, :, :, 0], z[:, :, :, 1])
                ins = nc.vector.tensor_copy(u[:, :, :, SIDE - 1], z[:, :, :, SIDE - 2])
            link(ins)
            for first, n, rows in ((0, 9, P), (9, 1, 32)):
                z, u = pr[0:rows, first * T:(first + n) * T], tmp[0:rows, first * T:(first + n) * T]
                ins = nc.vector.scalar_tensor_tensor(out=u, in0=u, scalar=0.5, in1=z, op0=ALU.mult, op1=ALU.subtract)
            link(ins)
            for i in (6, 7, 8, 9, 0, 1, 2, 3, 4, 5):
                rows = P if i < 9 else 32
                z, u = pr[0:rows, i * T:(i + 1) * T], tmp[0:rows, i * T:(i + 1) * T]
                ins = nc.vector.scalar_tensor_tensor(out=z, in0=u, scalar=pc(Q_MU, i, rows), in1=z, op0=ALU.mult, op1=ALU.add)
                if i == 9:
                    ins.then_inc(S("shifted"), 1)
            ins.then_inc(S("tmp_free"), 1)
            for n, (t0, o) in enumerate(((T_HQ, 0), (T_HG, 2))):
                dve.wait_ge(S("silu_sig"), n + 1)
                nc.vector.tensor_tensor(tiles(pr, t0, 2), tiles(pr, t0, 2), tiles(tmp, o, 2), ALU.mult)

        @block.scalar
        def _(act):
            nc.scalar.activation(sf, tiles(pr, T_HF, 4), ACT.Sigmoid).then_inc(S("sf"), 1)
            nc.scalar.activation(tiles(pr, T_MO, 2), tiles(pr, T_MO, 2), ACT.Sigmoid)
            act.wait_ge(S("sf"), 1)
            nc.scalar.activation(tiles(pr, T_HF, 4), tiles(pr, T_HF, 4), ACT.Sigmoid, scale=-1.0)
            act.wait_ge(S("conv"), 1)
            nc.scalar.activation(tiles(pr, T_MQ, 4), tiles(tmp, 0, 4), ACT.Sigmoid).then_inc(S("conv_sig"), 1)
            act.wait_ge(S("shifted"), 1)
            nc.scalar.activation(tiles(pr, T_WD, 1), tiles(pr, T_WD, 1), ACT.Tanh)
            nc.scalar.activation(tiles(pr, T_GD, 1), tiles(pr, T_GD, 1), ACT.Sigmoid)
            nc.scalar.activation(pr[0:32, T_GD2 * T:(T_GD2 + 1) * T], pr[0:32, T_GD2 * T:(T_GD2 + 1) * T], ACT.Sigmoid)
            act.wait_ge(S("tmp_free"), 1)
            for t0, o in ((T_HQ, 0), (T_HG, 2)):
                nc.scalar.activation(tiles(tmp, o, 2), tiles(pr, t0, 2), ACT.Sigmoid).then_inc(S("silu_sig"), 1)


def active(layer):
    return (0, 1, 2, 3) if layer < DEPTH - 1 else (2, 3)


def span(layer):
    lo = active(layer)[0] * P
    return lo, T - lo


def two(t, layer):
    lo, n = span(layer)
    return t.rearrange("p (i t) -> p i t", i=2)[:, :, lo:]


def halves(t, B, second):
    v = t.rearrange("p (m b t) -> p m b t", b=P // B, t=B)
    return v[:, :, :, B // 2:] if second else v[:, :, :, :B // 2]


def head_sums(E, pe, src, banks, layer):
    nc, c, ps = E["nc"], E["c"], E["ps"]
    lo, n = span(layer)
    for i in range(2):
        mm = nc.tensor.matmul(ps[banks[i]][:, lo:], c(C_HONES), src[:, i * T + lo:(i + 1) * T], start=True, stop=True)
    return mm


def diff_attention(E, layer):
    nc, A, c, par, pr, work, mix, ps, ident = (E[k] for k in ("nc", "A", "c", "par", "pr", "work", "mix", "ps", "ident"))
    act_tiles = active(layer)
    units = [(i, j, hh) for i in range(2) for j in act_tiles for hh in range(2)]
    lam_init = 0.8 - 0.6 * float(np.exp(-0.3 * layer))
    scale = (HD // 2) ** -0.5
    vT = work[:, 2048:2048 + 1024]
    e = work[:, 3072:3072 + 2048]
    prob = work[:, 5120:5120 + 1024]
    pT = work[:, 6144:6144 + 1024]
    rtmp = work[:, 7168:7168 + 1024]
    y = work[:, 8192:8192 + 1024]
    st = work[:, 9216:9216 + 256]
    sq = work[:, 9472:9472 + 1024]

    with Stage(nc) as S, nc.Block() as block:
        for n in ("link", "link_act"):
            S(n)

        def keys(j):
            return (0, SIDE) if j < 2 else (0, T)

        def score_bank(u, q):
            return 6 * (u % 2) + q

        @block.tensor
        def _(pe):
            for m in range(4):
                mm = nc.tensor.matmul(ps[m // 2][:, (m % 2) * SIDE:(m % 2 + 1) * SIDE], c(C_ROT),
                                      pr[:, (T_DQ + m) * T + SIDE:(T_DQ + m + 1) * T], start=True, stop=True)
            mm.then_inc(S("rot"), 1)
            for j in range(TILES):
                for i in range(2):
                    mm = nc.tensor.transpose(ps[2 + j // 2][:, (j % 2) * 256 + i * P:(j % 2) * 256 + (i + 1) * P],
                                             pr[:, (T_DV + i) * T + j * P:(T_DV + i) * T + (j + 1) * P], ident)
            mm.then_inc(S("vT"), 1)
            pe.wait_ge(S("roped"), 1)
            pe.wait_ge(S("vT_out"), 1)

            def scores(u):
                i, j, hh = units[u]
                if u >= 2:
                    pe.wait_ge(S("exp"), 2 * u - 2)
                lo, n = keys(j)
                for q in range(2):
                    r = hh * HD + q * 32
                    mm = nc.tensor.matmul(ps[score_bank(u, q)][:, 0:n], pr[r:r + 32, (T_DQ + i) * T + j * P:(T_DQ + i) * T + (j + 1) * P],
                                          pr[r:r + 32, (T_DK + i) * T:(T_DK + i) * T + n], start=True, stop=True,
                                          tile_position=(r, 0))
                mm.then_inc(S("scores"), 1)

            def turn(u):
                pe.wait_ge(S("prob"), u + 1)
                if u >= 2:
                    pe.wait_ge(S("pT"), u - 1)
                n = keys(units[u][1])[1]
                for b in range(n // P):
                    mm = nc.tensor.transpose(ps[2 + u % 2][:, b * P:(b + 1) * P],
                                             prob[:, (u % 2) * T + b * P:(u % 2) * T + (b + 1) * P], ident)
                mm.then_inc(S("turned"), 1)

            def values(u):
                i, j, hh = units[u]
                pe.wait_ge(S("pT"), u + 1)
                n = keys(j)[1] // P
                for b in range(n):
                    mm = nc.tensor.matmul(ps[4 + i][hh * HD:(hh + 1) * HD, j * P:(j + 1) * P],
                                          vT[:, b * 256 + i * P + hh * HD:b * 256 + i * P + (hh + 1) * HD],
                                          pT[:, (u % 2) * T + b * P:(u % 2) * T + (b + 1) * P],
                                          start=(b == 0), stop=(b == n - 1))
                mm.then_inc(S("values"), 1)

            for u in range(len(units) + 3):
                if u < len(units):
                    scores(u)
                if 2 <= u <= len(units) + 1:
                    turn(u - 2)
                if u >= 3:
                    values(u - 3)
            pe.wait_ge(S("sq"), 1)
            head_sums(E, pe, sq, (6, 7), layer).then_inc(S("ss"), 1)

        @block.vector
        def _(dve):
            link = linker(dve, S("link"))
            lam = par[:, Q_LAM:Q_LAM + 128].rearrange("p (a b d) -> p a b d", a=2, b=2)
            link(nc.vector.tensor_tensor(st[:, 0:64].rearrange("p (a d) -> p a d", a=2), lam[:, :, 0, :], lam[:, :, 1, :], ALU.mult))
            nc.vector.tensor_reduce(st[:, 64:66], st[:, 0:64].rearrange("p (a d) -> p a d", a=2), AX_X, ALU.add).then_inc(S("lam_in"), 1)
            cosb = c(C_COS, SIDE).rearrange("p (i t) -> p i t", i=1).to_broadcast([P, 4, SIDE])
            sinb = c(C_SIN, SIDE).rearrange("p (i t) -> p i t", i=1).to_broadcast([P, 4, SIDE])
            qk = tiles(pr, T_DQ, 4).rearrange("p (m t) -> p m t", m=4)[:, :, SIDE:]
            rt = rtmp.rearrange("p (m t) -> p m t", m=4)
            dve.wait_ge(S("rot"), 1)
            for b in range(2):
                nc.vector.tensor_tensor(rt[:, 2 * b:2 * b + 2, :], ps[b][:, :].rearrange("p (m t) -> p m t", m=2),
                                        sinb[:, 0:2, :], ALU.mult)
            link(nc.vector.tensor_tensor(qk, qk, cosb, ALU.mult))
            nc.vector.tensor_tensor(qk, qk, rt, ALU.add).then_inc(S("roped"), 1)
            dve.wait_ge(S("lam_exp"), 1)
            link(nc.vector.tensor_tensor(st[:, 68:69], st[:, 67:68], st[:, 66:67], ALU.subtract))
            link(nc.vector.tensor_scalar(st[:, 69:70], st[:, 68:69], -lam_init, None, ALU.add))

            def maxima(u):
                dve.wait_ge(S("scores"), u + 1)
                if u >= 2:
                    dve.wait_ge(S("exp"), 2 * u - 2)
                n = keys(units[u][1])[1]
                for q in range(2):
                    ins = nc.vector.tensor_reduce(st[:, 80 + 8 * (u % 2) + q:81 + 8 * (u % 2) + q], ps[score_bank(u, q)][:, 0:n], AX_X, ALU.max)
                link(ins)
                s = 80 + 8 * (u % 2)
                nc.vector.tensor_scalar(st[:, s + 2:s + 4], st[:, s:s + 2], -scale, None, ALU.mult).then_inc(S("max"), 1)

            def combine(u):
                s = 80 + 8 * (u % 2)
                n = keys(units[u][1])[1]
                dve.wait_ge(S("exp"), 2 * u + 2)
                link(nc.vector.reciprocal(st[:, s + 6:s + 8], st[:, s + 4:s + 6]))
                link(nc.vector.tensor_tensor(st[:, s + 7:s + 8], st[:, s + 7:s + 8], st[:, 69:70], ALU.mult))
                e0, e1 = (e[:, (u % 2) * 1024 + q * 512:(u % 2) * 1024 + q * 512 + n] for q in range(2))
                link(nc.vector.tensor_scalar(e1, e1, st[:, s + 7:s + 8], None, ALU.mult))
                if u >= 2:
                    dve.wait_ge(S("turned"), u - 1)
                nc.vector.scalar_tensor_tensor(out=prob[:, (u % 2) * T:(u % 2) * T + n], in0=e0, scalar=st[:, s + 6:s + 7], in1=e1,
                                               op0=ALU.mult, op1=ALU.add).then_inc(S("prob"), 1)

            for u in range(len(units) + 1):
                if u < len(units):
                    maxima(u)
                if u >= 1:
                    combine(u - 1)
            dve.wait_ge(S("values"), len(units))
            lo, n = span(layer)
            for i in range(2):
                ins = nc.vector.tensor_copy(y[:, i * T + lo:(i + 1) * T], ps[4 + i][:, lo:])
            link(ins)
            nc.vector.tensor_tensor(two(sq, layer), two(y, layer), two(y, layer), ALU.mult).then_inc(S("sq"), 1)
            dve.wait_ge(S("rn"), 1)
            link(nc.vector.tensor_tensor(two(y, layer), two(y, layer), two(sq, layer), ALU.mult))
            nc.vector.tensor_scalar(two(tiles(mix, 2, 2), layer), two(y, layer), par[:, Q_DN:Q_DN + 1], 1.0 - lam_init,
                                    ALU.mult, ALU.mult)

        @block.scalar
        def _(act):
            act.wait_ge(S("vT"), 1)
            nc.scalar.copy(vT[:, 0:512], ps[2][:, :])
            nc.scalar.copy(vT[:, 512:1024], ps[3][:, :]).then_inc(S("vT_out"), 1)
            act.wait_ge(S("lam_in"), 1)
            nc.scalar.activation(st[:, 66:68], st[:, 64:66], ACT.Exp).then_inc(S("lam_exp"), 1)

            def exps(u):
                s = 80 + 8 * (u % 2)
                n = keys(units[u][1])[1]
                act.wait_ge(S("max"), u + 1)
                if u >= 2:
                    act.wait_ge(S("prob"), u - 1)
                for q in range(2):
                    nc.scalar.activation(e[:, (u % 2) * 1024 + q * 512:(u % 2) * 1024 + q * 512 + n], ps[score_bank(u, q)][:, 0:n], ACT.Exp,
                                         bias=st[:, s + 2 + q:s + 3 + q], scale=scale,
                                         accum_out=st[:, s + 4 + q:s + 5 + q]).then_inc(S("exp"), 1)

            def pt_out(u):
                n = keys(units[u][1])[1]
                act.wait_ge(S("turned"), u + 1)
                if u >= 2:
                    act.wait_ge(S("values"), u - 1)
                nc.scalar.copy(pT[:, (u % 2) * T:(u % 2) * T + n], ps[2 + u % 2][:, 0:n]).then_inc(S("pT"), 1)

            for u in range(len(units) + 2):
                if u < len(units):
                    exps(u)
                if u >= 2:
                    pt_out(u - 2)
            inverse_rms(E, S, act, (6, 7), sq, layer, 1.0 / HD, Q_EPS)


def inverse_rms(E, S, act, banks, dst, layer, scale, eps):
    nc, ps, par = E["nc"], E["ps"], E["par"]
    lo, n = span(layer)
    act.wait_ge(S("ss"), 1)
    for i in range(2):
        ins = nc.scalar.activation(dst[:, i * T + lo:(i + 1) * T], ps[banks[i]][:, lo:], ACT.Ln, bias=par[:, eps:eps + 1], scale=scale)
    ins.then_inc(S("ln"), 1)
    act.wait_ge(S("ln"), 1)
    nc.scalar.activation(two(dst, layer), two(dst, layer), ACT.Exp, scale=-0.5).then_inc(S("rn"), 1)


def mlstm(E, layer):
    nc, c, par, pr, work, mix, ps, ident = (E[k] for k in ("nc", "c", "par", "pr", "work", "mix", "ps", "ident"))
    js = active(layer)
    lo0, n0 = span(layer)
    PADW = P + SIDE
    o = [2048]

    def take(n):
        o[0] += n
        return work[:, o[0] - n:o[0]]

    vT = take(1024)
    w = take(4096)
    x = take(1024)
    pad = take(3072)[0:4, :]
    brow = take(1024)[0:4, :]
    floor = pr[0:4, T_DQ * T:(T_DQ + 2) * T]
    small = pr[:, (T_DQ + 2) * T:(T_DQ + 3) * T]
    gt = small[:, 0:64].rearrange("p (j g) -> p j g", j=TILES)
    lf = small[:, 64:96]
    la, lb_, gc = small[:, 96:128], small[:, 128:160], small[:, 160:192]
    ys = tiles(pr, T_DQ + 3, 2)
    y = tiles(mix, 6, 2)
    sq = x

    def padded(d, pp):
        return pad[:, (2 * d + pp) * 2 * PADW:(2 * d + pp + 1) * 2 * PADW].rearrange("p (s t) -> p s t", s=2)

    def own(d, pp, shift=0):
        a = P - shift if d == 0 else shift
        return padded(d, pp)[:, :, a:a + SIDE]

    def reach(d, s):
        lo = s * P if d == 0 else (0 if s < 2 else SIDE)
        return max(lo, lo0), (T if (d == 0 or s != 2) else 3 * P)

    def earlier(d, j):
        return ORDER[d][:ORDER[d].index(j)]

    with Stage(nc) as S, nc.Block() as block:
        for n in ("link", "vT", "gates", "rows", "cols", "mb", "qk", "w", "values", "x", "e"):
            S(n)

        @block.tensor
        def _(pe):
            for j in range(TILES):
                mm = nc.tensor.transpose(ps[0][:, j * 64:(j + 1) * 64], pr[0:64, T_GD2 * T + j * P:T_GD2 * T + (j + 1) * P], c(C_ID, 64, 64))
            mm.then_inc(S("gates"), 1)
            for j in range(TILES):
                for i in range(2):
                    mm = nc.tensor.transpose(ps[1 + j // 2][:, (j % 2) * 256 + i * P:(j % 2) * 256 + (i + 1) * P],
                                             pr[:, (T_MV + i) * T + j * P:(T_MV + i) * T + (j + 1) * P], ident)
            mm.then_inc(S("vT"), 1)
            pe.wait_ge(S("lf"), 1)
            for d in range(2):
                for j in range(TILES):
                    out = ps[3 + d][0:4, j * P:(j + 1) * P]
                    for n, s in enumerate((*earlier(d, j), j)):
                        nc.tensor.matmul(out, lf[:, s * 8 + d * 4:s * 8 + d * 4 + 4], c(C_ONES) if s != j else c(C_TRI + d * P),
                                         start=(n == 0), stop=(s == j))
                for j in range(TILES):
                    nc.tensor.matmul(ps[5 + d][0:4, j * P:(j + 1) * P], gt[:, j, d * 4:d * 4 + 4], ident, start=True, stop=True)
            for d in range(2):
                for j in range(TILES):
                    out = ps[7][:, j * 8 + d * 4:j * 8 + d * 4 + 4]
                    for n, s in enumerate((*earlier(d, j), j)):
                        mm = nc.tensor.matmul(out, c(C_ONES) if s != j else c(C_TRI + d * P), lf[:, s * 8 + d * 4:s * 8 + d * 4 + 4],
                                              start=(n == 0), stop=(s == j))
            mm.then_inc(S("rows"), 1)
            pe.wait_ge(S("vT_out"), 1)

            def broadcasts(hd):
                if hd == 0:
                    pe.wait_ge(S("maxed"), 1)
                else:
                    pe.wait_ge(S("x"), 2 * TILES * hd)
                if hd == 2:
                    pe.wait_ge(S("pair_out"), 2)
                for d in range(2):
                    M = own(d, 0)[:, lo0 // SIDE:, :]
                    mm = nc.tensor.matmul(ps[d][:, lo0:], c(C_SELH + hd * P, P, 4), M, start=True, stop=True)
                mm.then_inc(S("mb"), 1)

            def qk(hd, s):
                n = TILES * hd + s
                if n >= 2:
                    pe.wait_ge(S("w"), 2 * (n - 1))
                r = (hd % 2) * HD
                i = hd // 2
                lo = lo0 if s < 2 else SIDE
                nc.tensor.matmul(ps[2 + s % 2][:, lo:], pr[r:r + HD, (T_MK + i) * T + s * P:(T_MK + i) * T + (s + 1) * P],
                                 pr[r:r + HD, (T_MQ + i) * T + lo:(T_MQ + i + 1) * T], start=True, stop=True).then_inc(S("qk"), 1)

            def values(hd):
                r = (hd % 2) * HD
                pe.wait_ge(S("w"), 2 * TILES * (hd + 1))
                pe.wait_ge(S("masked"), 1 + hd)
                if hd == 2:
                    pe.wait_ge(S("pair_out"), 2)
                for d in range(2):
                    for j in js:
                        seen = (*earlier(d, j), j)
                        for bank, lhs in ((4 + d, None), (6 + d, c(C_ONES, HD))):
                            for n, s in enumerate(seen):
                                l = lhs if lhs is not None else vT[:, s * 256 + hd * HD:s * 256 + (hd + 1) * HD]
                                mm = nc.tensor.matmul(ps[bank][r:r + HD, j * P:(j + 1) * P], l,
                                                      w[:, d * 2048 + s * T + j * P:d * 2048 + s * T + (j + 1) * P],
                                                      start=(n == 0), stop=(n == len(seen) - 1))
                mm.then_inc(S("values"), 1)

            for hd in range(HEADS):
                broadcasts(hd)
                for s in range(TILES):
                    qk(hd, s)
                values(hd)
                if hd % 2:
                    pe.wait_ge(S("floor"), 1)
                    for d in range(2):
                        mm = nc.tensor.matmul(ps[d][:, lo0:], c(C_SELP + (hd // 2) * P, P, 4), floor[:, d * T + lo0:(d + 1) * T],
                                              start=True, stop=True)
                    mm.then_inc(S("floor_b"), 1)
            pe.wait_ge(S("pair_out"), 4)
            head_sums(E, pe, y, (6, 7), layer).then_inc(S("mean"), 1)
            pe.wait_ge(S("sq"), 1)
            head_sums(E, pe, sq, (4, 5), layer).then_inc(S("ss"), 1)

        @block.gpsimd
        def _(pool):
            pool.memset(pad[:, :], 0.0).then_inc(S("pad0"), 1)
            for hd in range(HEADS):
                pool.wait_ge(S("w"), 2 * TILES * (hd + 1))
                for d in range(2):
                    for j in js:
                        b = w[:, d * 2048 + j * T + j * P:d * 2048 + j * T + (j + 1) * P]
                        ins = nc.gpsimd.tensor_tensor(b, b, c(C_TRI + d * P), ALU.mult)
                ins.then_inc(S("masked"), 1)

        @block.vector
        def _(dve):
            link = linker(dve, S("link"))
            dve.wait_ge(S("gates"), 1)
            gb = par[:, Q_GB:Q_GB + 16].rearrange("p (j g) -> p j g", j=1).to_broadcast([P, TILES, 16])
            g4 = small[:, 0:64].rearrange("p (j g) -> p j g", j=TILES)
            link(nc.vector.tensor_tensor(g4, ps[0][:, 0:256].rearrange("p (j g) -> p j g", j=TILES)[:, :, GATE_ROW:GATE_ROW + 16], gb, ALU.add))
            f = g4[:, :, 8:16]
            lf3, la3, lb3 = (v.rearrange("p (j g) -> p j g", j=TILES) for v in (lf, la, lb_))
            link(nc.vector.tensor_scalar(la3, f, -1.0, None, ALU.mult))
            link(nc.vector.tensor_tensor(la3, la3, f, ALU.min))
            nc.vector.tensor_scalar(lb3, f, 0.0, None, ALU.min).then_inc(S("absf"), 1)
            dve.wait_ge(S("lnf"), 1)
            nc.vector.tensor_tensor(lf3, lb3, la3, ALU.subtract).then_inc(S("lf"), 1)
            dve.wait_ge(S("pad0"), 1)
            dve.wait_ge(S("brow"), 1)
            for d in range(2):
                ins = nc.vector.tensor_tensor(own(d, 0), ps[5 + d][0:4, :].rearrange("p (s t) -> p s t", s=2),
                                              brow[:, d * T:(d + 1) * T].rearrange("p (s t) -> p s t", s=2), ALU.subtract)
            link(ins)
            nc.vector.tensor_tensor(gc.rearrange("p (j g) -> p j g", j=TILES), g4[:, :, 0:8],
                                    ps[7][:, 0:32].rearrange("p (j g) -> p j g", j=TILES), ALU.subtract)
            pp = 0
            for k in (1, 2, 4, 8, 16, 32, 64, 128):
                for d in range(2):
                    ins = nc.vector.tensor_tensor(own(d, 1 - pp), own(d, pp), own(d, pp, k), ALU.max)
                link(ins)
                pp = 1 - pp
            for d in range(2):
                end = own(d, 0)[:, 0, SIDE - 1:SIDE] if d == 0 else own(d, 0)[:, 0, 0:1]
                ins = nc.vector.tensor_scalar(own(d, 0)[:, 1, :], own(d, 0)[:, 1, :], end, 0.0, ALU.max, ALU.max)
            link(ins)
            for d in range(2):
                ins = nc.vector.tensor_scalar(own(d, 0)[:, 0, :], own(d, 0)[:, 0, :], 0.0, None, ALU.max)
            ins.then_inc(S("maxed"), 1)
            dve.wait_ge(S("maxed"), 1)
            for d in range(2):
                ins = nc.vector.tensor_tensor(floor[:, d * T:(d + 1) * T].rearrange("p (s t) -> p s t", s=2), own(d, 0),
                                              brow[:, d * T:(d + 1) * T].rearrange("p (s t) -> p s t", s=2), ALU.add)
            link(ins)
            nc.vector.tensor_scalar(floor, floor, -1.0, 60.0, ALU.mult, ALU.min).then_inc(S("floor_in"), 1)

            def exponents(hd, s):
                for d in range(2):
                    n = 2 * (TILES * hd + s) + d
                    if n >= 2:
                        dve.wait_ge(S("w"), n - 1)
                    a, b = reach(d, s)
                    nc.vector.tensor_scalar(x[:, d * T + a:d * T + b], ps[d][:, a:b], gc[:, s * 8 + d * 4 + hd:s * 8 + d * 4 + hd + 1],
                                            0.0, ALU.subtract, ALU.max).then_inc(S("x"), 1)

            def weights(hd, s):
                dve.wait_ge(S("qk"), TILES * hd + s + 1)
                if hd >= 1:
                    dve.wait_ge(S("values"), hd)
                for d in range(2):
                    dve.wait_ge(S("e"), 2 * (TILES * hd + s) + d + 1)
                    a, b = reach(d, s)
                    nc.vector.tensor_tensor(w[:, d * 2048 + s * T + a:d * 2048 + s * T + b], x[:, d * T + a:d * T + b],
                                            ps[2 + s % 2][:, a:b], ALU.mult).then_inc(S("w"), 1)

            for hd in range(HEADS):
                dve.wait_ge(S("mb"), hd + 1)
                for s in range(TILES):
                    exponents(hd, s)
                    weights(hd, s)
                if hd % 2:
                    i = hd // 2
                    dve.wait_ge(S("den"), 2 * (i + 1))
                    dve.wait_ge(S("floor_b"), i + 1)
                    for d in range(2):
                        yd = ys[:, d * T + lo0:(d + 1) * T]
                        link(nc.vector.tensor_tensor(yd, yd, ps[d][:, lo0:], ALU.max))
                        link(nc.vector.reciprocal(yd, yd))
                        ins = nc.vector.tensor_tensor(yd, yd, ps[4 + d][:, lo0:], ALU.mult)
                        ins.then_inc(S("pair_y"), 1)
                    dve.wait_ge(S("pair_y"), 2 * (i + 1))
                    nc.vector.tensor_tensor(y[:, i * T + lo0:(i + 1) * T], ys[:, lo0:T], ys[:, T + lo0:2 * T], ALU.add).then_inc(S("pair_out"), 2)
            dve.wait_ge(S("pair_out"), 4)
            dve.wait_ge(S("mean"), 1)
            for i in range(2):
                v = y[:, i * T + lo0:(i + 1) * T]
                ins = nc.vector.scalar_tensor_tensor(out=v, in0=ps[6 + i][:, lo0:], scalar=-1.0 / HD, in1=v, op0=ALU.mult, op1=ALU.add)
            link(ins)
            nc.vector.tensor_tensor(two(sq, layer), two(y, layer), two(y, layer), ALU.mult).then_inc(S("sq"), 1)
            dve.wait_ge(S("rn"), 1)
            link(nc.vector.tensor_tensor(two(y, layer), two(y, layer), two(sq, layer), ALU.mult))
            for i in range(2):
                v = y[:, i * T + lo0:(i + 1) * T]
                nc.vector.scalar_tensor_tensor(out=v, in0=v, scalar=par[:, Q_MN + i:Q_MN + i + 1],
                                               in1=pr[:, (T_MO + i) * T + lo0:(T_MO + i + 1) * T], op0=ALU.mult, op1=ALU.mult)

        @block.scalar
        def _(act):
            act.wait_ge(S("vT"), 1)
            nc.scalar.copy(vT[:, 0:512], ps[1][:, :])
            nc.scalar.copy(vT[:, 512:1024], ps[2][:, :]).then_inc(S("vT_out"), 1)
            act.wait_ge(S("absf"), 1)
            nc.scalar.activation(la, la, ACT.Exp).then_inc(S("link_act"), 1)
            act.wait_ge(S("link_act"), 1)
            nc.scalar.activation(la, la, ACT.Ln, bias=1.0).then_inc(S("lnf"), 1)
            act.wait_ge(S("rows"), 1)
            nc.scalar.copy(brow[:, 0:T], ps[3][0:4, :])
            nc.scalar.copy(brow[:, T:2 * T], ps[4][0:4, :]).then_inc(S("brow"), 1)
            act.wait_ge(S("floor_in"), 1)
            nc.scalar.activation(floor, floor, ACT.Exp).then_inc(S("floor"), 1)
            for hd in range(HEADS):
                for s in range(TILES):
                    for d in range(2):
                        act.wait_ge(S("x"), 2 * (TILES * hd + s) + d + 1)
                        a, b = reach(d, s)
                        nc.scalar.activation(x[:, d * T + a:d * T + b], x[:, d * T + a:d * T + b], ACT.Exp, scale=-1.0).then_inc(S("e"), 1)
                if hd % 2:
                    act.wait_ge(S("values"), hd + 1)
                    if hd == 3:
                        act.wait_ge(S("pair_out"), 2)
                    for d in range(2):
                        nc.scalar.activation(ys[:, d * T + lo0:(d + 1) * T], ps[6 + d][:, lo0:], ACT.Abs).then_inc(S("den"), 1)
            inverse_rms(E, S, act, (4, 5), sq, layer, 1.0 / HD, Q_EPS)


def hgrn(E, layer):
    nc, c, par, pr, work, mix, ring, ps, ident = (E[k] for k in ("nc", "c", "par", "pr", "work", "mix", "ring", "ps", "ident"))
    js = active(layer)
    lo0, n0 = span(layer)
    o = [0]

    def take(n):
        o[0] += n
        return work[:, o[0] - n:o[0]]

    cum = take(2048)
    lT = take(2048)
    vT = take(1024)
    at = take(4096)
    st = take(1024)
    A0 = take(3072)
    A1 = tiles(pr, T_DQ, 6)
    expo = (A0[:, 0:1024], A1[:, 0:1024])
    keys = (A0[:, 2048:3072], A1[:, 2048:3072])
    queries = (ring[:, 0:2048], ring[:, 2048:4096])
    qd = pr[:, T_MQ * T:(T_MQ + 4) * T]
    kd = pr[:, (T_MQ + 4) * T:(T_MQ + 8) * T]
    y = tiles(mix, 4, 2)
    sq = A0[:, 0:1024]
    col = tiles(mix, 0, 1)[:, 0:16]
    ecol = tiles(mix, 0, 1)[:, 16:32]
    nb = len(js) // 2
    steps = [(d, l) for l in range(LEVELS) for d in range(2)]

    with Stage(nc) as S, nc.Block() as block:
        for n in ("link", "at", "s_mm", "qf", "kf"):
            S(n)

        def end(d):
            return P - 1 if d == 0 else 0

        def blocks(t, l):
            return t.rearrange("p (i b t) -> p i b t", i=2, t=2 << l)[:, :, lo0 // (2 << l):, :]

        def half(t, l, second):
            h_ = 1 << l
            return blocks(t, l)[:, :, :, h_:] if second else blocks(t, l)[:, :, :, :h_]

        def later(t, d, l):
            return blocks(t, 0) if l == 0 else half(t, l, d == 0)

        def score_bank(n, j):
            return ps[4 * (n % 2) + j]

        def sooner(t, d, l):
            return blocks(t, 0) if l == 0 else half(t, l, d == 1)

        @block.tensor
        def _(pe):
            for j in range(TILES):
                for i in range(2):
                    mm = nc.tensor.transpose(ps[j // 2][:, (j % 2) * 256 + i * P:(j % 2) * 256 + (i + 1) * P],
                                             pr[:, (T_HI + i) * T + j * P:(T_HI + i) * T + (j + 1) * P], ident)
            mm.then_inc(S("vT"), 1)
            pe.wait_ge(S("logf"), 1)
            for d in range(2):
                for j in range(TILES):
                    for i in range(2):
                        mm = nc.tensor.transpose(ps[2 + 2 * d + j // 2][:, (j % 2) * 256 + i * P:(j % 2) * 256 + (i + 1) * P],
                                                 cum[:, (2 * d + i) * T + j * P:(2 * d + i) * T + (j + 1) * P], ident)
            mm.then_inc(S("lT"), 1)
            pe.wait_ge(S("lT_out"), 2)
            pe.wait_ge(S("vT_out"), 1)
            for d in range(2):
                for i in range(2):
                    for j in range(TILES):
                        mm = nc.tensor.matmul(ps[(6, 7, 0, 1)[2 * d + i]][:, j * P:(j + 1) * P],
                                              lT[:, (d * TILES + j) * 256 + i * P:(d * TILES + j) * 256 + (i + 1) * P],
                                              c(C_TRI + d * P), start=True, stop=True)
            mm.then_inc(S("cum"), 1)
            pe.wait_ge(S("kd"), 1)
            for d in range(2):
                for j in range(TILES):
                    for i in range(2):
                        mm = nc.tensor.transpose(ps[2 + 2 * d + j // 2][:, (j % 2) * 256 + i * P:(j % 2) * 256 + (i + 1) * P],
                                                 kd[:, (2 * d + i) * T + j * P:(2 * d + i) * T + (j + 1) * P], ident)
            mm.then_inc(S("kT"), 1)
            pe.wait_ge(S("kT_out"), 2)
            for d in range(2):
                for j in range(TILES):
                    for hd in range(HEADS):
                        r, i = (hd % 2) * HD, hd // 2
                        mm = nc.tensor.matmul(ps[6 + d][r:r + HD, (2 * j + i) * HD:(2 * j + i + 1) * HD],
                                              lT[:, (d * TILES + j) * 256 + hd * HD:(d * TILES + j) * 256 + (hd + 1) * HD],
                                              vT[:, j * 256 + hd * HD:j * 256 + (hd + 1) * HD], start=True, stop=True)
            mm.then_inc(S("kv"), 1)
            for n, (d, l) in enumerate(steps):
                pe.wait_ge(S("kf"), n + 1)
                for m, j in enumerate(js):
                    if n >= 2:
                        pe.wait_ge(S("at"), len(js) * (n - 2) + m + 1)
                    for i in range(2):
                        t0 = i * T + j * P
                        both = queries[d].rearrange("p (q t) -> p q t", q=2)[:, :, t0:t0 + P]
                        mm = nc.tensor.matmul(score_bank(n, j)[:, i * 256:(i + 1) * 256], keys[d][:, t0:t0 + P], both, start=True, stop=True)
                    mm.then_inc(S("s_mm"), 1)
            pe.wait_ge(S("at"), len(js) * len(steps))
            for hd in range(HEADS):
                r, i = (hd % 2) * HD, hd // 2
                for j in js:
                    terms = []
                    for d in range(2):
                        terms.append((vT[:, j * 256 + hd * HD:j * 256 + (hd + 1) * HD],
                                      at[:, d * 2048 + (4 * j + hd) * P:d * 2048 + (4 * j + hd + 1) * P]))
                    for d in range(2):
                        if ORDER[d].index(j) > 0:
                            terms.append((st[r:r + HD, d * 512 + (2 * j + i) * HD:d * 512 + (2 * j + i + 1) * HD],
                                          qd[r:r + HD, (2 * d + i) * T + j * P:(2 * d + i) * T + (j + 1) * P]))
                    for n, (l, rh) in enumerate(terms):
                        mm = nc.tensor.matmul(ps[4 + i][r:r + HD, j * P:(j + 1) * P], l, rh, start=(n == 0), stop=(n == len(terms) - 1))
            mm.then_inc(S("y"), 1)
            pe.wait_ge(S("sq"), 1)
            head_sums(E, pe, sq, (6, 7), layer).then_inc(S("ss"), 1)

        @block.gpsimd
        def _(pool):
            nc.gpsimd.memset(ring[:, :], 0.0)
            nc.gpsimd.memset(at[:, :], 0.0).then_inc(S("at0"), 1)

        @block.vector
        def _(dve):
            link = linker(dve, S("link"))
            if layer == 0:
                link(nc.vector.memset(col[:, 0:2], 0.0))
            else:
                nc.vector.tensor_tensor(col[:, 4:6], par[:, Q_LB:Q_LB + 2], par[:, Q_LB + 2:Q_LB + 4], ALU.max).then_inc(S("lb_max"), 1)
                dve.wait_ge(S("lb_max"), 1)
                link(nc.vector.tensor_tensor(col[:, 6:8], par[:, Q_LB:Q_LB + 2], col[:, 4:6], ALU.subtract))
                nc.vector.tensor_tensor(col[:, 8:10], par[:, Q_LB + 2:Q_LB + 4], col[:, 4:6], ALU.subtract).then_inc(S("lb_in"), 1)
                dve.wait_ge(S("lb_exp"), 1)
                link(nc.vector.tensor_tensor(col[:, 10:12], col[:, 6:8], col[:, 8:10], ALU.add))
                link(nc.vector.reciprocal(col[:, 10:12], col[:, 10:12]))
                link(nc.vector.tensor_tensor(col[:, 0:2], col[:, 8:10], col[:, 10:12], ALU.mult))
            nc.vector.tensor_scalar(col[:, 2:4], col[:, 0:2], -1.0, 1.0, ALU.mult, ALU.add)
            nc.vector.tensor_scalar(col[:, 12:14], col[:, 0:2], 1e-30, None, ALU.max).then_inc(S("lb"), 1)
            dve.wait_ge(S("lb"), 1)
            for d in range(2):
                for i in range(2):
                    t = tiles(pr, T_HF + 2 * d + i, 1)
                    ins = nc.vector.tensor_scalar(t, t, col[:, 2 + i:3 + i], None, ALU.mult)
            link(ins)
            dve.wait_ge(S("lT"), 1)
            nc.vector.tensor_copy(lT[:, 0:512], ps[2][:, :])
            nc.vector.tensor_copy(lT[:, 512:1024], ps[3][:, :]).then_inc(S("lT_out"), 1)
            dve.wait_ge(S("cum"), 1)
            for n, b in enumerate((6, 7, 0, 1)):
                ins = nc.vector.tensor_copy(cum[:, n * T:(n + 1) * T], ps[b][:, :])
            ins.then_inc(S("cum_out"), 1)
            dve.wait_ge(S("cum_out"), 1)
            for d in range(2):
                cv = tiles(cum, 2 * d, 2).rearrange("p (b t) -> p b t", t=P)
                ev = cv[:, :, end(d):end(d) + 1].to_broadcast([P, 2 * TILES, P])
                ins = nc.vector.tensor_tensor(tiles(kd, 2 * d, 2).rearrange("p (b t) -> p b t", t=P), ev, cv, ALU.subtract)
            ins.then_inc(S("rest"), 1)

            def exponents(n):
                d, l = steps[n]
                cv, dv = blocks(tiles(cum, 2 * d, 2), l), blocks(expo[d], l)
                ref = (1 << l) - 1 if d == 0 else 1 << l
                if n >= 2:
                    dve.wait_ge(S("kf"), n - 1)
                nc.vector.tensor_tensor(dv, cv, cv[:, :, :, ref:ref + 1].to_broadcast(list(cv.shape)),
                                        ALU.subtract).then_inc(S("dv"), 1)

            def factors(n):
                d, l = steps[n]
                dve.wait_ge(S("exps"), n + 1)
                if n >= 2:
                    dve.wait_ge(S("s_mm"), len(js) * (n - 1))
                for q in range(2):
                    half_, zeros = slice(q * HD, (q + 1) * HD), queries[d][:, q * 1024:(q + 1) * 1024]
                    nc.vector.tensor_tensor(later(zeros, d, l)[half_], later(expo[d], d, l)[half_], later(tiles(pr, T_HQ, 2), d, l)[half_], ALU.mult)
                nc.vector.tensor_tensor(sooner(keys[d], d, l), sooner(keys[d], d, l), sooner(tiles(pr, T_HF + 2 * d, 2), d, l),
                                        ALU.mult).then_inc(S("kf"), 1)

            def collect(n):
                d, l = steps[n]
                B = 2 << l
                for m, j in enumerate(js):
                    dve.wait_ge(S("s_mm"), len(js) * n + m + 1)
                    dst, src = at[:, d * 2048 + j * 512:d * 2048 + (j + 1) * 512], score_bank(n, j)[:, :]
                    if l == 0:
                        dst, src = (v.rearrange("p (b t) -> p b t", b=4) for v in (dst, src))
                        mask = c(C_BASE + d * P).bitcast(I32).rearrange("p (b t) -> p b t", b=1).to_broadcast([P, 4, P])
                    else:
                        dst, src = (halves(v, B, d == 0) for v in (dst, src))
                        mask = halves(c(C_LEVEL + (d * LEVELS + l) * P).bitcast(I32), B, d == 0).to_broadcast(list(dst.shape))
                    nc.vector.copy_predicated(dst, mask, src).then_inc(S("at"), 1)

            dve.wait_ge(S("kd_exp"), 1)
            nc.vector.tensor_tensor(kd, kd, tiles(pr, T_HF, 4), ALU.mult).then_inc(S("kd"), 1)
            for d in range(2):
                ins = nc.vector.tensor_tensor(tiles(qd, 2 * d, 2), tiles(qd, 2 * d, 2), tiles(pr, T_HQ, 2), ALU.mult)
            link(ins)
            dve.wait_ge(S("kT"), 1)
            nc.vector.tensor_copy(lT[:, 0:512], ps[2][:, :])
            nc.vector.tensor_copy(lT[:, 512:1024], ps[3][:, :]).then_inc(S("kT_out"), 1)
            dve.wait_ge(S("kv"), 1)
            for m in range(1, TILES):
                for d in range(2):
                    j0, j1 = ORDER[d][m - 1], ORDER[d][m]
                    for i in range(2):
                        new = st[:, d * 512 + (2 * j1 + i) * HD:d * 512 + (2 * j1 + i + 1) * HD]
                        old = st[:, d * 512 + (2 * j0 + i) * HD:d * 512 + (2 * j0 + i + 1) * HD]
                        kv = ps[6 + d][:, (2 * j0 + i) * HD:(2 * j0 + i + 1) * HD]
                        if m == 1:
                            ins = nc.vector.tensor_copy(new, kv)
                        else:
                            e_ = ecol[:, (2 * d + i) * TILES + j0:(2 * d + i) * TILES + j0 + 1]
                            ins = nc.vector.scalar_tensor_tensor(out=new, in0=old, scalar=e_, in1=kv, op0=ALU.mult, op1=ALU.add)
                link(ins)
            dve.wait_ge(S("at0"), 1)
            exponents(0)
            exponents(1)
            for n in range(len(steps)):
                factors(n)
                if n + 2 < len(steps):
                    exponents(n + 2)
                if n >= 1:
                    collect(n - 1)
            collect(len(steps) - 1)
            dve.wait_ge(S("y"), 1)
            for i in range(2):
                ins = nc.vector.tensor_copy(y[:, i * T + lo0:(i + 1) * T], ps[4 + i][:, lo0:])
            link(ins)
            nc.vector.tensor_tensor(two(sq, layer), two(y, layer), two(y, layer), ALU.mult).then_inc(S("sq"), 1)
            dve.wait_ge(S("rn"), 1)
            link(nc.vector.tensor_tensor(two(y, layer), two(y, layer), two(sq, layer), ALU.mult))
            for i in range(2):
                v = y[:, i * T + lo0:(i + 1) * T]
                nc.vector.scalar_tensor_tensor(out=v, in0=v, scalar=par[:, Q_HN:Q_HN + 1],
                                               in1=pr[:, (T_HG + i) * T + lo0:(T_HG + i + 1) * T], op0=ALU.mult, op1=ALU.mult)

        @block.scalar
        def _(act):
            if layer:
                act.wait_ge(S("lb_in"), 1)
                nc.scalar.activation(col[:, 6:10], col[:, 6:10], ACT.Exp).then_inc(S("lb_exp"), 1)
            act.wait_ge(S("vT"), 1)
            nc.scalar.copy(vT[:, 0:512], ps[0][:, :])
            nc.scalar.copy(vT[:, 512:1024], ps[1][:, :]).then_inc(S("vT_out"), 1)
            act.wait_ge(S("lb"), 1)
            for n in range(4):
                i = n % 2
                ins = nc.scalar.activation(tiles(cum, n, 1), tiles(cum, n, 1), ACT.Ln, bias=col[:, 12 + i:13 + i], scale=col[:, 2 + i:3 + i])
            ins.then_inc(S("logf"), 1)
            act.wait_ge(S("lT"), 1)
            nc.scalar.copy(lT[:, 1024:1536], ps[4][:, :])
            nc.scalar.copy(lT[:, 1536:2048], ps[5][:, :]).then_inc(S("lT_out"), 1)
            act.wait_ge(S("cum_out"), 1)
            nc.scalar.activation(qd, cum, ACT.Exp)
            for d in range(2):
                cv = tiles(cum, 2 * d, 2).rearrange("p (b t) -> p b t", t=P)
                nc.scalar.activation(ecol[:, 8 * d:8 * d + 8].rearrange("p (b t) -> p b t", t=1), cv[:, :, end(d):end(d) + 1], ACT.Exp)
            act.wait_ge(S("rest"), 1)
            nc.scalar.activation(kd, kd, ACT.Exp).then_inc(S("kd_exp"), 1)
            act.wait_ge(S("kT"), 1)
            nc.scalar.copy(lT[:, 1024:1536], ps[4][:, :])
            nc.scalar.copy(lT[:, 1536:2048], ps[5][:, :]).then_inc(S("kT_out"), 1)
            for n, (d, l) in enumerate(steps):
                act.wait_ge(S("dv"), n + 1)
                if n >= 2:
                    act.wait_ge(S("s_mm"), len(js) * (n - 1))
                nc.scalar.activation(sooner(keys[d], d, l), sooner(expo[d], d, l), ACT.Exp, scale=-1.0).then_inc(S("k_exp"), 1)
                if l == 0:
                    act.wait_ge(S("k_exp"), n + 1)
                nc.scalar.activation(later(expo[d], d, l), later(expo[d], d, l), ACT.Exp).then_inc(S("exps"), 1)
            inverse_rms(E, S, act, (6, 7), sq, layer, 1.0 / HD, Q_EPS)


def rwkv(E, layer):
    nc, c, par, pr, work, mix, ring, ps, ident = (E[k] for k in ("nc", "c", "par", "pr", "work", "mix", "ring", "ps", "ident"))
    js = active(layer)
    lo0, n0 = span(layer)
    KAPPA = float(np.exp(-0.5))
    MID = P // 2
    o = [0]

    def take(n):
        o[0] += n
        return work[:, o[0] - n:o[0]]

    sg, sa, cum, tm = take(2048), take(2048), take(2048), take(2048)
    vT, kk, kT, Q, ct = take(1024), take(1024), take(1024), take(1024), take(1024)
    al, rr, be, ks = (ring[:, n * 1024:(n + 1) * 1024] for n in range(4))
    alT, beT = tm[:, 0:1024], tm[:, 1024:2048]
    free = tiles(pr, 10, 24)
    NT, AkT, RbT, RkT = (free[:, n * 2048:(n + 1) * 2048] for n in range(4))
    X, XT = free[:, 8192:10240], free[:, 10240:12288]
    t1 = tiles(pr, T_WD, 2)
    PT, Qp = t1, ct
    U, st = NT[:, 0:1024], NT[:, 1024:1536]
    y = tiles(mix, 0, 2)
    sq = al
    units = [(l, j) for l in range(1, LEVELS) for j in range(TILES)]
    NU = len(units)

    def mat(m, j, hd):
        return m[:, (j * HEADS + hd) * P:(j * HEADS + hd + 1) * P]

    def four(m, j):
        return m[:, j * 512:(j + 1) * 512]

    with Stage(nc) as S, nc.Block() as block:
        for n in ("link", "tT", "raw", "raw_out", "ct", "t1", "t1_out", "x_up", "d_mm", "u_mm", "s_mm", "u", "s"):
            S(n)
        fcol = E["fcol"]

        def turns(src, dst_banks, n=2):
            for j in range(TILES):
                for i in range(n):
                    mm = nc.tensor.transpose(ps[dst_banks[j // 2]][:, (j % 2) * 256 + i * P:(j % 2) * 256 + (i + 1) * P],
                                             src[:, i * T + j * P:i * T + (j + 1) * P], ident)
            return mm

        @block.tensor
        def _(pe):
            for d in range(2):
                for i in range(2):
                    for n, t in ((0, T_WD), (1, T_AD)):
                        mm = nc.tensor.matmul(ps[4 * n + 2 * d + i][:, :], par[d * 64:(d + 1) * 64, Q_LORA + n * 256 + i * P:Q_LORA + n * 256 + (i + 1) * P],
                                              pr[d * 64:(d + 1) * 64, t * T:(t + 1) * T], start=True, stop=True)
            mm.then_inc(S("lora"), 1)
            pe.wait_ge(S("sig"), 1)
            turns(sg[:, 0:1024], (0, 1))
            turns(sg[:, 1024:2048], (2, 3))
            turns(tiles(pr, T_V, 2), (4, 5)).then_inc(S("sT"), 1)
            pe.wait_ge(S("kk"), 1)
            for i in range(2):
                mm = nc.tensor.matmul(ps[6 + i][:, :], c(C_HONES), al[:, i * T:(i + 1) * T], start=True, stop=True)
            mm.then_inc(S("kk_ss"), 1)
            pe.wait_ge(S("sT_out"), 1)
            for d in range(2):
                for i in range(2):
                    for j in range(TILES):
                        mm = nc.tensor.matmul(ps[2 * d + i][:, j * P:(j + 1) * P], tm[:, (d * TILES + j) * 256 + i * P:(d * TILES + j) * 256 + (i + 1) * P],
                                              c(C_TRI + d * P), start=True, stop=True)
            mm.then_inc(S("cum"), 1)
            for d in range(2):
                pe.wait_ge(S("scaled"), d + 1)
                turns(al, (0, 1))
                turns(be, (2, 3))
                turns(ks, (4, 5)).then_inc(S("tT"), 1)
                pe.wait_ge(S("tT_out"), 2 * (d + 1))
                for j in range(TILES):
                    b0 = 4 * (j % 2)
                    if j >= 2:
                        pe.wait_ge(S("raw_out"), 2 * (TILES * d + j - 1))
                    for n, rh in enumerate((al, rr)):
                        for q in range(2):
                            for i in range(2):
                                for m, lh in enumerate((be, ks)):
                                    mm = nc.tensor.matmul(ps[b0 + 2 * n + q][:, (2 * m + i) * P:(2 * m + i + 1) * P],
                                                          lh[q * HD:(q + 1) * HD, i * T + j * P:i * T + (j + 1) * P],
                                                          rh[q * HD:(q + 1) * HD, i * T + j * P:i * T + (j + 1) * P], start=True, stop=True)
                        mm.then_inc(S("raw"), 1)
                pe.wait_ge(S("raw_out"), 2 * TILES * (d + 1))
                for j in range(TILES):
                    pe.wait_ge(S("x0T"), TILES * d + j + 1)
                    for hd in range(HEADS):
                        mm = nc.tensor.transpose(ps[j][:, hd * P:(hd + 1) * P], mat(X, j, hd), ident)
                    mm.then_inc(S("x0"), 1)

                def first(u):
                    l, j = units[u]
                    pe.wait_ge(S("ct"), NU * d + u + 1)
                    pe.wait_ge(S("x_up"), (NU + TILES) * d + u + 1)
                    if u >= 2:
                        pe.wait_ge(S("t1_out"), NU * d + u - 1)
                    else:
                        pe.wait_ge(S("x_up"), (NU + TILES) * d + TILES)
                    for hd in range(HEADS):
                        mm = nc.tensor.matmul(ps[u % 2][:, hd * P:(hd + 1) * P], ct[:, (u % 2) * 512 + hd * P:(u % 2) * 512 + (hd + 1) * P],
                                              mat(X, j, hd), start=True, stop=True)
                    mm.then_inc(S("t1"), 1)

                def second(u):
                    l, j = units[u]
                    pe.wait_ge(S("t1_out"), NU * d + u + 1)
                    if u >= 2:
                        pe.wait_ge(S("x_up"), (NU + TILES) * d + TILES + u - 1)
                    for hd in range(HEADS):
                        t = t1[:, (u % 2) * 512 + hd * P:(u % 2) * 512 + (hd + 1) * P]
                        nc.tensor.matmul(ps[4 + u % 2][:, hd * P:(hd + 1) * P], t, mat(XT, j, hd), start=True, stop=True)
                    for hd in range(HEADS):
                        t = t1[:, (u % 2) * 512 + hd * P:(u % 2) * 512 + (hd + 1) * P]
                        mm = nc.tensor.matmul(ps[2 + u % 2][:, hd * P:(hd + 1) * P], mat(XT, j, hd), t, start=True, stop=True)
                    mm.then_inc(S("d_mm"), 1)

                for u in range(NU + 1):
                    if u < NU:
                        first(u)
                    if u >= 1:
                        second(u - 1)
                pe.wait_ge(S("x_up"), (NU + TILES) * (d + 1))
                for i in range(2):
                    for j in range(TILES):
                        for q in range(2):
                            hd = 2 * i + q
                            nc.tensor.matmul(ps[6 + i][q * HD:(q + 1) * HD, j * P:(j + 1) * P],
                                             alT[:, j * 256 + hd * HD:j * 256 + (hd + 1) * HD], mat(XT, j, hd), start=True, stop=True)
                for j in range(TILES):
                    for hd in range(HEADS):
                        mm = nc.tensor.matmul(ps[j // 2][:, (j % 2) * 256 + hd * HD:(j % 2) * 256 + (hd + 1) * HD], mat(AkT, j, hd),
                                              vT[:, j * 256 + hd * HD:j * 256 + (hd + 1) * HD], start=True, stop=True)
                mm.then_inc(S("pq"), 1)
                pe.wait_ge(S("qp_out"), d + 1)
                for j in range(TILES):
                    for hd in range(HEADS):
                        mm = nc.tensor.matmul(ps[2 + j // 2][:, (j % 2) * 256 + hd * HD:(j % 2) * 256 + (hd + 1) * HD], mat(XT, j, hd),
                                              Qp[:, j * 256 + hd * HD:j * 256 + (hd + 1) * HD], start=True, stop=True)
                mm.then_inc(S("q"), 1)
                pe.wait_ge(S("q_out"), d + 1)
                for m, j in enumerate(ORDER[d]):
                    if m:
                        pe.wait_ge(S("s"), (TILES - 1) * d + m)
                        for q in range(2):
                            for i in range(2):
                                mm = nc.tensor.matmul(ps[q][:, i * HD:(i + 1) * HD], PT[q * HD:(q + 1) * HD, i * T + j * P:i * T + (j + 1) * P],
                                                      st[q * HD:(q + 1) * HD, (2 * j + i) * HD:(2 * j + i + 1) * HD], start=True, stop=True)
                        mm.then_inc(S("u_mm"), 1)
                        pe.wait_ge(S("u"), (TILES - 1) * d + m)
                    if m < TILES - 1:
                        for hd in range(HEADS):
                            q, i = hd % 2, hd // 2
                            out = ps[2][q * HD:(q + 1) * HD, i * HD:(i + 1) * HD]
                            a = j * 256 + hd * HD
                            nc.tensor.matmul(out, beT[:, a:a + HD], (U if m else Q)[:, a:a + HD], start=True, stop=False)
                            mm = nc.tensor.matmul(out, kT[:, a:a + HD], vT[:, a:a + HD], start=False, stop=True)
                        mm.then_inc(S("s_mm"), 1)
                for hd in range(HEADS):
                    q, i = hd % 2, hd // 2
                    for j in js:
                        out = ps[4 + i][q * HD:(q + 1) * HD, j * P:(j + 1) * P]
                        a = j * 256 + hd * HD
                        first_ = ORDER[d][0] == j
                        nc.tensor.matmul(out, (Q if first_ else U)[:, a:a + HD], mat(RbT, j, hd), start=True, stop=False)
                        mm = nc.tensor.matmul(out, vT[:, a:a + HD], mat(RkT, j, hd), start=False, stop=first_)
                        if not first_:
                            mm = nc.tensor.matmul(out, st[q * HD:(q + 1) * HD, (2 * j + i) * HD:(2 * j + i + 1) * HD],
                                                  rr[q * HD:(q + 1) * HD, i * T + j * P:i * T + (j + 1) * P], start=False, stop=True)
                mm.then_inc(S("y"), 1)
            for i in range(2):
                nc.tensor.matmul(ps[i][:, lo0:], par[:, Q_LORA + 512 + i * P:Q_LORA + 512 + (i + 1) * P], pr[:, T_GD * T + lo0:(T_GD + 1) * T],
                                 start=True, stop=False)
                nc.tensor.matmul(ps[i][:, lo0:], par[0:32, Q_LORA + 768 + i * P:Q_LORA + 768 + (i + 1) * P],
                                 pr[0:32, T_GD2 * T + lo0:(T_GD2 + 1) * T], start=False, stop=True)
            pe.wait_ge(S("bonus"), 1)
            head_sums(E, pe, rr, (2, 3), layer)
            head_sums(E, pe, y, (6, 7), layer).then_inc(S("mean"), 1)
            pe.wait_ge(S("sq"), 1)
            head_sums(E, pe, sq, (4, 5), layer).then_inc(S("ss"), 1)

        @block.gpsimd
        def _(pool):
            for d in range(2):
                for u, (l, j) in enumerate(units):
                    if u == 0:
                        pool.wait_ge(S("raw_out"), 2 * TILES * (d + 1))
                        if d:
                            pool.wait_ge(S("x0T"), TILES * d + 1)
                    if u >= 2:
                        pool.wait_ge(S("t1"), NU * d + u - 1)
                    mask = c(C_LEVEL + (d * LEVELS + l) * P).rearrange("p (b t) -> p b t", b=1).to_broadcast([P, HEADS, P])
                    nc.gpsimd.tensor_tensor(ct[:, (u % 2) * 512:(u % 2 + 1) * 512].rearrange("p (b t) -> p b t", b=HEADS),
                                            four(NT, j).rearrange("p (b t) -> p b t", b=HEADS), mask, ALU.mult).then_inc(S("ct"), 1)

        def tile_view(t):
            return t.rearrange("p (b t) -> p b t", t=P)

        @block.vector
        def _(dve):
            link = linker(dve, S("link"))
            for i in range(2):
                ins = nc.vector.tensor_scalar(tiles(kk, i, 1), tiles(pr, T_K + i, 1), par[:, Q_KK + i:Q_KK + i + 1], None, ALU.mult)
            link(ins)
            nc.vector.tensor_tensor(al, kk, kk, ALU.mult).then_inc(S("kk"), 1)
            dve.wait_ge(S("sT"), 1)
            nc.vector.tensor_copy(vT[:, 0:512], ps[4][:, :])
            nc.vector.tensor_copy(vT[:, 512:1024], ps[5][:, :])
            dve.wait_ge(S("kk_ss"), 1)
            for i in range(2):
                ins = nc.vector.tensor_scalar(tiles(al, i, 1), ps[6 + i][:, :], 1e-24, None, ALU.max)
            ins.then_inc(S("kk_max"), 1)
            dve.wait_ge(S("cum"), 1)
            for n in range(4):
                ins = nc.vector.tensor_copy(tiles(cum, n, 1), ps[n][:, :])
            link(ins)
            dve.wait_ge(S("kk_norm"), 1)
            link(nc.vector.reciprocal(al, al))
            link(nc.vector.tensor_tensor(kk, kk, al, ALU.mult))
            for d in range(2):
                end = P - 1 if d == 0 else 0
                if d:
                    dve.wait_ge(S("y"), d)
                    for i in range(2):
                        ins = nc.vector.tensor_copy(y[:, i * T + lo0:(i + 1) * T], ps[4 + i][:, lo0:])
                    link(ins)
                cv = tile_view(tiles(cum, 2 * d, 2))
                mid = cv[:, :, MID:MID + 1]
                link(nc.vector.tensor_tensor(tile_view(rr), cv, mid.to_broadcast([P, 2 * TILES, P]), ALU.subtract))
                nc.vector.tensor_tensor(al, rr, tiles(sg, 2 * d, 2), ALU.subtract)
                fc = fcol[:, 0:8].rearrange("p (i j) -> p i j", i=2)
                c4 = tiles(cum, 2 * d, 2).rearrange("p (i j t) -> p i j t", i=2, t=P)
                for m in range(TILES - 1):
                    j0, j1 = ORDER[d][m], ORDER[d][m + 1]
                    ins = nc.vector.tensor_tensor(fc[:, :, j0:j0 + 1], c4[:, :, j0, end:end + 1], c4[:, :, j0, MID:MID + 1], ALU.subtract)
                link(ins)
                for m in range(TILES - 1):
                    j0, j1 = ORDER[d][m], ORDER[d][m + 1]
                    ins = nc.vector.tensor_tensor(fc[:, :, j0:j0 + 1], fc[:, :, j0:j0 + 1], c4[:, :, j1, MID:MID + 1], ALU.add)
                ins.then_inc(S("dv"), 1)
                for i in range(2):
                    ins = nc.vector.tensor_scalar(tiles(ct, i, 1), tiles(sa, 2 * d + i, 1), -1.0, par[:, Q_KA + i:Q_KA + i + 1], ALU.add, ALU.mult)
                link(ins)
                link(nc.vector.scalar_tensor_tensor(out=ct, in0=ct, scalar=1.0, in1=tiles(pr, T_K, 2), op0=ALU.add, op1=ALU.mult))
                dve.wait_ge(S("exp"), d + 1)
                link(nc.vector.tensor_tensor(ks, ct, be, ALU.mult))
                link(nc.vector.tensor_tensor(ct, kk, tiles(sa, 2 * d, 2), ALU.mult))
                nc.vector.scalar_tensor_tensor(out=be, in0=be, scalar=-1.0, in1=ct, op0=ALU.mult, op1=ALU.mult)
                nc.vector.tensor_tensor(al, al, kk, ALU.mult)
                nc.vector.tensor_tensor(rr, rr, tiles(pr, T_R, 2), ALU.mult).then_inc(S("scaled"), 1)
                dve.wait_ge(S("scaled"), d + 1)
                dve.wait_ge(S("tT"), d + 1)
                for n, (dst, b) in enumerate(((alT, 0), (alT, 1), (beT, 2))):
                    ins = nc.vector.tensor_copy(dst[:, (b % 2) * 512:(b % 2 + 1) * 512], ps[b][:, :])
                ins.then_inc(S("tT_out"), 1)
                for j in range(TILES):
                    for n, (m0, msk) in enumerate(((0, C_STRICT), (4096, C_TRI))):
                        dve.wait_ge(S("raw"), 2 * (TILES * d + j) + n + 1)
                        mask = c(msk + d * P).rearrange("p (a b t) -> p a b t", a=1, b=1).to_broadcast([P, 2, 2, P])
                        for q in range(2):
                            dst = free[:, m0:m0 + 4096].rearrange("p (k j i q t) -> p k j i q t", k=2, j=TILES, i=2, q=2)[:, :, j, :, q, :]
                            src = ps[4 * (j % 2) + 2 * n + q][:, :].rearrange("p (k i t) -> p k i t", k=2, i=2)
                            ins = nc.vector.tensor_tensor(dst, src, mask, ALU.mult)
                        ins.then_inc(S("raw_out"), 1)
                dve.wait_ge(S("raw_out"), 2 * TILES * (d + 1))
                idb = ident.rearrange("p (b t) -> p b t", b=1).to_broadcast([P, HEADS, P])
                mask = c(C_LEVEL + d * LEVELS * P).rearrange("p (b t) -> p b t", b=1).to_broadcast([P, HEADS, P])
                for j in range(TILES):
                    nc.vector.tensor_tensor(four(X, j).rearrange("p (b t) -> p b t", b=HEADS), four(NT, j).rearrange("p (b t) -> p b t", b=HEADS),
                                            mask, ALU.mult).then_inc(S("x0T"), 1)
                dve.wait_ge(S("x0T"), TILES * (d + 1))
                for j in range(TILES):
                    ins = nc.vector.tensor_tensor(four(XT, j).rearrange("p (b t) -> p b t", b=HEADS),
                                                  four(X, j).rearrange("p (b t) -> p b t", b=HEADS), idb, ALU.add)
                link(ins)
                for j in range(TILES):
                    dve.wait_ge(S("x0"), TILES * d + j + 1)
                    nc.vector.tensor_tensor(four(X, j).rearrange("p (b t) -> p b t", b=HEADS), ps[j][:, :].rearrange("p (b t) -> p b t", b=HEADS),
                                            idb, ALU.add).then_inc(S("x_up"), 1)
                for u, (l, j) in enumerate(units):
                    dve.wait_ge(S("d_mm"), NU * d + u + 1)
                    dve.wait_ge(S("x_up"), (NU + TILES) * d + u + 1)
                    nc.vector.tensor_tensor(four(XT, j), four(XT, j), ps[4 + u % 2][:, :], ALU.add)
                    nc.vector.tensor_tensor(four(X, j), four(X, j), ps[2 + u % 2][:, :], ALU.add).then_inc(S("x_up"), 1)
                dve.wait_ge(S("x_up"), (NU + TILES) * (d + 1))
                dve.wait_ge(S("pq"), d + 1)
                nc.vector.tensor_copy(Qp[:, 0:512], ps[0][:, :])
                nc.vector.tensor_copy(Qp[:, 512:1024], ps[1][:, :]).then_inc(S("qp_out"), 1)
                dve.wait_ge(S("q"), d + 1)
                dve.wait_ge(S("pt_out"), d + 1)
                nc.vector.tensor_copy(Q[:, 0:512], ps[2][:, :])
                nc.vector.tensor_copy(Q[:, 512:1024], ps[3][:, :]).then_inc(S("q_out"), 1)
                dve.wait_ge(S("q_out"), d + 1)
                for m, j in enumerate(ORDER[d]):
                    if m:
                        dve.wait_ge(S("u_mm"), (TILES - 1) * d + m)
                        for q in range(2):
                            uv, qv = (t[:, j * 256:(j + 1) * 256].rearrange("p (i q v) -> p i q v", i=2, q=2)[:, :, q, :] for t in (U, Q))
                            ins = nc.vector.tensor_tensor(uv, qv, ps[q][:, 0:P].rearrange("p (i v) -> p i v", i=2), ALU.add)
                        ins.then_inc(S("u"), 1)
                    if m < TILES - 1:
                        dve.wait_ge(S("s_mm"), (TILES - 1) * d + m + 1)
                        j1 = ORDER[d][m + 1]
                        new, old = st[:, j1 * P:(j1 + 1) * P], st[:, j * P:(j + 1) * P]
                        if m:
                            link(nc.vector.tensor_tensor(new, old, ps[2][:, 0:P], ALU.add))
                        for i in range(2):
                            ins = nc.vector.tensor_scalar(new[:, i * HD:(i + 1) * HD], (new if m else ps[2][:, 0:P])[:, i * HD:(i + 1) * HD],
                                                          fcol[:, 8 + i * TILES + j:9 + i * TILES + j], None, ALU.mult)
                        ins.then_inc(S("s"), 1)
                        dve.wait_ge(S("s"), (TILES - 1) * d + m + 1)
            dve.wait_ge(S("y"), 2)
            for i in range(2):
                v = y[:, i * T + lo0:(i + 1) * T]
                ins = nc.vector.tensor_tensor(v, v, ps[4 + i][:, lo0:], ALU.add)
            link(nc.vector.tensor_tensor(ks, tiles(sa, 0, 2), tiles(sa, 2, 2), ALU.add))
            for i in range(2):
                ins = nc.vector.tensor_scalar(tiles(ks, i, 1), tiles(ks, i, 1), -2.0, par[:, Q_KA + i:Q_KA + i + 1], ALU.add, ALU.mult)
            link(ins)
            link(nc.vector.scalar_tensor_tensor(out=ks, in0=ks, scalar=2.0, in1=tiles(pr, T_K, 2), op0=ALU.add, op1=ALU.mult))
            for i in range(2):
                ins = nc.vector.scalar_tensor_tensor(out=tiles(rr, i, 1), in0=tiles(pr, T_R + i, 1), scalar=par[:, Q_RK + i:Q_RK + i + 1],
                                                     in1=tiles(ks, i, 1), op0=ALU.mult, op1=ALU.mult)
            ins.then_inc(S("bonus"), 1)
            dve.wait_ge(S("mean"), 1)
            for i in range(2):
                v = y[:, i * T + lo0:(i + 1) * T]
                ins = nc.vector.scalar_tensor_tensor(out=v, in0=ps[6 + i][:, lo0:], scalar=-1.0 / HD, in1=v, op0=ALU.mult, op1=ALU.add)
            link(ins)
            nc.vector.tensor_tensor(two(sq, layer), two(y, layer), two(y, layer), ALU.mult).then_inc(S("sq"), 1)
            for i in range(2):
                ins = nc.vector.tensor_tensor(be[:, i * T + lo0:(i + 1) * T], pr[:, (T_V + i) * T + lo0:(T_V + i + 1) * T], ps[2 + i][:, lo0:], ALU.mult)
            dve.wait_ge(S("rn"), 1)
            link(nc.vector.tensor_tensor(two(y, layer), two(y, layer), two(sq, layer), ALU.mult))
            for i in range(2):
                v = y[:, i * T + lo0:(i + 1) * T]
                ins = nc.vector.tensor_scalar(v, v, par[:, Q_XG + i:Q_XG + i + 1], par[:, Q_XB + i:Q_XB + i + 1], ALU.mult, ALU.add)
            link(ins)
            link(nc.vector.tensor_tensor(two(y, layer), two(y, layer), two(be, layer), ALU.add))
            for i in range(2):
                v = y[:, i * T + lo0:(i + 1) * T]
                nc.vector.tensor_tensor(v, v, ps[i][:, lo0:], ALU.mult)

        @block.scalar
        def _(act):
            act.wait_ge(S("lora"), 1)
            for d in range(2):
                for i in range(2):
                    n = 2 * d + i
                    nc.scalar.activation(tiles(sg, n, 1), ps[n][:, :], ACT.Sigmoid, bias=par[:, Q_W0 + n:Q_W0 + n + 1])
                    ins = nc.scalar.activation(tiles(sa, n, 1), ps[4 + n][:, :], ACT.Sigmoid, bias=par[:, Q_A0 + n:Q_A0 + n + 1])
            ins.then_inc(S("sig"), 1)
            act.wait_ge(S("sT"), 1)
            for n in range(4):
                ins = nc.scalar.copy(tm[:, n * 512:(n + 1) * 512], ps[n][:, :])
            ins.then_inc(S("sT_out"), 1)
            act.wait_ge(S("kk_max"), 1)
            nc.scalar.activation(al, al, ACT.Sqrt).then_inc(S("kk_norm"), 1)
            for d in range(2):
                act.wait_ge(S("dv"), d + 1)
                nc.scalar.activation(be, rr, ACT.Exp, scale=KAPPA).then_inc(S("be_exp"), 1)
                act.wait_ge(S("be_exp"), d + 1)
                nc.scalar.activation(rr, rr, ACT.Exp, scale=-KAPPA)
                nc.scalar.activation(al, al, ACT.Exp, scale=-KAPPA)
                fc = fcol[:, 0:8].rearrange("p (i j) -> p i j", i=2)
                fo = fcol[:, 8:16].rearrange("p (i j) -> p i j", i=2)
                last = ORDER[d][-1]
                a, b = (0, 3) if d == 0 else (0, 4)
                if d == 0:
                    nc.scalar.activation(fo[:, :, 0:3], fc[:, :, 0:3], ACT.Exp, scale=-KAPPA).then_inc(S("exp"), 1)
                else:
                    nc.scalar.activation(fo[:, :, 0:2], fc[:, :, 0:2], ACT.Exp, scale=-KAPPA)
                    nc.scalar.activation(fo[:, :, 3:4], fc[:, :, 3:4], ACT.Exp, scale=-KAPPA).then_inc(S("exp"), 1)
                act.wait_ge(S("tT"), d + 1)
                nc.scalar.copy(beT[:, 512:1024], ps[3][:, :])
                nc.scalar.copy(kT[:, 0:512], ps[4][:, :])
                nc.scalar.copy(kT[:, 512:1024], ps[5][:, :]).then_inc(S("tT_out"), 1)
                for u in range(NU):
                    act.wait_ge(S("t1"), NU * d + u + 1)
                    if u >= 2:
                        act.wait_ge(S("d_mm"), NU * d + u - 1)
                    nc.scalar.copy(t1[:, (u % 2) * 512:(u % 2 + 1) * 512], ps[u % 2][:, :]).then_inc(S("t1_out"), 1)
                act.wait_ge(S("pq"), d + 1)
                nc.scalar.copy(PT[:, 0:512], ps[6][:, :])
                nc.scalar.copy(PT[:, 512:1024], ps[7][:, :]).then_inc(S("pt_out"), 1)
            inverse_rms(E, S, act, (4, 5), sq, layer, 1.0 / HD, Q_EPS + 1)


def residual_norm(E, S, dve, act, layer, which, lnp):
    nc, h, gate, ps, par = (E[k] for k in ("nc", "h", "gate", "ps", "par"))
    js = active(layer)
    g0 = 2 * which
    tmp, stats = E["pr"][:, 30 * T:32 * T], E["pr"][:, 29 * T:29 * T + 128]
    if dve:
        link = linker(dve, S("link"))

        def residual(m, j):
            dve.wait_ge(S("y"), m + 1)
            side = j // 2
            hj = h[:, j * D:(j + 1) * D]
            for b in range(2):
                ins = nc.vector.tensor_tensor(tmp[:, b * 512:(b + 1) * 512], ps[2 * j + b][:, :],
                                              gate[:, (g0 + side) * D + b * 512:(g0 + side) * D + (b + 1) * 512], ALU.mult)
            link(ins)
            link(nc.vector.scalar_tensor_tensor(out=hj, in0=hj, scalar=ALPHA, in1=tmp, op0=ALU.mult, op1=ALU.add))
            s = stats[:, 32 * m:32 * m + 32]
            for b in range(2):
                ins = nc.vector.bn_stats(s[:, 6 * b:6 * b + 6], hj[:, b * 512:(b + 1) * 512])
            link(ins)
            nc.vector.bn_aggr(s[:, 12:14], s[:, 0:12]).then_inc(S("var"), 1)

        def normed(m, j):
            hj, s = h[:, j * D:(j + 1) * D], stats[:, 32 * m:32 * m + 32]
            if m == 0:
                dve.wait_ge(S("ln_par"), 16)
            dve.wait_ge(S("var"), m + 1)
            link(nc.vector.scalar_tensor_tensor(out=hj, in0=hj, scalar=s[:, 12:13], in1=lnp[:, 0:D], op0=ALU.subtract, op1=ALU.mult))
            dve.wait_ge(S("rstd"), m + 1)
            nc.vector.scalar_tensor_tensor(out=hj, in0=hj, scalar=s[:, 15:16], in1=lnp[:, D:2 * D], op0=ALU.mult, op1=ALU.add)

        for m in range(len(js) + 1):
            if m < len(js):
                residual(m, js[m])
            if m >= 1:
                normed(m - 1, js[m - 1])
    if act:
        for m, j in enumerate(js):
            s = stats[:, 32 * m:32 * m + 32]
            act.wait_ge(S("var"), m + 1)
            nc.scalar.activation(s[:, 14:15], s[:, 13:14], ACT.Ln, bias=par[:, Q_EPS:Q_EPS + 1]).then_inc(S("lnv"), 1)
            act.wait_ge(S("lnv"), m + 1)
            nc.scalar.activation(s[:, 15:16], s[:, 14:15], ACT.Exp, scale=-0.5).then_inc(S("rstd"), 1)


def output_projection(E, layer):
    nc, A, mix, pr, ps = (E[k] for k in ("nc", "A", "mix", "pr", "ps"))
    js = active(layer)
    lo, n = span(layer)
    lnp = pr[:, 24 * T:28 * T]
    RAW = 8
    with Stage(nc) as S, nc.Block() as block:
        wr = S.sb("wr", KD * 2 * D // 2, F32R)
        xr = S.sb("xr", 4 * 2 * T, F32R)

        def raw(k):
            return pr[:, (k % RAW) * D:(k % RAW + 1) * D]

        def part(k, p):
            return wr[:, (2 * (k % 4) + p) * D:(2 * (k % 4) + p + 1) * D]

        def xpart(k, p, a=0, b=T):
            return xr[:, (2 * (k % 4) + p) * T + a:(2 * (k % 4) + p) * T + b]

        @block.sync
        def _(sp):
            for k in range(KD):
                sp.dma_start(raw(k), A["w_out"][layer, k]).then_inc(S(f"w{k}"), 16)
            sp.dma_start(lnp, A["ln"][layer, 0]).then_inc(S("ln_par"), 16)

        @block.tensor
        def _(pe):
            def slice_of(k, j):
                for b in range(2):
                    mm = product(nc, ps[2 * j + b][:, :], [xpart(k, p, j * P, (j + 1) * P) for p in (0, 1)],
                                 [part(k, p)[:, b * 512:(b + 1) * 512] for p in (0, 1)], k == 0, k == KD - 1)
                return mm

            for k in range(KD - 4):
                pe.wait_ge(S("low"), k + 1)
                for j in js:
                    mm = slice_of(k, j)
                mm.then_inc(S("mm"), 1)
            for j in js:
                for k in range(KD - 4, KD):
                    pe.wait_ge(S("low"), k + 1)
                    mm = slice_of(k, j)
                mm.then_inc(S("y"), 1)

        @block.vector
        def _(dve):
            for k in range(KD):
                dve.wait_ge(S("high"), k + 1)
                if k >= 4:
                    dve.wait_ge(S("mm"), k - 3)
                split_low(nc, dve, mix[:, k * T + lo:(k + 1) * T], xpart(k, 0, lo), xpart(k, 1, lo))
                split_low(nc, dve, raw(k), part(k, 0), part(k, 1)).then_inc(S("low"), 1)
            residual_norm(E, S, dve, None, layer, 0, lnp)

        @block.scalar
        def _(act):
            for k in range(KD):
                act.wait_ge(S(f"w{k}"), 16)
                if k >= 4:
                    act.wait_ge(S("mm"), k - 3)
                split_high(nc, act, mix[:, k * T + lo:(k + 1) * T], xpart(k, 0, lo))
                split_high(nc, act, raw(k), part(k, 0)).then_inc(S("high"), 1)
            residual_norm(E, S, None, act, layer, 0, lnp)


def ffn(E, layer):
    nc, A, par, pr, mix, ps = (E[k] for k in ("nc", "A", "par", "pr", "mix", "ps"))
    js = active(layer)
    lo0, n0 = span(layer)
    ns = n0 // SIDE
    lnp = pr[:, 24 * T:28 * T]
    W = 2 * D
    raws = (pr[:, 22 * T:26 * T], pr[:, 26 * T:30 * T], pr[:, 30 * T:34 * T], mix[:, 0:W], mix[:, W:2 * W])
    RAW = len(raws)
    LOADS = KF + KF // 2
    with Stage(nc) as S, nc.Block() as block:
        hr = [S.sb(f"hr{p}", KD * T, F32R) for p in range(2)]
        wr = S.sb("wr", 2 * 2 * W, F32R)
        tb = S.sb("tmp", 2 * T)

        def part(n, p):
            return wr[:, (2 * (n % 2) + p) * W:(2 * (n % 2) + p + 1) * W]

        def xpart(k, p, a=0, b=T):
            return hr[p][:, (k % 4) * T + a:(k % 4) * T + b]

        @block.sync
        def _(sp):
            for n in range(LOADS):
                if n >= RAW:
                    sp.wait_ge(S("low"), n - RAW + 1)
                if n < KF:
                    sp.dma_start(raws[n % RAW], A["w_up"][layer, n]).then_inc(S(f"w{n % RAW}"), 16)
                else:
                    k = 2 * (n - KF)
                    sp.dma_start(raws[n % RAW].rearrange("p (a n) -> p a n", a=2), A["w_down"][layer, k:k + 2].rearrange("a p n -> p a n"))\
                        .then_inc(S(f"w{n % RAW}"), 16)
            sp.wait_ge(S("low"), LOADS)
            sp.dma_start(lnp, A["ln"][layer, 1]).then_inc(S("ln_par"), 16)

        @block.tensor
        def _(pe):
            transpose_modulate(E, S, hr, js, tb, pe=pe)
            for f in range(KF):
                pe.wait_ge(S("low"), f + 1)
                if f >= 4:
                    pe.wait_ge(S("acts"), f - 3)
                for v in range(2):
                    for k in range(KD):
                        if f == 0 and v == 0:
                            pe.wait_ge(S("hT"), k + 1)
                        mm = product(nc, ps[2 * (f % 4) + v][:, lo0:], [part(f, p)[:, v * D + k * P:v * D + (k + 1) * P] for p in (0, 1)],
                                     [x[:, k * T + lo0:(k + 1) * T] for x in hr], k == 0, k == KD - 1)
                mm.then_inc(S("mm"), 1)

            def slice_of(k, j):
                n = KF + k // 2
                for b in range(2):
                    mm = product(nc, ps[2 * j + b][:, :], [xpart(k, p, j * P, (j + 1) * P) for p in (0, 1)],
                                 [part(n, p)[:, (k % 2) * D + b * 512:(k % 2) * D + (b + 1) * 512] for p in (0, 1)],
                                 k == 0, k == KF - 1)
                return mm

            for k in range(KF - 4):
                pe.wait_ge(S("low"), KF + k // 2 + 1)
                pe.wait_ge(S("x_low"), k + 1)
                for j in js:
                    if k == 0:
                        pe.wait_ge(S("acts"), KF - (KF - 1 - j) % 4)
                    mm = slice_of(k, j)
                mm.then_inc(S("down"), 1)
                if k % 2:
                    pe.wait_ge(S("down"), k + 1)
                    pe.sem_inc(S("mm"), 1)
            for j in js:
                for k in range(KF - 4, KF):
                    pe.wait_ge(S("low"), KF + k // 2 + 1)
                    pe.wait_ge(S("x_low"), k + 1)
                    mm = slice_of(k, j)
                mm.then_inc(S("y"), 1)

        @block.vector
        def _(dve):
            link = linker(dve, S("dd"))

            def low(n):
                dve.wait_ge(S("high"), n + 1)
                if n >= 2:
                    dve.wait_ge(S("mm"), n - 1)
                split_low(nc, dve, raws[n % RAW], part(n, 0), part(n, 1)).then_inc(S("low"), 1)

            def x_low(k):
                dve.wait_ge(S("x_high"), k + 1)
                if k >= 4:
                    dve.wait_ge(S("down"), k - 3)
                split_low(nc, dve, pr[:, k * T + lo0:(k + 1) * T], xpart(k, 0, lo0), xpart(k, 1, lo0)).then_inc(S("x_low"), 1)

            low(0)
            transpose_modulate(E, S, hr, js, tb, dve=dve)
            for f in range(KF + 1):
                if f < KF:
                    low(f + 1)
                    dve.wait_ge(S("mm"), f + 1)
                    if f >= 2:
                        dve.wait_ge(S("gelu"), f - 1)
                    z = ps[2 * (f % 4)][:, lo0:]
                    t = tb[:, (f % 2) * T + lo0:(f % 2 + 1) * T]
                    z3, t3 = (v.rearrange("p (s t) -> p s t", s=ns) for v in (z, t))
                    a = Q_FCW + 3 * f
                    link(nc.vector.tensor_scalar(t, z, par[:, a + 1:a + 2], par[:, Q_FCB + f:Q_FCB + f + 1], ALU.mult, ALU.add))
                    link(nc.vector.scalar_tensor_tensor(out=t3[:, :, 1:], in0=z3[:, :, :-1], scalar=par[:, a:a + 1], in1=t3[:, :, 1:],
                                                        op0=ALU.mult, op1=ALU.add))
                    nc.vector.scalar_tensor_tensor(out=t3[:, :, :-1], in0=z3[:, :, 1:], scalar=par[:, a + 2:a + 3], in1=t3[:, :, :-1],
                                                   op0=ALU.mult, op1=ALU.add).then_inc(S("conv"), 1)
                if f >= 1:
                    g = f - 1
                    dve.wait_ge(S("gelu"), g + 1)
                    o = pr[:, g * T + lo0:(g + 1) * T]
                    nc.vector.tensor_tensor(o, o, ps[2 * (g % 4) + 1][:, lo0:], ALU.mult).then_inc(S("acts"), 1)
            for k in range(KF):
                if k % 2 == 0 and k:
                    low(KF + k // 2)
                x_low(k)
            residual_norm(E, S, dve, None, layer, 1, lnp)

        @block.scalar
        def _(act):
            def high(n):
                act.wait_ge(S(f"w{n % RAW}"), 16 * (n // RAW + 1))
                if n >= 2:
                    act.wait_ge(S("mm"), n - 1)
                split_high(nc, act, raws[n % RAW], part(n, 0)).then_inc(S("high"), 1)

            high(0)
            transpose_modulate(E, S, hr, js, tb, act=act, shift=3, scale=4)
            for f in range(KF):
                high(f + 1)
                act.wait_ge(S("conv"), f + 1)
                nc.scalar.activation(pr[:, f * T + lo0:(f + 1) * T], tb[:, (f % 2) * T + lo0:(f % 2 + 1) * T],
                                     ACT.Gelu_apprx_tanh).then_inc(S("gelu"), 1)
            act.wait_ge(S("mm"), KF)
            for k in range(KF):
                if k % 2 == 0 and k:
                    high(KF + k // 2)
                act.wait_ge(S("acts"), k + 1)
                if k >= 4:
                    act.wait_ge(S("down"), k - 3)
                split_high(nc, act, pr[:, k * T + lo0:(k + 1) * T], xpart(k, 0, lo0)).then_inc(S("x_high"), 1)
            residual_norm(E, S, None, act, layer, 1, lnp)


def store_output(E):
    nc, h, out = (E[k] for k in ("nc", "h", "out"))
    with Stage(nc) as S, nc.Block() as block:
        @block.sync
        def _(sp):
            sp.dma_start(out.rearrange("(j p) d -> p j d", p=P), h[:, :].rearrange("p (j d) -> p j d", j=TILES)[:, 2:4, :])\
                .then_inc(E["stored"], 16)
            sp.wait_ge(E["stored"], 16)


def constants():
    t = np.zeros((P, N_CONST), np.float32)
    s, q = np.arange(P)[:, None], np.arange(P)[None, :]
    t[:, C_ID:C_ID + P] = s == q
    for d in range(2):
        before = (s <= q) if d == 0 else (s >= q)
        t[:, C_TRI + d * P:C_TRI + (d + 1) * P] = before
        t[:, C_STRICT + d * P:C_STRICT + (d + 1) * P] = before & (s != q)
        t[:, C_BASE + d * P:C_BASE + (d + 1) * P] = before & (s // 2 == q // 2)
        for l in range(LEVELS):
            a = C_LEVEL + (d * LEVELS + l) * P
            t[:, a:a + P] = (s // (2 << l) == q // (2 << l)) & (s // (1 << l) != q // (1 << l)) & before
    t[:, C_ONES:C_ONES + P] = 1
    t[:, C_HONES:C_HONES + P] = s // HD == q // HD
    t[:, C_ROT:C_ROT + P] = np.where(s // 32 == q // 32, np.where((q % 32 < 16) & (s == q + 16), -1.0, 0.0) + ((q % 32 >= 16) & (s == q - 16)), 0.0)
    tok = np.arange(SIDE)
    n_freq = HD // 8
    inv = (np.float32(10000.0) ** (-np.arange(n_freq, dtype=np.float32) / np.float32(n_freq))).astype(np.float32)
    ang = np.concatenate([(tok // 64).astype(np.float32)[:, None] * inv, (tok % 64).astype(np.float32)[:, None] * inv], axis=1)
    ch = np.arange(P) % 16
    t[:, C_COS:C_COS + SIDE] = np.cos(ang)[:, ch].T
    t[:, C_SIN:C_SIN + SIDE] = np.sin(ang)[:, ch].T
    for hd in range(HEADS):
        t[hd, C_SELH + hd * P:C_SELH + (hd + 1) * P] = 1
        t[hd, C_SELP + (hd // 2) * P + (hd % 2) * HD:C_SELP + (hd // 2) * P + (hd % 2 + 1) * HD] = 1
    for side in range(2):
        t[side, C_SEL2 + side * P:C_SEL2 + (side + 1) * P] = 1
    return t


def lay_out(x, c, ctx, c_ctx, ada_w, ada_b, w_in, rwkv_mu, rwkv_w0, rwkv_w2, rwkv_a0, rwkv_a2, rwkv_g2, rwkv_k_k, rwkv_k_a,
            rwkv_r_k, rwkv_lnx_g, rwkv_lnx_b, diff_lambda, diff_norm_g, hgrn_lb_logits, hgrn_norm_g, mlstm_conv_w, mlstm_conv_b,
            mlstm_gate_b, mlstm_norm_g, w_out, ffn_w_up, ffn_conv_w, ffn_conv_b, ffn_w_down, ln_g, ln_b):
    L = DEPTH
    w = np.zeros((L, D, IN_TILES * P), np.float32)
    w[:, :, 0:1184] = w_in[:, :, 0:1184]
    w[:, :, 1184:1200] = w_in[:, :, 4256:4272]
    w[:, :, 10 * P:] = w_in[:, :, 1184:4256]
    w = w.reshape(L, KD, P, IN_TILES, P).transpose(0, 3, 2, 1, 4).reshape(L, IN_TILES, P, KD * P)
    up = ffn_w_up.reshape(L, KD, P, 2, KF, P).transpose(0, 4, 2, 3, 1, 5).reshape(L, KF, P, 2 * KD * P)
    ada = ada_w.reshape(L, KD, P, 12, 512).transpose(0, 3, 2, 1, 4).reshape(L, 12, P, KD * 512)
    par = np.zeros((L, P, N_PAR), np.float32)

    def put(o, a, n):
        par[:, :, o:o + n] = a.reshape(L, n, P).transpose(0, 2, 1)

    mu = np.zeros((L, 10 * P), np.float32)
    mu[:, 0:1184] = rwkv_mu
    put(Q_MU, mu, 10)
    put(Q_W0, rwkv_w0, 4)
    put(Q_A0, rwkv_a0, 4)
    for o, a in ((Q_KK, rwkv_k_k), (Q_KA, rwkv_k_a), (Q_RK, rwkv_r_k), (Q_XG, rwkv_lnx_g), (Q_XB, rwkv_lnx_b), (Q_MN, mlstm_norm_g)):
        put(o, a, 2)
    put(Q_DN, np.tile(diff_norm_g, (1, 2)), 1)
    put(Q_HN, np.tile(hgrn_norm_g, (1, 2)), 1)
    for l in range(L):
        put(Q_LB + 2 * l, np.broadcast_to(hgrn_lb_logits[l], (L, 256)), 2)
    par[:, :, Q_MCW:Q_MCW + 12] = mlstm_conv_w.reshape(L, 3, 4, P).transpose(0, 3, 2, 1).reshape(L, P, 12)
    put(Q_MCB, mlstm_conv_b, 4)
    par[:, :, Q_FCW:Q_FCW + 3 * KF] = ffn_conv_w.reshape(L, 3, KF, P).transpose(0, 3, 2, 1).reshape(L, P, 3 * KF)
    put(Q_FCB, ffn_conv_b, KF)
    par[:, :, Q_GB:Q_GB + 16] = mlstm_gate_b.reshape(L, 1, 16)
    par[:, :, Q_LAM:Q_LAM + 128] = diff_lambda.reshape(L, 1, 128)
    par[:, :, Q_EPS] = LN_EPS
    par[:, :, Q_EPS + 1] = LNX_EPS
    par[:, :, Q_LORA:Q_LORA + 256] = rwkv_w2.reshape(L, P, 256)
    par[:, :, Q_LORA + 256:Q_LORA + 512] = rwkv_a2.reshape(L, P, 256)
    par[:, :, Q_LORA + 512:Q_LORA + 768] = rwkv_g2[:, 0:P]
    par[:, 0:32, Q_LORA + 768:Q_LORA + 1024] = rwkv_g2[:, P:160]
    ln = np.stack([ln_g, ln_b], axis=2).reshape(L, 2, 1, 2 * D)
    return {
        "x": x[0], "ctx": ctx[0], "const": constants(), "par": par,
        "cond": np.stack([c_ctx.reshape(KD, P), c.reshape(KD, P)], axis=0).transpose(2, 1, 0).reshape(P, 2 * KD),
        "ada_w": ada, "ada_b": np.broadcast_to(ada_b[:, None, :], (L, 2, 6 * D)), "w_in": w, "w_out": w_out.reshape(L, KD, P, D),
        "w_up": up, "w_down": ffn_w_down.reshape(L, KF, P, D), "ln": np.broadcast_to(ln, (L, 2, P, 2 * D)),
    }


def kernel(**inputs):
    import concourse.bacc as bacc
    from concourse.bass_utils import run_bass_kernel_spmd

    nc = bacc.Bacc("TRN2", target_bir_lowering=False, num_devices=1)
    arrays = {k: np.ascontiguousarray(v) for k, v in lay_out(**{k: np.asarray(v) for k, v in inputs.items()}).items()}
    A = {k: nc.dram_tensor(f"in_{k}", v.shape, F32, kind="ExternalInput").ap() for k, v in arrays.items()}
    out = nc.dram_tensor("out", (SIDE, D), F32, kind="ExternalOutput").ap()
    build(nc, A, out)
    r = run_bass_kernel_spmd(nc, [{f"in_{k}": v for k, v in arrays.items()}], core_ids=[0])
    return r.results[0]["out"].reshape(1, SIDE, D)
```

```python
from contextlib import ExitStack

import numpy as np
import concourse.bass as bass
from concourse import mybir

F32 = mybir.dt.float32
F32R = mybir.dt.float32r
I32 = mybir.dt.int32
ALU = mybir.AluOpType
ACT = mybir.ActivationFunctionType
AX_X = mybir.AxisListType.X

P = 128
D = 1024
KD = D // P
SIDE = 256
T = 2 * SIDE
TILES = T // P
DEPTH = 2
HEADS = 4
HD = 64
FF = 2816
KF = FF // P
ALPHA = (2.0 * DEPTH) ** 0.25
LN_EPS = 1e-5
LNX_EPS = 64e-5
ORDER = ((0, 1, 2, 3), (1, 0, 3, 2))
LEVELS = 7

T_R, T_K, T_V, T_WD, T_AD, T_GD, T_GD2 = 0, 2, 4, 6, 7, 8, 9
GATE_ROW = 32
T_DQ, T_DK, T_DV = 10, 12, 14
T_HQ, T_HF, T_HB, T_HI, T_HG = 16, 18, 20, 22, 24
T_MQ, T_MK, T_MV, T_MO = 26, 28, 30, 32
IN_TILES = 34

C_ID = 0
C_TRI = C_ID + P
C_STRICT = C_TRI + 2 * P
C_BASE = C_STRICT + 2 * P
C_ONES = C_BASE + 2 * P
C_HONES = C_ONES + P
C_ROT = C_HONES + P
C_COS = C_ROT + P
C_SIN = C_COS + SIDE
C_LEVEL = C_SIN + SIDE
C_SELH = C_LEVEL + 2 * LEVELS * P
C_SELP = C_SELH + HEADS * P
C_SEL2 = C_SELP + 2 * P
N_CONST = C_SEL2 + 2 * P

_o = 0


def _cols(n):
    global _o
    _o += n
    return _o - n


Q_MU, Q_W0, Q_A0, Q_KK, Q_KA, Q_RK, Q_XG, Q_XB = (_cols(n) for n in (10, 4, 4, 2, 2, 2, 2, 2))
Q_DN, Q_HN, Q_LB, Q_MCW, Q_MCB, Q_MN = (_cols(n) for n in (1, 1, 4, 12, 4, 2))
Q_FCW, Q_FCB, Q_GB, Q_LAM, Q_EPS, Q_LORA = (_cols(n) for n in (3 * KF, KF, 16, 128, 4, 1024))
N_PAR = _o


class Stage:

    zeroed, made = [], 0

    def __init__(self, nc):
        Stage.made += 1
        self.nc, self.sems, self.tag, self.memory = nc, {}, Stage.made, ExitStack()

    def sb(self, name, cols, dtype=F32):
        return self.memory.enter_context(self.nc.sbuf_tensor(f"{name}_{self.tag}", [P, cols], dtype))

    def __enter__(self):
        return self

    def __call__(self, name):
        if name not in self.sems:
            self.sems[name] = self.nc.alloc_semaphore(f"{name}_{self.tag}")
        return self.sems[name]

    def __exit__(self, *exc):
        self.memory.close()
        if exc[0] is None:
            for sem in Stage.zeroed:
                self.nc.release_semaphore(sem)
            for sem in self.sems.values():
                self.nc.sync.sem_clear(sem)
            Stage.zeroed = list(self.sems.values())


def linker(eng, sem):
    count = [0]

    def link(ins):
        count[0] += 1
        ins.then_inc(sem, 1)
        eng.wait_ge(sem, count[0])

    return link


def build(nc, A, out):
    Stage.zeroed, Stage.made = [], 0
    with ExitStack() as ctx:
        def sb(name, cols):
            return ctx.enter_context(nc.sbuf_tensor(name, [P, cols], F32))

        const = sb("const", N_CONST)
        par = sb("par", N_PAR)
        h = sb("h", TILES * D)
        pr = sb("pr", IN_TILES * T)
        mix = sb("mix", KD * T)
        gate = sb("gate", 4 * D)
        modc = sb("modc", 48 * 2)
        cond = sb("cond", KD * 2)
        fcol = sb("fcol", 16)
        ps = [ctx.enter_context(nc.psum_tensor(f"ps{i}", [P, 512], F32)) for i in range(8)]

        def c(o, n=P, rows=P):
            return const[0:rows, o:o + n]

        ident = c(C_ID)
        stored = ctx.enter_context(nc.semaphore("stored"))
        E = dict(stored=stored, nc=nc, A=A, out=out, c=c, const=const, ident=ident, par=par, h=h, pr=pr, mix=mix,
                 gate=gate, modc=modc, cond=cond, fcol=fcol, ps=ps)
        load_inputs(E)
        for layer in range(DEPTH):
            adaln(E, layer)
            input_projection(E, layer)
            with nc.sbuf_tensor(f"work{layer}", [P, 13312], F32) as E["work"], \
                    nc.sbuf_tensor(f"ring{layer}", [P, 4096], F32) as E["ring"]:
                diff_attention(E, layer)
                mlstm(E, layer)
                hgrn(E, layer)
                rwkv(E, layer)
            output_projection(E, layer)
            ffn(E, layer)
        store_output(E)


def load_inputs(E):
    nc, A, cond = (E[k] for k in ("nc", "A", "cond"))
    with Stage(nc) as S, nc.Block() as block:
        work = S.sb("sigmoid", 16)

        @block.sync
        def _(sp):
            sp.dma_start(cond[:, :], A["cond"]).then_inc(S("c"), 16)

        @block.scalar
        def _(act):
            act.wait_ge(S("c"), 16)
            nc.scalar.activation(work[:, 0:16], cond[:, :], ACT.Sigmoid).then_inc(S("sig"), 1)

        @block.vector
        def _(dve):
            dve.wait_ge(S("sig"), 1)
            nc.vector.tensor_tensor(cond[:, :], cond[:, :], work[:, 0:16], ALU.mult)


def split_high(nc, act, raw, high):
    return nc.scalar.copy(high, raw)


def split_low(nc, dve, raw, high, low):
    return nc.vector.tensor_tensor(low, raw, high.bitcast(F32), ALU.subtract)


def product(nc, out, stationary, moving, first, last):
    (sh, sl), (mh, ml) = stationary, moving
    nc.tensor.matmul(out, sh, mh, start=first, stop=False)
    nc.tensor.matmul(out, sh, ml, start=False, stop=False)
    return nc.tensor.matmul(out, sl, mh, start=False, stop=last)


def adaln(E, layer):
    nc, A, c, const, par, pr, h, mix, gate, modc, cond, ps = (
        E[k] for k in ("nc", "A", "c", "const", "par", "pr", "h", "mix", "gate", "modc", "cond", "ps"))
    NB, W = 12, KD * 512
    raw = (pr[:, 0:W], pr[:, W:2 * W], mix[:, :])
    SLOTS = len(raw)
    bias = pr[0:2, 2 * W:2 * W + NB * 512]
    rows = pr[0:2, 2 * W + NB * 512:2 * W + NB * 512 + 1024]
    with Stage(nc) as S, nc.Block() as block:
        condr = S.sb("condr", 2 * (2 * KD + P), F32R)
        wr = S.sb("wr", 4 * W, F32R)

        def high(n):
            return wr[:, (n % 2) * 2 * W:(n % 2) * 2 * W + W]

        def low(n):
            return wr[:, (n % 2) * 2 * W + W:(n % 2 + 1) * 2 * W]

        def cpart(p):
            return condr[:, p * (2 * KD + P):(p + 1) * (2 * KD + P)]

        @block.sync
        def _(sp):
            for n in range(NB):
                if n >= SLOTS:
                    sp.wait_ge(S("low"), n - SLOTS + 1)
                sp.dma_start(raw[n % SLOTS], A["ada_w"][layer, n]).then_inc(S(f"w{n % SLOTS}"), 16)
                if n == 0:
                    sp.dma_start(bias, A["ada_b"][layer]).then_inc(S("bias"), 16)
                    if layer == 0:
                        sp.dma_start(const[:, :], A["const"]).then_inc(S("const"), 16)
                if n == 2:
                    sp.dma_start(par[:, :], A["par"][layer]).then_inc(S("rest"), 16)
                    if layer == 0:
                        for first, source in ((0, "ctx"), (2, "x")):
                            sp.dma_start(h[:, :].rearrange("p (j d) -> p j d", j=TILES)[:, first:first + 2, :],
                                         A[source].rearrange("(j p) d -> p j d", p=P)).then_inc(S("rest"), 16)
            sp.wait_ge(S("rest"), 16 if layer else 48)

        @block.tensor
        def _(pe):
            def products(n):
                pe.wait_ge(S("high"), n + 1)
                pe.wait_ge(S("low"), n + 1)
                if n >= 2:
                    pe.wait_ge(S("row"), n - 1)
                for k in range(KD):
                    mm = product(nc, ps[n % 2][:, :], [cpart(p)[:, 2 * k:2 * k + P] for p in (0, 1)],
                                 [w[:, k * 512:(k + 1) * 512] for w in (high(n), low(n))], k == 0, k == KD - 1)
                mm.then_inc(S("mm"), 1)

            def spread(n):
                pe.wait_ge(S("row"), n + 1)
                if n >= 1:
                    pe.wait_ge(S("spread_out"), n)
                row = rows[:, (n % 2) * 512:(n % 2 + 1) * 512]
                if n // 2 in (2, 5):
                    for side in range(2):
                        mm = nc.tensor.matmul(ps[2 + side][:, :], c(C_SEL2 + side * P, P, 2), row, start=True, stop=True)
                else:
                    for b in range(4):
                        mm = nc.tensor.matmul(ps[2][:, 2 * b:2 * b + 2], row[:, b * P:(b + 1) * P],
                                              c(C_ID, 2, 2), start=True, stop=True)
                mm.then_inc(S("spread"), 1)

            pe.wait_ge(S("condr"), 2)
            if layer == 0:
                pe.wait_ge(S("const"), 16)
            for n in range(NB):
                products(n)
                if n >= 1:
                    spread(n - 1)
            spread(NB - 1)

        @block.scalar
        def _(act):
            act.wait_ge(S("condr0"), 1)
            nc.scalar.copy(cpart(0)[:, 0:2 * KD], cond[:, :]).then_inc(S("condr"), 1)
            for n in range(NB):
                act.wait_ge(S(f"w{n % SLOTS}"), 16 * (n // SLOTS + 1))
                if n >= 2:
                    act.wait_ge(S("mm"), n - 1)
                split_high(nc, act, raw[n % SLOTS], high(n)).then_inc(S("high"), 1)

        @block.vector
        def _(dve):
            nc.vector.memset(condr[:, :].bitcast(F32), 0.0).then_inc(S("condr0"), 1)
            dve.wait_ge(S("condr"), 1)
            split_low(nc, dve, cond[:, :], cpart(0)[:, 0:2 * KD], cpart(1)[:, 0:2 * KD]).then_inc(S("condr"), 1)
            for n in range(NB + 2):
                if n < NB:
                    dve.wait_ge(S("high"), n + 1)
                    if n >= 2:
                        dve.wait_ge(S("mm"), n - 1)
                    split_low(nc, dve, raw[n % SLOTS], high(n), low(n)).then_inc(S("low"), 1)
                if 1 <= n <= NB:
                    m = n - 1
                    if m == 0:
                        dve.wait_ge(S("bias"), 16)
                    dve.wait_ge(S("mm"), m + 1)
                    if m >= 2:
                        dve.wait_ge(S("spread"), m - 1)
                    nc.vector.tensor_tensor(rows[:, (m % 2) * 512:(m % 2 + 1) * 512], ps[m % 2][0:2, :],
                                            bias[:, m * 512:(m + 1) * 512], ALU.add).then_inc(S("row"), 1)
                if n >= 2:
                    m = n - 2
                    dve.wait_ge(S("spread"), m + 1)
                    if m // 2 in (2, 5):
                        g = m // 2 // 3
                        for side in range(2):
                            o = (2 * g + side) * D + (m % 2) * 512
                            ins = nc.vector.tensor_copy(gate[:, o:o + 512], ps[2 + side][:, :])
                    else:
                        ins = nc.vector.tensor_scalar(modc[:, 8 * m:8 * m + 8], ps[2][:, 0:8],
                                                      1.0 if m // 2 in (1, 4) else 0.0, None, ALU.add)
                    ins.then_inc(S("spread_out"), 1)


def transpose_modulate(E, S, hr, layer_tiles, tmp, pe=None, dve=None, act=None, shift=0, scale=1):
    nc, h, ps, modc, ident = (E[k] for k in ("nc", "h", "ps", "modc", "ident"))
    lo = layer_tiles[0] * P
    for k in range(KD):
        buf = tmp[:, (k % 2) * T:(k % 2 + 1) * T]
        if pe:
            if k >= 4:
                pe.wait_ge(S("modulated"), k - 3)
            for j in layer_tiles:
                mm = nc.tensor.transpose(ps[4 + k % 4][:, j * P:(j + 1) * P],
                                         h[:, j * D + k * P:j * D + (k + 1) * P], ident)
            mm.then_inc(S("turned"), 1)
        if act:
            act.wait_ge(S("turned"), k + 1)
            if k >= 2:
                act.wait_ge(S("hT"), k - 1)
            for side in range(layer_tiles[0] // 2, 2):
                a = modc[:, (scale * KD + k) * 2 + side:(scale * KD + k) * 2 + side + 1]
                b = modc[:, (shift * KD + k) * 2 + side:(shift * KD + k) * 2 + side + 1]
                ins = nc.scalar.activation(buf[:, side * SIDE:(side + 1) * SIDE], ps[4 + k % 4][:, side * SIDE:(side + 1) * SIDE],
                                           ACT.Identity, bias=b, scale=a)
            ins.then_inc(S("modulated"), 1)
            act.wait_ge(S("modulated"), k + 1)
            split_high(nc, act, buf[:, lo:], hr[0][:, k * T + lo:(k + 1) * T]).then_inc(S("hT_high"), 1)
        if dve:
            dve.wait_ge(S("hT_high"), k + 1)
            split_low(nc, dve, buf[:, lo:], hr[0][:, k * T + lo:(k + 1) * T], hr[1][:, k * T + lo:(k + 1) * T]).then_inc(S("hT"), 1)


def input_projection(E, layer):
    nc, A, ps, pr, mix, par = (E[k] for k in ("nc", "A", "ps", "pr", "mix", "par"))
    RAW, SLOTS, W = 4, 3, KD * P
    SHIFTED, SILU, CONV = range(0, T_GD2 + 1), (T_HQ, T_HQ + 1, T_HG, T_HG + 1), range(T_MQ, T_MQ + 4)

    def owner(m):
        return "dve" if m in SHIFTED or m in SILU or m in CONV else "act"

    def freed(m):
        return sum(owner(n) == owner(m) for n in range(m + 1))

    with Stage(nc) as S, nc.Block() as block:
        hr = [S.sb(f"hr{p}", KD * T, F32R) for p in range(2)]
        wr = S.sb("wr", SLOTS * 2 * W, F32R)
        tmp = S.sb("tmp", 2 * T)
        coef = S.sb("coef", 20)

        def raw(m):
            return mix[:, (m % RAW) * W:(m % RAW + 1) * W]

        def part(m, p):
            return wr[:, (2 * (m % SLOTS) + p) * W:(2 * (m % SLOTS) + p + 1) * W]

        @block.sync
        def _(sp):
            for m in range(IN_TILES):
                if m >= RAW:
                    sp.wait_ge(S("low"), m - RAW + 1)
                sp.dma_start(raw(m), A["w_in"][layer, m]).then_inc(S(f"w{m % RAW}"), 16)

        @block.tensor
        def _(pe):
            transpose_modulate(E, S, hr, range(TILES), tmp, pe=pe)
            for m in range(IN_TILES):
                pe.wait_ge(S("high"), m + 1)
                pe.wait_ge(S("low"), m + 1)
                if m >= 8:
                    pe.wait_ge(S(f"{owner(m - 8)}_out"), freed(m - 8))
                for k in range(KD):
                    if m == 0:
                        pe.wait_ge(S("hT"), k + 1)
                    mm = product(nc, ps[m % 8][:, :], [part(m, p)[:, k * P:(k + 1) * P] for p in (0, 1)],
                                 [x[:, k * T:(k + 1) * T] for x in hr], k == 0, k == KD - 1)
                mm.then_inc(S("mm"), 1)

        @block.vector
        def _(dve):
            link = linker(dve, S("link"))

            def low(m):
                dve.wait_ge(S("high"), m + 1)
                if m >= SLOTS:
                    dve.wait_ge(S("mm"), m - SLOTS + 1)
                split_low(nc, dve, raw(m), part(m, 0), part(m, 1)).then_inc(S("low"), 1)

            def three_taps(out, z, before, at, after, bias):
                o3, z3 = (v.rearrange("p (s t) -> p s t", s=2) for v in (out, z))
                if bias is None:
                    link(nc.vector.tensor_scalar(out, z, at, None, ALU.mult))
                else:
                    link(nc.vector.tensor_scalar(out, z, at, bias, ALU.mult, ALU.add))
                link(nc.vector.scalar_tensor_tensor(out=o3[:, :, 1:], in0=z3[:, :, :-1], scalar=before, in1=o3[:, :, 1:],
                                                    op0=ALU.mult, op1=ALU.add))
                return nc.vector.scalar_tensor_tensor(out=o3[:, :, :-1], in0=z3[:, :, 1:], scalar=after, in1=o3[:, :, :-1],
                                                      op0=ALU.mult, op1=ALU.add)

            def taps(n):
                z = ps[n % 8][:, :]
                if n in SHIFTED:
                    dve.wait_ge(S("mm"), n + 1)
                    near = coef[:, 10 + n:11 + n]
                    three_taps(pr[:, n * T:(n + 1) * T], z, near, coef[:, n:n + 1], near, None).then_inc(S("dve_out"), 1)
                if n in CONV:
                    dve.wait_ge(S("mm"), n + 1)
                    i = n - T_MQ
                    if i >= 2:
                        dve.wait_ge(S("conv_used"), i - 1)
                    w = [par[:, Q_MCW + 3 * i + k:Q_MCW + 3 * i + k + 1] for k in range(3)]
                    three_taps(tmp[:, (i % 2) * T:(i % 2 + 1) * T], z, *w, par[:, Q_MCB + i:Q_MCB + i + 1]).then_inc(S("dve_out"), 1)

            def silus(n):
                out = pr[:, n * T:(n + 1) * T]
                if n in SILU:
                    dve.wait_ge(S("sigmoid"), SILU.index(n) + 1)
                    nc.vector.tensor_tensor(out, ps[n % 8][:, :], out, ALU.mult).then_inc(S("dve_out"), 1)
                if n in CONV:
                    i = n - T_MQ
                    dve.wait_ge(S("conv_sigmoid"), i + 1)
                    nc.vector.scalar_tensor_tensor(out=out, in0=tmp[:, (i % 2) * T:(i % 2 + 1) * T], scalar=1.0 if i < 2 else HD ** -0.5,
                                                   in1=out, op0=ALU.mult, op1=ALU.mult).then_inc(S("conv_used"), 1)

            nc.vector.tensor_scalar(coef[:, 0:10], par[:, Q_MU:Q_MU + 10], -1.0, 1.0, ALU.mult, ALU.add)
            link(nc.vector.tensor_scalar(coef[:, 10:20], par[:, Q_MU:Q_MU + 10], 0.5, None, ALU.mult))
            low(0)
            low(1)
            transpose_modulate(E, S, hr, range(TILES), tmp, dve=dve)
            for n in range(IN_TILES + 1):
                if n + 2 < IN_TILES:
                    low(n + 2)
                silus(n - 1)
                taps(n)

        @block.scalar
        def _(act):
            def high(m):
                act.wait_ge(S(f"w{m % RAW}"), 16 * (m // RAW + 1))
                if m >= SLOTS:
                    act.wait_ge(S("mm"), m - SLOTS + 1)
                split_high(nc, act, raw(m), part(m, 0)).then_inc(S("high"), 1)

            def leave(n):
                z, out = ps[n % 8][:, :], pr[:, n * T:(n + 1) * T]
                if n in (T_WD, T_GD, T_GD2):
                    act.wait_ge(S("dve_out"), freed(n))
                    rows = 32 if n == T_GD2 else P
                    nc.scalar.activation(out[0:rows], out[0:rows], ACT.Tanh if n == T_WD else ACT.Sigmoid)
                elif n in CONV:
                    act.wait_ge(S("dve_out"), freed(n))
                    i = n - T_MQ
                    nc.scalar.activation(out, tmp[:, (i % 2) * T:(i % 2 + 1) * T], ACT.Sigmoid).then_inc(S("conv_sigmoid"), 1)
                elif n in SILU:
                    act.wait_ge(S("mm"), n + 1)
                    nc.scalar.activation(out, z, ACT.Sigmoid).then_inc(S("sigmoid"), 1)
                elif n not in SHIFTED:
                    act.wait_ge(S("mm"), n + 1)
                    if n >= T_MO:
                        nc.scalar.activation(out, z, ACT.Sigmoid).then_inc(S("act_out"), 1)
                    else:
                        nc.scalar.copy(out, z).then_inc(S("act_out"), 1)

            high(0)
            high(1)
            transpose_modulate(E, S, hr, range(TILES), tmp, act=act, shift=0, scale=1)
            for n in range(IN_TILES):
                if n + 2 < IN_TILES:
                    high(n + 2)
                leave(n)


def tiles(t, first, n):
    return t[:, first * T:(first + n) * T]


def active(layer):
    return (0, 1, 2, 3) if layer < DEPTH - 1 else (2, 3)


def span(layer):
    lo = active(layer)[0] * P
    return lo, T - lo


def two(t, layer):
    lo, _ = span(layer)
    return t.rearrange("p (i t) -> p i t", i=2)[:, :, lo:]


def halves(t, B, second):
    v = t.rearrange("p (m b t) -> p m b t", b=P // B, t=B)
    return v[:, :, :, B // 2:] if second else v[:, :, :, :B // 2]


def head_sums(E, pe, src, banks, layer):
    nc, c, ps = E["nc"], E["c"], E["ps"]
    lo, n = span(layer)
    for i in range(2):
        mm = nc.tensor.matmul(ps[banks[i]][:, lo:], c(C_HONES), src[:, i * T + lo:(i + 1) * T], start=True, stop=True)
    return mm


def diff_attention(E, layer):
    nc, c, par, pr, work, ring, mix, ps, ident = (E[k] for k in ("nc", "c", "par", "pr", "work", "ring", "mix", "ps", "ident"))
    act_tiles = active(layer)
    units = [(i, j, hh) for i in range(2) for j in act_tiles for hh in range(2)]
    lam_init = 0.8 - 0.6 * float(np.exp(-0.3 * layer))
    scale = (HD // 2) ** -0.5
    vT = work[:, 2048:2048 + 1024]
    e = work[:, 3072:3072 + 2048]
    prob = work[:, 5120:5120 + 1024]
    pT = work[:, 6144:6144 + 1024]
    rtmp = work[:, 7168:7168 + 1024]
    y = work[:, 8192:8192 + 1024]
    st = work[:, 9216:9216 + 256]
    sq = work[:, 9472:9472 + 1024]
    single = ring[:, 0:4096]

    with Stage(nc) as S, nc.Block() as block:
        for n in ("link", "link_act"):
            S(n)

        def keys(j):
            return (0, SIDE) if j < 2 else (0, T)

        def score_bank(u, q):
            return 6 * (u % 2) + q

        @block.tensor
        def _(pe):
            for m in range(4):
                mm = nc.tensor.matmul(ps[m // 2][:, (m % 2) * SIDE:(m % 2 + 1) * SIDE], c(C_ROT),
                                      pr[:, (T_DQ + m) * T + SIDE:(T_DQ + m + 1) * T], start=True, stop=True)
            mm.then_inc(S("rot"), 1)
            for j in range(TILES):
                for i in range(2):
                    mm = nc.tensor.transpose(ps[2 + j // 2][:, (j % 2) * 256 + i * P:(j % 2) * 256 + (i + 1) * P],
                                             pr[:, (T_DV + i) * T + j * P:(T_DV + i) * T + (j + 1) * P], ident)
            mm.then_inc(S("vT"), 1)
            pe.wait_ge(S("roped"), 1)
            pe.wait_ge(S("single"), 2)
            pe.wait_ge(S("vT_out"), 1)

            def scores(u):
                i, j, hh = units[u]
                if u >= 2:
                    pe.wait_ge(S("exp"), 2 * u - 2)
                lo, n = keys(j)
                for q in range(2):
                    t0 = ((2 * hh + q) * 2 + i) * T + j * P
                    mm = nc.tensor.matmul(ps[score_bank(u, q)][:, 0:n], single[:, t0:t0 + P],
                                          pr[:, (T_DK + i) * T:(T_DK + i) * T + n], start=True, stop=True)
                mm.then_inc(S("scores"), 1)

            def turn(u):
                pe.wait_ge(S("prob"), u + 1)
                if u >= 2:
                    pe.wait_ge(S("pT"), u - 1)
                n = keys(units[u][1])[1]
                for b in range(n // P):
                    mm = nc.tensor.transpose(ps[2 + u % 2][:, b * P:(b + 1) * P],
                                             prob[:, (u % 2) * T + b * P:(u % 2) * T + (b + 1) * P], ident)
                mm.then_inc(S("turned"), 1)

            def values(u):
                i, j, hh = units[u]
                pe.wait_ge(S("pT"), u + 1)
                n = keys(j)[1] // P
                for b in range(n):
                    mm = nc.tensor.matmul(ps[4 + i][hh * HD:(hh + 1) * HD, j * P:(j + 1) * P],
                                          vT[:, b * 256 + i * P + hh * HD:b * 256 + i * P + (hh + 1) * HD],
                                          pT[:, (u % 2) * T + b * P:(u % 2) * T + (b + 1) * P],
                                          start=(b == 0), stop=(b == n - 1))
                mm.then_inc(S("values"), 1)

            for u in range(len(units) + 3):
                if u < len(units):
                    scores(u)
                if 2 <= u <= len(units) + 1:
                    turn(u - 2)
                if u >= 3:
                    values(u - 3)
            pe.wait_ge(S("sq"), 1)
            head_sums(E, pe, sq, (6, 7), layer).then_inc(S("ss"), 1)

        @block.gpsimd
        def _(pool):
            nc.gpsimd.memset(single, 0.0).then_inc(S("zeros"), 1)

        @block.vector
        def _(dve):
            link = linker(dve, S("link"))
            lam = par[:, Q_LAM:Q_LAM + 128].rearrange("p (a b d) -> p a b d", a=2, b=2)
            link(nc.vector.tensor_tensor(st[:, 0:64].rearrange("p (a d) -> p a d", a=2), lam[:, :, 0, :], lam[:, :, 1, :], ALU.mult))
            nc.vector.tensor_reduce(st[:, 64:66], st[:, 0:64].rearrange("p (a d) -> p a d", a=2), AX_X, ALU.add).then_inc(S("lam_in"), 1)
            cosb = c(C_COS, SIDE).rearrange("p (i t) -> p i t", i=1).to_broadcast([P, 4, SIDE])
            sinb = c(C_SIN, SIDE).rearrange("p (i t) -> p i t", i=1).to_broadcast([P, 4, SIDE])
            qk = tiles(pr, T_DQ, 4).rearrange("p (m t) -> p m t", m=4)[:, :, SIDE:]
            rt = rtmp.rearrange("p (m t) -> p m t", m=4)
            dve.wait_ge(S("rot"), 1)
            for b in range(2):
                nc.vector.tensor_tensor(rt[:, 2 * b:2 * b + 2, :], ps[b][:, :].rearrange("p (m t) -> p m t", m=2),
                                        sinb[:, 0:2, :], ALU.mult)
            link(nc.vector.tensor_tensor(qk, qk, cosb, ALU.mult))
            nc.vector.tensor_tensor(qk, qk, rt, ALU.add).then_inc(S("roped"), 1)
            dve.wait_ge(S("roped"), 1)
            dve.wait_ge(S("zeros"), 1)
            for m in range(2):
                ins = nc.vector.tensor_copy(single[32 * m:32 * m + 32, m * 1024:(m + 1) * 1024], pr[32 * m:32 * m + 32, T_DQ * T:(T_DQ + 2) * T])
            ins.then_inc(S("single"), 1)
            dve.wait_ge(S("lam_exp"), 1)
            link(nc.vector.tensor_tensor(st[:, 68:69], st[:, 67:68], st[:, 66:67], ALU.subtract))
            link(nc.vector.tensor_scalar(st[:, 69:70], st[:, 68:69], -lam_init, None, ALU.add))

            def maxima(u):
                dve.wait_ge(S("scores"), u + 1)
                if u >= 2:
                    dve.wait_ge(S("exp"), 2 * u - 2)
                n = keys(units[u][1])[1]
                for q in range(2):
                    ins = nc.vector.tensor_reduce(st[:, 80 + 8 * (u % 2) + q:81 + 8 * (u % 2) + q], ps[score_bank(u, q)][:, 0:n], AX_X, ALU.max)
                link(ins)
                s = 80 + 8 * (u % 2)
                nc.vector.tensor_scalar(st[:, s + 2:s + 4], st[:, s:s + 2], -scale, None, ALU.mult).then_inc(S("max"), 1)

            def combine(u):
                s = 80 + 8 * (u % 2)
                n = keys(units[u][1])[1]
                dve.wait_ge(S("exp"), 2 * u + 2)
                link(nc.vector.reciprocal(st[:, s + 6:s + 8], st[:, s + 4:s + 6]))
                link(nc.vector.tensor_tensor(st[:, s + 7:s + 8], st[:, s + 7:s + 8], st[:, 69:70], ALU.mult))
                e0, e1 = (e[:, (u % 2) * 1024 + q * 512:(u % 2) * 1024 + q * 512 + n] for q in range(2))
                link(nc.vector.tensor_scalar(e1, e1, st[:, s + 7:s + 8], None, ALU.mult))
                if u >= 2:
                    dve.wait_ge(S("turned"), u - 1)
                nc.vector.scalar_tensor_tensor(out=prob[:, (u % 2) * T:(u % 2) * T + n], in0=e0, scalar=st[:, s + 6:s + 7], in1=e1,
                                               op0=ALU.mult, op1=ALU.add).then_inc(S("prob"), 1)

            for u in range(len(units) + 1):
                if u < len(units):
                    maxima(u)
                if u >= 1:
                    combine(u - 1)
            dve.wait_ge(S("values"), len(units))
            lo, n = span(layer)
            for i in range(2):
                ins = nc.vector.tensor_copy(y[:, i * T + lo:(i + 1) * T], ps[4 + i][:, lo:])
            link(ins)
            nc.vector.tensor_tensor(two(sq, layer), two(y, layer), two(y, layer), ALU.mult).then_inc(S("sq"), 1)
            dve.wait_ge(S("rn"), 1)
            link(nc.vector.tensor_tensor(two(y, layer), two(y, layer), two(sq, layer), ALU.mult))
            nc.vector.tensor_scalar(two(tiles(mix, 2, 2), layer), two(y, layer), par[:, Q_DN:Q_DN + 1], 1.0 - lam_init,
                                    ALU.mult, ALU.mult)

        @block.scalar
        def _(act):
            act.wait_ge(S("vT"), 1)
            nc.scalar.copy(vT[:, 0:512], ps[2][:, :])
            nc.scalar.copy(vT[:, 512:1024], ps[3][:, :]).then_inc(S("vT_out"), 1)
            act.wait_ge(S("lam_in"), 1)
            nc.scalar.activation(st[:, 66:68], st[:, 64:66], ACT.Exp).then_inc(S("lam_exp"), 1)

            act.wait_ge(S("roped"), 1)
            act.wait_ge(S("zeros"), 1)
            for m in range(2, 4):
                ins = nc.scalar.copy(single[32 * m:32 * m + 32, m * 1024:(m + 1) * 1024], pr[32 * m:32 * m + 32, T_DQ * T:(T_DQ + 2) * T])
            ins.then_inc(S("single"), 1)

            def exps(u):
                s = 80 + 8 * (u % 2)
                n = keys(units[u][1])[1]
                act.wait_ge(S("max"), u + 1)
                if u >= 2:
                    act.wait_ge(S("prob"), u - 1)
                for q in range(2):
                    nc.scalar.activation(e[:, (u % 2) * 1024 + q * 512:(u % 2) * 1024 + q * 512 + n], ps[score_bank(u, q)][:, 0:n], ACT.Exp,
                                         bias=st[:, s + 2 + q:s + 3 + q], scale=scale,
                                         accum_out=st[:, s + 4 + q:s + 5 + q]).then_inc(S("exp"), 1)

            def pt_out(u):
                n = keys(units[u][1])[1]
                act.wait_ge(S("turned"), u + 1)
                if u >= 2:
                    act.wait_ge(S("values"), u - 1)
                nc.scalar.copy(pT[:, (u % 2) * T:(u % 2) * T + n], ps[2 + u % 2][:, 0:n]).then_inc(S("pT"), 1)

            for u in range(len(units) + 2):
                if u < len(units):
                    exps(u)
                if u >= 2:
                    pt_out(u - 2)
            inverse_rms(E, S, act, (6, 7), sq, layer, 1.0 / HD, Q_EPS)


def inverse_rms(E, S, act, banks, dst, layer, scale, eps):
    nc, ps, par = E["nc"], E["ps"], E["par"]
    lo, n = span(layer)
    act.wait_ge(S("ss"), 1)
    for i in range(2):
        ins = nc.scalar.activation(dst[:, i * T + lo:(i + 1) * T], ps[banks[i]][:, lo:], ACT.Ln, bias=par[:, eps:eps + 1], scale=scale)
    ins.then_inc(S("ln"), 1)
    act.wait_ge(S("ln"), 1)
    nc.scalar.activation(two(dst, layer), two(dst, layer), ACT.Exp, scale=-0.5).then_inc(S("rn"), 1)


def mlstm(E, layer):
    nc, c, par, pr, work, ring, mix, ps, ident = (E[k] for k in ("nc", "c", "par", "pr", "work", "ring", "mix", "ps", "ident"))
    js = active(layer)
    lo0, _ = span(layer)
    PADW = P + SIDE
    o = [2048]

    def take(n):
        o[0] += n
        return work[:, o[0] - n:o[0]]

    vT = take(1024)
    ws = (take(4096), ring[:, 0:4096])
    xs = (take(1024), take(1024))
    pads = take(3072)
    pad = pads[0:4, :]
    brows = take(1024)
    brow = brows[0:4, :]
    single = work[:, 0:2048]
    floors = ((brows[:, 0:T], brows[:, T:2 * T]), (pads[:, 2 * (P + SIDE):2 * (P + SIDE) + T], pads[:, 6 * (P + SIDE):6 * (P + SIDE) + T]))
    floor = pr[0:4, T_DQ * T:(T_DQ + 2) * T]
    small = pr[:, (T_DQ + 2) * T:(T_DQ + 3) * T]
    gt = small[:, 0:64].rearrange("p (j g) -> p j g", j=TILES)
    lf = small[:, 64:96]
    la, lb_, gc = small[:, 96:128], small[:, 128:160], small[:, 160:192]
    ys = tiles(pr, T_DQ + 3, 2)
    y = tiles(mix, 6, 2)
    sq = xs[0]

    def padded(d, pp):
        return pad[:, (2 * d + pp) * 2 * PADW:(2 * d + pp + 1) * 2 * PADW].rearrange("p (s t) -> p s t", s=2)

    def own(d, pp, shift=0):
        a = P - shift if d == 0 else shift
        return padded(d, pp)[:, :, a:a + SIDE]

    def reach(d, s):
        lo = s * P if d == 0 else (0 if s < 2 else SIDE)
        return max(lo, lo0), (T if (d == 0 or s != 2) else 3 * P)

    def earlier(d, j):
        return ORDER[d][:ORDER[d].index(j)]

    with Stage(nc) as S, nc.Block() as block:
        for n in ("link", "vT", "gates", "rows", "mb", "qk", "w", "values", "x", "e", "den"):
            S(n)

        @block.tensor
        def _(pe):
            for j in range(TILES):
                mm = nc.tensor.transpose(ps[0][:, j * 64:(j + 1) * 64], pr[0:64, T_GD2 * T + j * P:T_GD2 * T + (j + 1) * P], c(C_ID, 64, 64))
            mm.then_inc(S("gates"), 1)
            for j in range(TILES):
                for i in range(2):
                    mm = nc.tensor.transpose(ps[1 + j // 2][:, (j % 2) * 256 + i * P:(j % 2) * 256 + (i + 1) * P],
                                             pr[:, (T_MV + i) * T + j * P:(T_MV + i) * T + (j + 1) * P], ident)
            mm.then_inc(S("vT"), 1)
            pe.wait_ge(S("lf"), 1)
            for d in range(2):
                for j in range(TILES):
                    out = ps[3 + d][0:4, j * P:(j + 1) * P]
                    for n, s in enumerate((*earlier(d, j), j)):
                        nc.tensor.matmul(out, lf[:, s * 8 + d * 4:s * 8 + d * 4 + 4], c(C_ONES) if s != j else c(C_TRI + d * P),
                                         start=(n == 0), stop=(s == j))
                for j in range(TILES):
                    nc.tensor.matmul(ps[5 + d][0:4, j * P:(j + 1) * P], gt[:, j, d * 4:d * 4 + 4], ident, start=True, stop=True)
            for d in range(2):
                for j in range(TILES):
                    out = ps[7][:, j * 8 + d * 4:j * 8 + d * 4 + 4]
                    for n, s in enumerate((*earlier(d, j), j)):
                        mm = nc.tensor.matmul(out, c(C_ONES) if s != j else c(C_TRI + d * P), lf[:, s * 8 + d * 4:s * 8 + d * 4 + 4],
                                              start=(n == 0), stop=(s == j))
            mm.then_inc(S("rows"), 1)
            pe.wait_ge(S("vT_out"), 1)

            def broadcasts(hd):
                if hd == 0:
                    pe.wait_ge(S("maxed"), 1)
                else:
                    pe.wait_ge(S("x"), 2 * TILES * hd)
                for d in range(2):
                    M = own(d, 0)[:, lo0 // SIDE:, :]
                    mm = nc.tensor.matmul(ps[d][:, lo0:], c(C_SELH + hd * P, P, 4), M, start=True, stop=True)
                mm.then_inc(S("mb"), 1)

            def qk(hd, s):
                n = TILES * hd + s
                if n >= 2:
                    pe.wait_ge(S("w"), 2 * (n - 1))
                i = hd // 2
                lo = lo0 if s < 2 else SIDE
                t0 = ((hd % 2) * 2 + i) * T + s * P
                nc.tensor.matmul(ps[2 + s % 2][:, lo:], single[:, t0:t0 + P],
                                 pr[:, (T_MQ + i) * T + lo:(T_MQ + i + 1) * T], start=True, stop=True).then_inc(S("qk"), 1)

            def values(hd):
                r = (hd % 2) * HD
                pe.wait_ge(S("w"), 2 * TILES * (hd + 1))
                pe.wait_ge(S("masked"), len(js) * (hd + 1))
                if hd == 2:
                    pe.wait_ge(S("pair_out"), 2)
                for d in range(2):
                    for j in js:
                        seen = (*earlier(d, j), j)
                        for bank, lhs in ((4 + d, None), (6 + d, c(C_ONES, HD))):
                            for n, s in enumerate(seen):
                                l = lhs if lhs is not None else vT[:, s * 256 + hd * HD:s * 256 + (hd + 1) * HD]
                                mm = nc.tensor.matmul(ps[bank][r:r + HD, j * P:(j + 1) * P], l,
                                                      ws[hd % 2][:, d * 2048 + s * T + j * P:d * 2048 + s * T + (j + 1) * P],
                                                      start=(n == 0), stop=(n == len(seen) - 1))
                mm.then_inc(S("values"), 1)

            pe.wait_ge(S("floor"), 1)
            for i in range(2):
                for d in range(2):
                    mm = nc.tensor.matmul(ps[4 + 2 * i + d][:, lo0:], c(C_SELP + i * P, P, 4), floor[:, d * T + lo0:(d + 1) * T],
                                          start=True, stop=True)
            mm.then_inc(S("floor_b"), 1)
            pe.wait_ge(S("single"), 1)
            for hd in range(HEADS + 1):
                if hd < HEADS:
                    broadcasts(hd)
                    qk(hd, 0)
                    qk(hd, 1)
                if hd >= 1:
                    if hd == 1:
                        pe.wait_ge(S("floors"), 1)
                    values(hd - 1)
                if hd < HEADS:
                    qk(hd, 2)
                    qk(hd, 3)
            pe.wait_ge(S("pair_out"), 4)
            head_sums(E, pe, y, (6, 7), layer).then_inc(S("mean"), 1)
            pe.wait_ge(S("sq"), 1)
            head_sums(E, pe, sq, (4, 5), layer).then_inc(S("ss"), 1)

        @block.gpsimd
        def _(pool):
            pool.memset(pad[:, :], 0.0).then_inc(S("pad0"), 1)
            nc.gpsimd.memset(single, 0.0).then_inc(S("zeros"), 1)
            for hd in range(HEADS):
                for s in js:
                    pool.wait_ge(S("w"), 2 * (TILES * hd + s + 1))
                    for d in range(2):
                        b = ws[hd % 2][:, d * 2048 + s * T + s * P:d * 2048 + s * T + (s + 1) * P]
                        ins = nc.gpsimd.tensor_tensor(b, b, c(C_TRI + d * P), ALU.mult)
                    ins.then_inc(S("masked"), 1)

        @block.vector
        def _(dve):
            link = linker(dve, S("link"))
            dve.wait_ge(S("zeros"), 1)
            for q in range(2):
                ins = nc.vector.tensor_copy(single[q * HD:(q + 1) * HD, q * 1024:(q + 1) * 1024], pr[q * HD:(q + 1) * HD, T_MK * T:(T_MK + 2) * T])
            ins.then_inc(S("single"), 1)
            dve.wait_ge(S("gates"), 1)
            gb = par[:, Q_GB:Q_GB + 16].rearrange("p (j g) -> p j g", j=1).to_broadcast([P, TILES, 16])
            g4 = small[:, 0:64].rearrange("p (j g) -> p j g", j=TILES)
            link(nc.vector.tensor_tensor(g4, ps[0][:, 0:256].rearrange("p (j g) -> p j g", j=TILES)[:, :, GATE_ROW:GATE_ROW + 16], gb, ALU.add))
            f = g4[:, :, 8:16]
            lf3, la3, lb3 = (v.rearrange("p (j g) -> p j g", j=TILES) for v in (lf, la, lb_))
            link(nc.vector.tensor_scalar(la3, f, -1.0, None, ALU.mult))
            link(nc.vector.tensor_tensor(la3, la3, f, ALU.min))
            nc.vector.tensor_scalar(lb3, f, 0.0, None, ALU.min).then_inc(S("absf"), 1)
            dve.wait_ge(S("lnf"), 1)
            nc.vector.tensor_tensor(lf3, lb3, la3, ALU.subtract).then_inc(S("lf"), 1)
            dve.wait_ge(S("pad0"), 1)
            dve.wait_ge(S("brow"), 1)
            for d in range(2):
                ins = nc.vector.tensor_tensor(own(d, 0), ps[5 + d][0:4, :].rearrange("p (s t) -> p s t", s=2),
                                              brow[:, d * T:(d + 1) * T].rearrange("p (s t) -> p s t", s=2), ALU.subtract)
            link(ins)
            nc.vector.tensor_tensor(gc.rearrange("p (j g) -> p j g", j=TILES), g4[:, :, 0:8],
                                    ps[7][:, 0:32].rearrange("p (j g) -> p j g", j=TILES), ALU.subtract)
            pp = 0
            for k in (1, 2, 4, 8, 16, 32, 64, 128):
                for d in range(2):
                    ins = nc.vector.tensor_tensor(own(d, 1 - pp), own(d, pp), own(d, pp, k), ALU.max)
                link(ins)
                pp = 1 - pp
            for d in range(2):
                end = own(d, 0)[:, 0, SIDE - 1:SIDE] if d == 0 else own(d, 0)[:, 0, 0:1]
                ins = nc.vector.tensor_scalar(own(d, 0)[:, 1, :], own(d, 0)[:, 1, :], end, 0.0, ALU.max, ALU.max)
            link(ins)
            for d in range(2):
                ins = nc.vector.tensor_scalar(own(d, 0)[:, 0, :], own(d, 0)[:, 0, :], 0.0, None, ALU.max)
            ins.then_inc(S("maxed"), 1)
            dve.wait_ge(S("maxed"), 1)
            for d in range(2):
                ins = nc.vector.tensor_tensor(floor[:, d * T:(d + 1) * T].rearrange("p (s t) -> p s t", s=2), own(d, 0),
                                              brow[:, d * T:(d + 1) * T].rearrange("p (s t) -> p s t", s=2), ALU.add)
            link(ins)
            nc.vector.tensor_scalar(floor, floor, -1.0, 60.0, ALU.mult, ALU.min).then_inc(S("floor_in"), 1)

            def exponents(n):
                hd, s = divmod(n, TILES)
                x = xs[s % 2]
                dve.wait_ge(S("mb"), hd + 1)
                for d in range(2):
                    if n >= 2:
                        dve.wait_ge(S("w"), 2 * (n - 2) + d + 1)
                    a, b = reach(d, s)
                    nc.vector.tensor_scalar(x[:, d * T + a:d * T + b], ps[d][:, a:b], gc[:, s * 8 + d * 4 + hd:s * 8 + d * 4 + hd + 1],
                                            0.0, ALU.subtract, ALU.max).then_inc(S("x"), 1)

            def weights(n):
                hd, s = divmod(n, TILES)
                x, w = xs[s % 2], ws[hd % 2]
                dve.wait_ge(S("qk"), n + 1)
                if hd >= 2:
                    dve.wait_ge(S("values"), hd - 1)
                for d in range(2):
                    dve.wait_ge(S("e"), 2 * n + d + 1)
                    a, b = reach(d, s)
                    nc.vector.tensor_tensor(w[:, d * 2048 + s * T + a:d * 2048 + s * T + b], x[:, d * T + a:d * T + b],
                                            ps[2 + s % 2][:, a:b], ALU.mult).then_inc(S("w"), 1)

            def pair(i):
                dve.wait_ge(S("den"), 2 * (i + 1))
                for d in range(2):
                    yd = ys[:, d * T + lo0:(d + 1) * T]
                    ins = nc.vector.tensor_tensor(yd, yd, floors[i][d][:, lo0:], ALU.max)
                link(ins)
                for d in range(2):
                    ins = nc.vector.reciprocal(ys[:, d * T + lo0:(d + 1) * T], ys[:, d * T + lo0:(d + 1) * T])
                link(ins)
                for d in range(2):
                    yd = ys[:, d * T + lo0:(d + 1) * T]
                    nc.vector.tensor_tensor(yd, yd, ps[4 + d][:, lo0:], ALU.mult).then_inc(S("pair_y"), 1)
                dve.wait_ge(S("pair_y"), 2 * (i + 1))
                nc.vector.tensor_tensor(y[:, i * T + lo0:(i + 1) * T], ys[:, lo0:T], ys[:, T + lo0:2 * T], ALU.add).then_inc(S("pair_out"), 2)

            dve.wait_ge(S("floor_b"), 1)
            for i in range(2):
                for d in range(2):
                    ins = nc.vector.tensor_copy(floors[i][d][:, lo0:], ps[4 + 2 * i + d][:, lo0:])
            ins.then_inc(S("floors"), 1)
            exponents(0)
            for n in range(HEADS * TILES):
                if n + 1 < HEADS * TILES:
                    exponents(n + 1)
                weights(n)
                if n == 3 * TILES - 1:
                    pair(0)
            pair(1)
            dve.wait_ge(S("pair_out"), 4)
            dve.wait_ge(S("mean"), 1)
            for i in range(2):
                v = y[:, i * T + lo0:(i + 1) * T]
                ins = nc.vector.scalar_tensor_tensor(out=v, in0=ps[6 + i][:, lo0:], scalar=-1.0 / HD, in1=v, op0=ALU.mult, op1=ALU.add)
            link(ins)
            nc.vector.tensor_tensor(two(sq, layer), two(y, layer), two(y, layer), ALU.mult).then_inc(S("sq"), 1)
            dve.wait_ge(S("rn"), 1)
            link(nc.vector.tensor_tensor(two(y, layer), two(y, layer), two(sq, layer), ALU.mult))
            for i in range(2):
                v = y[:, i * T + lo0:(i + 1) * T]
                nc.vector.scalar_tensor_tensor(out=v, in0=v, scalar=par[:, Q_MN + i:Q_MN + i + 1],
                                               in1=pr[:, (T_MO + i) * T + lo0:(T_MO + i + 1) * T], op0=ALU.mult, op1=ALU.mult)

        @block.scalar
        def _(act):
            act.wait_ge(S("vT"), 1)
            nc.scalar.copy(vT[:, 0:512], ps[1][:, :])
            nc.scalar.copy(vT[:, 512:1024], ps[2][:, :]).then_inc(S("vT_out"), 1)
            act.wait_ge(S("absf"), 1)
            nc.scalar.activation(la, la, ACT.Exp).then_inc(S("link_act"), 1)
            act.wait_ge(S("link_act"), 1)
            nc.scalar.activation(la, la, ACT.Ln, bias=1.0).then_inc(S("lnf"), 1)
            act.wait_ge(S("rows"), 1)
            nc.scalar.copy(brow[:, 0:T], ps[3][0:4, :])
            nc.scalar.copy(brow[:, T:2 * T], ps[4][0:4, :]).then_inc(S("brow"), 1)
            act.wait_ge(S("floor_in"), 1)
            nc.scalar.activation(floor, floor, ACT.Exp).then_inc(S("floor"), 1)
            def denominators(i):
                act.wait_ge(S("values"), 2 * (i + 1))
                if i:
                    act.wait_ge(S("pair_out"), 2)
                for d in range(2):
                    nc.scalar.activation(ys[:, d * T + lo0:(d + 1) * T], ps[6 + d][:, lo0:], ACT.Abs).then_inc(S("den"), 1)

            for n in range(HEADS * TILES):
                s = n % TILES
                for d in range(2):
                    act.wait_ge(S("x"), 2 * n + d + 1)
                    a, b = reach(d, s)
                    x = xs[s % 2][:, d * T + a:d * T + b]
                    nc.scalar.activation(x, x, ACT.Exp, scale=-1.0).then_inc(S("e"), 1)
                if n == 3 * TILES - 1:
                    denominators(0)
            act.wait_ge(S("qk"), HEADS * TILES)
            nc.scalar.activation(work[:, 0:2048], tiles(pr, T_HF, 4), ACT.Sigmoid).then_inc(S("sigmoid"), 1)
            act.wait_ge(S("sigmoid"), 1)
            nc.scalar.activation(tiles(pr, T_HF, 4), tiles(pr, T_HF, 4), ACT.Sigmoid, scale=-1.0)
            denominators(1)
            inverse_rms(E, S, act, (4, 5), sq, layer, 1.0 / HD, Q_EPS)


def hgrn(E, layer):
    nc, c, par, pr, work, mix, ring, ps, ident = (E[k] for k in ("nc", "c", "par", "pr", "work", "mix", "ring", "ps", "ident"))
    js = active(layer)
    lo0, _ = span(layer)
    o = [0]

    def take(n):
        o[0] += n
        return work[:, o[0] - n:o[0]]

    cum = take(2048)
    lT = take(2048)
    vT = take(1024)
    at = take(4096)
    st = take(1024)
    A0 = take(3072)
    A1 = tiles(pr, T_DQ, 6)
    expo = (A0[:, 0:1024], A1[:, 0:1024])
    keys = (A0[:, 2048:3072], A1[:, 2048:3072])
    queries = (ring[:, 0:2048], ring[:, 2048:4096])
    qd = pr[:, T_MQ * T:(T_MQ + 4) * T]
    kd = pr[:, (T_MQ + 4) * T:(T_MQ + 8) * T]
    y = tiles(mix, 4, 2)
    sq = A0[:, 0:1024]
    col = tiles(mix, 0, 1)[:, 0:16]
    ecol = tiles(mix, 0, 1)[:, 16:32]
    steps = [(d, l) for l in range(LEVELS) for d in range(2)]

    with Stage(nc) as S, nc.Block() as block:
        def end(d):
            return P - 1 if d == 0 else 0

        def blocks(t, l):
            return t.rearrange("p (i b t) -> p i b t", i=2, t=2 << l)[:, :, lo0 // (2 << l):, :]

        def half(t, l, second):
            h_ = 1 << l
            return blocks(t, l)[:, :, :, h_:] if second else blocks(t, l)[:, :, :, :h_]

        def later(t, d, l):
            return blocks(t, 0) if l == 0 else half(t, l, d == 0)

        def score_bank(n, j):
            return ps[4 * (n % 2) + j]

        def sooner(t, d, l):
            return blocks(t, 0) if l == 0 else half(t, l, d == 1)

        @block.tensor
        def _(pe):
            for j in range(TILES):
                for i in range(2):
                    mm = nc.tensor.transpose(ps[j // 2][:, (j % 2) * 256 + i * P:(j % 2) * 256 + (i + 1) * P],
                                             pr[:, (T_HI + i) * T + j * P:(T_HI + i) * T + (j + 1) * P], ident)
            mm.then_inc(S("vT"), 1)
            pe.wait_ge(S("logf"), 1)
            for d in range(2):
                for j in range(TILES):
                    for i in range(2):
                        mm = nc.tensor.transpose(ps[2 + 2 * d + j // 2][:, (j % 2) * 256 + i * P:(j % 2) * 256 + (i + 1) * P],
                                                 cum[:, (2 * d + i) * T + j * P:(2 * d + i) * T + (j + 1) * P], ident)
            mm.then_inc(S("lT"), 1)
            pe.wait_ge(S("lT_out"), 2)
            pe.wait_ge(S("vT_out"), 1)
            for d in range(2):
                for i in range(2):
                    for j in range(TILES):
                        mm = nc.tensor.matmul(ps[(6, 7, 0, 1)[2 * d + i]][:, j * P:(j + 1) * P],
                                              lT[:, (d * TILES + j) * 256 + i * P:(d * TILES + j) * 256 + (i + 1) * P],
                                              c(C_TRI + d * P), start=True, stop=True)
            mm.then_inc(S("cum"), 1)
            pe.wait_ge(S("kd"), 1)
            for d in range(2):
                for j in range(TILES):
                    for i in range(2):
                        mm = nc.tensor.transpose(ps[2 + 2 * d + j // 2][:, (j % 2) * 256 + i * P:(j % 2) * 256 + (i + 1) * P],
                                                 kd[:, (2 * d + i) * T + j * P:(2 * d + i) * T + (j + 1) * P], ident)
            mm.then_inc(S("kT"), 1)
            pe.wait_ge(S("kT_out"), 2)
            for d in range(2):
                for j in range(TILES):
                    for hd in range(HEADS):
                        r, i = (hd % 2) * HD, hd // 2
                        mm = nc.tensor.matmul(ps[6 + d][r:r + HD, (2 * j + i) * HD:(2 * j + i + 1) * HD],
                                              lT[:, (d * TILES + j) * 256 + hd * HD:(d * TILES + j) * 256 + (hd + 1) * HD],
                                              vT[:, j * 256 + hd * HD:j * 256 + (hd + 1) * HD], start=True, stop=True)
            mm.then_inc(S("kv"), 1)
            for n, (d, l) in enumerate(steps):
                pe.wait_ge(S("kf"), n + 1)
                for m, j in enumerate(js):
                    if n >= 2:
                        pe.wait_ge(S("at"), len(js) * (n - 2) + m + 1)
                    for i in range(2):
                        t0 = i * T + j * P
                        both = queries[d].rearrange("p (q t) -> p q t", q=2)[:, :, t0:t0 + P]
                        mm = nc.tensor.matmul(score_bank(n, j)[:, i * 256:(i + 1) * 256], keys[d][:, t0:t0 + P], both, start=True, stop=True)
                    mm.then_inc(S("s_mm"), 1)
            pe.wait_ge(S("at"), len(js) * len(steps))
            for hd in range(HEADS):
                r, i = (hd % 2) * HD, hd // 2
                for j in js:
                    terms = []
                    for d in range(2):
                        terms.append((vT[:, j * 256 + hd * HD:j * 256 + (hd + 1) * HD],
                                      at[:, d * 2048 + (4 * j + hd) * P:d * 2048 + (4 * j + hd + 1) * P]))
                    for d in range(2):
                        if ORDER[d].index(j) > 0:
                            terms.append((st[r:r + HD, d * 512 + (2 * j + i) * HD:d * 512 + (2 * j + i + 1) * HD],
                                          qd[r:r + HD, (2 * d + i) * T + j * P:(2 * d + i) * T + (j + 1) * P]))
                    for n, (l, rh) in enumerate(terms):
                        mm = nc.tensor.matmul(ps[4 + i][r:r + HD, j * P:(j + 1) * P], l, rh, start=(n == 0), stop=(n == len(terms) - 1))
            mm.then_inc(S("y"), 1)
            pe.wait_ge(S("sq"), 1)
            head_sums(E, pe, sq, (6, 7), layer).then_inc(S("ss"), 1)

        @block.gpsimd
        def _(pool):
            nc.gpsimd.memset(ring[:, :], 0.0)
            nc.gpsimd.memset(at[:, :], 0.0).then_inc(S("at0"), 1)

        @block.vector
        def _(dve):
            link = linker(dve, S("link"))
            if layer == 0:
                link(nc.vector.memset(col[:, 0:2], 0.0))
            else:
                nc.vector.tensor_tensor(col[:, 4:6], par[:, Q_LB:Q_LB + 2], par[:, Q_LB + 2:Q_LB + 4], ALU.max).then_inc(S("lb_max"), 1)
                dve.wait_ge(S("lb_max"), 1)
                link(nc.vector.tensor_tensor(col[:, 6:8], par[:, Q_LB:Q_LB + 2], col[:, 4:6], ALU.subtract))
                nc.vector.tensor_tensor(col[:, 8:10], par[:, Q_LB + 2:Q_LB + 4], col[:, 4:6], ALU.subtract).then_inc(S("lb_in"), 1)
                dve.wait_ge(S("lb_exp"), 1)
                link(nc.vector.tensor_tensor(col[:, 10:12], col[:, 6:8], col[:, 8:10], ALU.add))
                link(nc.vector.reciprocal(col[:, 10:12], col[:, 10:12]))
                link(nc.vector.tensor_tensor(col[:, 0:2], col[:, 8:10], col[:, 10:12], ALU.mult))
            nc.vector.tensor_scalar(col[:, 2:4], col[:, 0:2], -1.0, 1.0, ALU.mult, ALU.add)
            nc.vector.tensor_scalar(col[:, 12:14], col[:, 0:2], 1e-30, None, ALU.max).then_inc(S("lb"), 1)
            dve.wait_ge(S("lb"), 1)
            for d in range(2):
                for i in range(2):
                    t = tiles(pr, T_HF + 2 * d + i, 1)
                    ins = nc.vector.tensor_scalar(t, t, col[:, 2 + i:3 + i], None, ALU.mult)
            link(ins)
            dve.wait_ge(S("lT"), 1)
            nc.vector.tensor_copy(lT[:, 0:512], ps[2][:, :])
            nc.vector.tensor_copy(lT[:, 512:1024], ps[3][:, :]).then_inc(S("lT_out"), 1)
            dve.wait_ge(S("cum"), 1)
            for n, b in enumerate((6, 7, 0, 1)):
                ins = nc.vector.tensor_copy(cum[:, n * T:(n + 1) * T], ps[b][:, :])
            ins.then_inc(S("cum_out"), 1)
            dve.wait_ge(S("cum_out"), 1)
            for d in range(2):
                cv = tiles(cum, 2 * d, 2).rearrange("p (b t) -> p b t", t=P)
                ev = cv[:, :, end(d):end(d) + 1].to_broadcast([P, 2 * TILES, P])
                ins = nc.vector.tensor_tensor(tiles(kd, 2 * d, 2).rearrange("p (b t) -> p b t", t=P), ev, cv, ALU.subtract)
            ins.then_inc(S("rest"), 1)

            def exponents(n):
                d, l = steps[n]
                cv, dv = blocks(tiles(cum, 2 * d, 2), l), blocks(expo[d], l)
                ref = (1 << l) - 1 if d == 0 else 1 << l
                if n >= 2:
                    dve.wait_ge(S("kf"), n - 1)
                nc.vector.tensor_tensor(dv, cv, cv[:, :, :, ref:ref + 1].to_broadcast(list(cv.shape)),
                                        ALU.subtract).then_inc(S("dv"), 1)

            def factors(n):
                d, l = steps[n]
                dve.wait_ge(S("exps"), n + 1)
                if n >= 2:
                    dve.wait_ge(S("s_mm"), len(js) * (n - 1))
                for q in range(2):
                    half_, zeros = slice(q * HD, (q + 1) * HD), queries[d][:, q * 1024:(q + 1) * 1024]
                    nc.vector.tensor_tensor(later(zeros, d, l)[half_], later(expo[d], d, l)[half_], later(tiles(pr, T_HQ, 2), d, l)[half_], ALU.mult)
                nc.vector.tensor_tensor(sooner(keys[d], d, l), sooner(keys[d], d, l), sooner(tiles(pr, T_HF + 2 * d, 2), d, l),
                                        ALU.mult).then_inc(S("kf"), 1)

            def collect(n):
                d, l = steps[n]
                B = 2 << l
                for m, j in enumerate(js):
                    dve.wait_ge(S("s_mm"), len(js) * n + m + 1)
                    dst, src = at[:, d * 2048 + j * 512:d * 2048 + (j + 1) * 512], score_bank(n, j)[:, :]
                    if l == 0:
                        dst, src = (v.rearrange("p (b t) -> p b t", b=4) for v in (dst, src))
                        mask = c(C_BASE + d * P).bitcast(I32).rearrange("p (b t) -> p b t", b=1).to_broadcast([P, 4, P])
                    else:
                        dst, src = (halves(v, B, d == 0) for v in (dst, src))
                        mask = halves(c(C_LEVEL + (d * LEVELS + l) * P).bitcast(I32), B, d == 0).to_broadcast(list(dst.shape))
                    nc.vector.copy_predicated(dst, mask, src).then_inc(S("at"), 1)

            dve.wait_ge(S("kd_exp"), 1)
            nc.vector.tensor_tensor(kd, kd, tiles(pr, T_HF, 4), ALU.mult).then_inc(S("kd"), 1)
            for d in range(2):
                ins = nc.vector.tensor_tensor(tiles(qd, 2 * d, 2), tiles(qd, 2 * d, 2), tiles(pr, T_HQ, 2), ALU.mult)
            link(ins)
            dve.wait_ge(S("kT"), 1)
            nc.vector.tensor_copy(lT[:, 0:512], ps[2][:, :])
            nc.vector.tensor_copy(lT[:, 512:1024], ps[3][:, :]).then_inc(S("kT_out"), 1)
            dve.wait_ge(S("kv"), 1)
            for m in range(1, TILES):
                for d in range(2):
                    j0, j1 = ORDER[d][m - 1], ORDER[d][m]
                    for i in range(2):
                        new = st[:, d * 512 + (2 * j1 + i) * HD:d * 512 + (2 * j1 + i + 1) * HD]
                        old = st[:, d * 512 + (2 * j0 + i) * HD:d * 512 + (2 * j0 + i + 1) * HD]
                        kv = ps[6 + d][:, (2 * j0 + i) * HD:(2 * j0 + i + 1) * HD]
                        if m == 1:
                            ins = nc.vector.tensor_copy(new, kv)
                        else:
                            e_ = ecol[:, (2 * d + i) * TILES + j0:(2 * d + i) * TILES + j0 + 1]
                            ins = nc.vector.scalar_tensor_tensor(out=new, in0=old, scalar=e_, in1=kv, op0=ALU.mult, op1=ALU.add)
                link(ins)
            dve.wait_ge(S("at0"), 1)
            exponents(0)
            exponents(1)
            for n in range(len(steps)):
                factors(n)
                if n + 2 < len(steps):
                    exponents(n + 2)
                if n >= 1:
                    collect(n - 1)
            collect(len(steps) - 1)
            dve.wait_ge(S("y"), 1)
            for i in range(2):
                ins = nc.vector.tensor_copy(y[:, i * T + lo0:(i + 1) * T], ps[4 + i][:, lo0:])
            link(ins)
            nc.vector.tensor_tensor(two(sq, layer), two(y, layer), two(y, layer), ALU.mult).then_inc(S("sq"), 1)
            dve.wait_ge(S("rn"), 1)
            link(nc.vector.tensor_tensor(two(y, layer), two(y, layer), two(sq, layer), ALU.mult))
            for i in range(2):
                v = y[:, i * T + lo0:(i + 1) * T]
                nc.vector.scalar_tensor_tensor(out=v, in0=v, scalar=par[:, Q_HN:Q_HN + 1],
                                               in1=pr[:, (T_HG + i) * T + lo0:(T_HG + i + 1) * T], op0=ALU.mult, op1=ALU.mult)

        @block.scalar
        def _(act):
            if layer:
                act.wait_ge(S("lb_in"), 1)
                nc.scalar.activation(col[:, 6:10], col[:, 6:10], ACT.Exp).then_inc(S("lb_exp"), 1)
            act.wait_ge(S("vT"), 1)
            nc.scalar.copy(vT[:, 0:512], ps[0][:, :])
            nc.scalar.copy(vT[:, 512:1024], ps[1][:, :]).then_inc(S("vT_out"), 1)
            act.wait_ge(S("lb"), 1)
            for n in range(4):
                i = n % 2
                ins = nc.scalar.activation(tiles(cum, n, 1), tiles(cum, n, 1), ACT.Ln, bias=col[:, 12 + i:13 + i], scale=col[:, 2 + i:3 + i])
            ins.then_inc(S("logf"), 1)
            act.wait_ge(S("lT"), 1)
            nc.scalar.copy(lT[:, 1024:1536], ps[4][:, :])
            nc.scalar.copy(lT[:, 1536:2048], ps[5][:, :]).then_inc(S("lT_out"), 1)
            act.wait_ge(S("cum_out"), 1)
            nc.scalar.activation(qd, cum, ACT.Exp)
            for d in range(2):
                cv = tiles(cum, 2 * d, 2).rearrange("p (b t) -> p b t", t=P)
                nc.scalar.activation(ecol[:, 8 * d:8 * d + 8].rearrange("p (b t) -> p b t", t=1), cv[:, :, end(d):end(d) + 1], ACT.Exp)
            act.wait_ge(S("rest"), 1)
            nc.scalar.activation(kd, kd, ACT.Exp).then_inc(S("kd_exp"), 1)
            act.wait_ge(S("kT"), 1)
            nc.scalar.copy(lT[:, 1024:1536], ps[4][:, :])
            nc.scalar.copy(lT[:, 1536:2048], ps[5][:, :]).then_inc(S("kT_out"), 1)
            for n, (d, l) in enumerate(steps):
                act.wait_ge(S("dv"), n + 1)
                if n >= 2:
                    act.wait_ge(S("s_mm"), len(js) * (n - 1))
                nc.scalar.activation(sooner(keys[d], d, l), sooner(expo[d], d, l), ACT.Exp, scale=-1.0).then_inc(S("k_exp"), 1)
                if l == 0:
                    act.wait_ge(S("k_exp"), n + 1)
                nc.scalar.activation(later(expo[d], d, l), later(expo[d], d, l), ACT.Exp).then_inc(S("exps"), 1)
            inverse_rms(E, S, act, (6, 7), sq, layer, 1.0 / HD, Q_EPS)


def rwkv(E, layer):
    nc, c, par, pr, work, mix, ring, ps, ident = (E[k] for k in ("nc", "c", "par", "pr", "work", "mix", "ring", "ps", "ident"))
    js = active(layer)
    lo0, _ = span(layer)
    KAPPA = float(np.exp(-0.5))
    MID = P // 2
    o = [0]

    def take(n):
        o[0] += n
        return work[:, o[0] - n:o[0]]

    sg, sa, cum, tm = take(2048), take(2048), take(2048), take(2048)
    vT, kk, kT, Q, ct = take(1024), take(1024), take(1024), take(1024), take(1024)
    al, rr, be, ks = (ring[:, n * 1024:(n + 1) * 1024] for n in range(4))
    rrs = (rr, sg[:, 0:1024])
    alTs, beTs, kTs = (tm[:, 0:1024], cum[:, 0:1024]), (tm[:, 1024:2048], cum[:, 1024:2048]), (kT, sg[:, 1024:2048])
    free = tiles(pr, 10, 24)
    NT, AkT, RbT, RkT = (free[:, n * 2048:(n + 1) * 2048] for n in range(4))
    X, XT = free[:, 8192:10240], free[:, 10240:12288]
    t1 = tiles(pr, T_WD, 2)
    PT, Qp = t1, ct
    Us = alTs
    st = XT[:, 0:512]
    alone = ((X, XT), (X, tm))
    tk = Q
    y = tiles(mix, 0, 2)
    sq = al
    units = [(l, j) for l in range(1, LEVELS) for j in range(TILES)]
    NU = len(units)
    PREPARE_AT = (0, 1, 2, 3, 4, 9, 10, 11, 12, 13)
    EXP_AT = (5, 6, 7)
    RAW_AT = (5, 8, 11, 14)
    TURN_AT = (NU - 6, NU - 4, NU - 2)

    def mat(m, j, hd):
        return m[:, (j * HEADS + hd) * P:(j * HEADS + hd + 1) * P]

    def four(m, j):
        return m[:, j * 512:(j + 1) * 512]

    with Stage(nc) as S, nc.Block() as block:
        for n in ("link", "tT", "raw", "raw_out", "ct", "t1", "t1_out", "x_up", "d_mm", "u_mm", "s_mm", "u", "s"):
            S(n)
        fcol = E["fcol"]

        def turns(src, dst_banks, n=2):
            for j in range(TILES):
                for i in range(n):
                    mm = nc.tensor.transpose(ps[dst_banks[j // 2]][:, (j % 2) * 256 + i * P:(j % 2) * 256 + (i + 1) * P],
                                             src[:, i * T + j * P:i * T + (j + 1) * P], ident)
            return mm

        @block.tensor
        def _(pe):
            turns(tiles(pr, T_V, 2), (4, 5)).then_inc(S("vT"), 1)
            pe.wait_ge(S("kk"), 1)
            for i in range(2):
                mm = nc.tensor.matmul(ps[6 + i][:, :], c(C_HONES), al[:, i * T:(i + 1) * T], start=True, stop=True)
            mm.then_inc(S("kk_ss"), 1)
            for n, t in ((0, T_WD), (1, T_AD)):
                for d in range(2):
                    if n == 1:
                        pe.wait_ge(S(("vT_out", "kk_max")[d]), 1)
                    for i in range(2):
                        nc.tensor.matmul(ps[4 * n + 2 * d + i][:, :], par[d * 64:(d + 1) * 64, Q_LORA + n * 256 + i * P:Q_LORA + n * 256 + (i + 1) * P],
                                         pr[d * 64:(d + 1) * 64, t * T:(t + 1) * T], start=True, stop=True).then_inc(S("lora"), 1)
            for d in range(2):
                pe.wait_ge(S("sg"), 2 * (d + 1))
                turns(tiles(sg, 2 * d, 2), (2 * d, 2 * d + 1)).then_inc(S("sT"), 1)
            for d in range(2):
                pe.wait_ge(S("sT_out"), d + 1)
                for i in range(2):
                    for j in range(TILES):
                        mm = nc.tensor.matmul(ps[2 * d + i][:, j * P:(j + 1) * P], tm[:, (d * TILES + j) * 256 + i * P:(d * TILES + j) * 256 + (i + 1) * P],
                                              c(C_TRI + d * P), start=True, stop=True)
                mm.then_inc(S("cum"), 1)
            pe.wait_ge(S("sa"), 4)
            pe.wait_ge(S("cum1_out"), 1)

            def raw(d, n, j, bank):
                pe.wait_ge(S(("al_alone", "rr_alone")[n]), 2 * (d + 1))
                for m, lh in enumerate((be, ks)):
                    for i in range(2):
                        t0 = i * T + j * P
                        both = alone[d][n].rearrange("p (q t) -> p q t", q=2)[:, :, t0:t0 + P]
                        mm = nc.tensor.matmul(ps[bank + m][:, i * 256:(i + 1) * 256], lh[:, t0:t0 + P], both, start=True, stop=True)
                return mm

            def bank_next(k):
                return 4 + 2 * (k % 2) if k < TILES else 6

            def raw_next(k):
                if k == 1:
                    pe.wait_ge(S("pt_out"), 1)
                if k >= 2:
                    pe.wait_ge(S("raw1_out"), k - 1 if k < TILES else k)
                raw(1, k // 4, k % 4, bank_next(k)).then_inc(S("raw1"), 1)

            pe.wait_ge(S("scaled"), 1)
            turns(al, (0, 1))
            turns(be, (2, 3))
            turns(ks, (4, 5)).then_inc(S("tT"), 1)
            pe.wait_ge(S("tT_out"), 2)
            for j in range(TILES):
                if j >= 2:
                    pe.wait_ge(S("raw_out"), 2 * (j - 1))
                for n in range(2):
                    raw(0, n, j, 4 * (j % 2) + 2 * n).then_inc(S("raw"), 1)
            pe.wait_ge(S("raw_out"), 2 * TILES)
            for d in range(2):
                alT, beT, kT, U, rr_ = alTs[d], beTs[d], kTs[d], Us[d], rrs[d]
                for j in range(TILES):
                    pe.wait_ge(S("x0T"), TILES * d + j + 1)
                    for hd in range(HEADS):
                        mm = nc.tensor.transpose(ps[j][:, hd * P:(hd + 1) * P], mat(X, j, hd), ident)
                    mm.then_inc(S("x0"), 1)

                def first(u):
                    l, j = units[u]
                    pe.wait_ge(S("ct"), NU * d + u + 1)
                    pe.wait_ge(S("x_up"), (NU + TILES) * d + u + 1)
                    if u >= 2:
                        pe.wait_ge(S("t1_out"), NU * d + u - 1)
                    else:
                        pe.wait_ge(S("x_up"), (NU + TILES) * d + TILES)
                    for hd in range(HEADS):
                        mm = nc.tensor.matmul(ps[u % 2][:, hd * P:(hd + 1) * P], ct[:, (u % 2) * 512 + hd * P:(u % 2) * 512 + (hd + 1) * P],
                                              mat(X, j, hd), start=True, stop=True)
                    mm.then_inc(S("t1"), 1)

                def second(u):
                    l, j = units[u]
                    pe.wait_ge(S("t1_out"), NU * d + u + 1)
                    if u >= 2:
                        pe.wait_ge(S("x_up"), (NU + TILES) * d + TILES + u - 1)
                    for hd in range(HEADS):
                        t = t1[:, (u % 2) * 512 + hd * P:(u % 2) * 512 + (hd + 1) * P]
                        mm = nc.tensor.matmul(ps[4 + u % 2][:, hd * P:(hd + 1) * P], t, mat(XT, j, hd), start=True, stop=True)
                    for hd in range(HEADS if l < LEVELS - 1 else 0):
                        t = t1[:, (u % 2) * 512 + hd * P:(u % 2) * 512 + (hd + 1) * P]
                        mm = nc.tensor.matmul(ps[2 + u % 2][:, hd * P:(hd + 1) * P], mat(XT, j, hd), t, start=True, stop=True)
                    mm.then_inc(S("d_mm"), 1)

                for u in range(NU + 1):
                    if u < NU:
                        first(u)
                    if u >= 1:
                        second(u - 1)
                    if d == 1 and u in RAW_AT:
                        raw_next(TILES + RAW_AT.index(u))
                    if d == 0 and u in TURN_AT:
                        r = TURN_AT.index(u)
                        if r == 0:
                            pe.wait_ge(S("scaled"), 2)
                        else:
                            pe.wait_ge(S("turned1_out"), r)
                        turns((al, be, ks)[r], (6, 7)).then_inc(S("turned1"), 1)
                pe.wait_ge(S("turned1_out"), len(TURN_AT))
                pe.wait_ge(S("x_up"), (NU + TILES) * (d + 1))
                for i in range(2):
                    for j in range(TILES):
                        for q in range(2):
                            hd = 2 * i + q
                            nc.tensor.matmul(ps[6 + i][q * HD:(q + 1) * HD, j * P:(j + 1) * P],
                                             alT[:, j * 256 + hd * HD:j * 256 + (hd + 1) * HD], mat(XT, j, hd), start=True, stop=True)
                for j in range(TILES):
                    for hd in range(HEADS):
                        mm = nc.tensor.matmul(ps[j // 2][:, (j % 2) * 256 + hd * HD:(j % 2) * 256 + (hd + 1) * HD], mat(AkT, j, hd),
                                              vT[:, j * 256 + hd * HD:j * 256 + (hd + 1) * HD], start=True, stop=True)
                mm.then_inc(S("pq"), 1)
                pe.wait_ge(S("qp_out"), d + 1)
                for j in range(TILES):
                    for hd in range(HEADS):
                        mm = nc.tensor.matmul(ps[2 + j // 2][:, (j % 2) * 256 + hd * HD:(j % 2) * 256 + (hd + 1) * HD], mat(XT, j, hd),
                                              Qp[:, j * 256 + hd * HD:j * 256 + (hd + 1) * HD], start=True, stop=True)
                mm.then_inc(S("q"), 1)
                pe.wait_ge(S("q_out"), d + 1)
                for m, j in enumerate(ORDER[d]):
                    if m:
                        pe.wait_ge(S("s"), (TILES - 1) * d + m)
                        for q in range(2):
                            for i in range(2):
                                mm = nc.tensor.matmul(ps[q][:, i * HD:(i + 1) * HD], PT[q * HD:(q + 1) * HD, i * T + j * P:i * T + (j + 1) * P],
                                                      st[q * HD:(q + 1) * HD, (2 * j + i) * HD:(2 * j + i + 1) * HD], start=True, stop=True)
                        mm.then_inc(S("u_mm"), 1)
                    if d == 0:
                        raw_next(m)
                    if m:
                        pe.wait_ge(S("u"), (TILES - 1) * d + m)
                    if m < TILES - 1:
                        for hd in range(HEADS):
                            q, i = hd % 2, hd // 2
                            out = ps[2][q * HD:(q + 1) * HD, i * HD:(i + 1) * HD]
                            a = j * 256 + hd * HD
                            nc.tensor.matmul(out, beT[:, a:a + HD], (U if m else Q)[:, a:a + HD], start=True, stop=False)
                            mm = nc.tensor.matmul(out, kT[:, a:a + HD], vT[:, a:a + HD], start=False, stop=True)
                        mm.then_inc(S("s_mm"), 1)
                if d == 0:
                    pe.wait_ge(S("raw1_out"), 3)
                for hd in range(HEADS):
                    q, i = hd % 2, hd // 2
                    for j in js:
                        out = ps[4 + i][q * HD:(q + 1) * HD, j * P:(j + 1) * P]
                        a = j * 256 + hd * HD
                        first_ = ORDER[d][0] == j
                        nc.tensor.matmul(out, (Q if first_ else U)[:, a:a + HD], mat(RbT, j, hd), start=True, stop=False)
                        mm = nc.tensor.matmul(out, vT[:, a:a + HD], mat(RkT, j, hd), start=False, stop=first_)
                        if not first_:
                            mm = nc.tensor.matmul(out, st[q * HD:(q + 1) * HD, (2 * j + i) * HD:(2 * j + i + 1) * HD],
                                                  rr_[q * HD:(q + 1) * HD, i * T + j * P:i * T + (j + 1) * P], start=False, stop=True)
                mm.then_inc(S("y"), 1)
            for i in range(2):
                nc.tensor.matmul(ps[i][:, lo0:], par[:, Q_LORA + 512 + i * P:Q_LORA + 512 + (i + 1) * P], pr[:, T_GD * T + lo0:(T_GD + 1) * T],
                                 start=True, stop=False)
                nc.tensor.matmul(ps[i][:, lo0:], par[0:32, Q_LORA + 768 + i * P:Q_LORA + 768 + (i + 1) * P],
                                 pr[0:32, T_GD2 * T + lo0:(T_GD2 + 1) * T], start=False, stop=True)
            pe.wait_ge(S("bonus"), 1)
            pe.wait_ge(S("y_sum"), 1)
            head_sums(E, pe, rr, (2, 3), layer)
            head_sums(E, pe, y, (6, 7), layer).then_inc(S("mean"), 1)
            pe.wait_ge(S("sq"), 1)
            head_sums(E, pe, sq, (4, 5), layer).then_inc(S("ss"), 1)

        @block.gpsimd
        def _(pool):
            nc.gpsimd.memset(X, 0.0).then_inc(S("zeros"), 1)
            nc.gpsimd.memset(XT, 0.0).then_inc(S("zeros"), 1)
            for d in range(2):
                for u, (l, j) in enumerate(units):
                    if u == 0:
                        if d == 0:
                            pool.wait_ge(S("raw_out"), 2 * TILES)
                        else:
                            pool.wait_ge(S("x_up"), NU + TILES)
                            nc.gpsimd.memset(X, 0.0).then_inc(S("zeros"), 1)
                            pool.wait_ge(S("y"), 1)
                            nc.gpsimd.memset(tm, 0.0).then_inc(S("zeros"), 1)
                            pool.wait_ge(S("raw1_out"), TILES)
                    if u >= 2:
                        pool.wait_ge(S("t1"), NU * d + u - 1)
                    mask = c(C_LEVEL + (d * LEVELS + l) * P).rearrange("p (b t) -> p b t", b=1).to_broadcast([P, HEADS, P])
                    nc.gpsimd.tensor_tensor(ct[:, (u % 2) * 512:(u % 2 + 1) * 512].rearrange("p (b t) -> p b t", b=HEADS),
                                            four(NT, j).rearrange("p (b t) -> p b t", b=HEADS), mask, ALU.mult).then_inc(S("ct"), 1)

        def tile_view(t):
            return t.rearrange("p (b t) -> p b t", t=P)

        @block.vector
        def _(dve):
            link = linker(dve, S("link"))
            for i in range(2):
                ins = nc.vector.tensor_scalar(tiles(kk, i, 1), tiles(pr, T_K + i, 1), par[:, Q_KK + i:Q_KK + i + 1], None, ALU.mult)
            link(ins)
            nc.vector.tensor_tensor(al, kk, kk, ALU.mult).then_inc(S("kk"), 1)
            dve.wait_ge(S("vT"), 1)
            nc.vector.tensor_copy(vT[:, 0:512], ps[4][:, :])
            nc.vector.tensor_copy(vT[:, 512:1024], ps[5][:, :]).then_inc(S("vT_out"), 1)
            dve.wait_ge(S("kk_ss"), 1)
            for i in range(2):
                ins = nc.vector.tensor_scalar(tiles(al, i, 1), ps[6 + i][:, :], 1e-24, None, ALU.max)
            ins.then_inc(S("kk_max"), 1)
            dve.wait_ge(S("kk_norm"), 1)
            link(nc.vector.reciprocal(al, al))
            link(nc.vector.tensor_tensor(kk, kk, al, ALU.mult))
            for d in range(2):
                dve.wait_ge(S("sT"), d + 1)
                for n in range(2 * d, 2 * d + 2):
                    ins = nc.vector.tensor_copy(tm[:, n * 512:(n + 1) * 512], ps[n][:, :])
                ins.then_inc(S("sT_out"), 1)
            dve.wait_ge(S("cum"), 1)
            for n in range(2):
                ins = nc.vector.tensor_copy(tiles(cum, n, 1), ps[n][:, :])
            link(ins)

            def prepare(d, step):
                end, rr_ = P - 1 if d == 0 else 0, rrs[d]
                cv = tile_view(tiles(cum, 2 * d, 2))
                fc = fcol[:, 0:8].rearrange("p (i j) -> p i j", i=2)
                c4 = tiles(cum, 2 * d, 2).rearrange("p (i j t) -> p i j t", i=2, t=P)
                if step == 0:
                    if d:
                        dve.wait_ge(S("cum1_out"), 1)
                    dve.wait_ge(S("sg"), 2 * (d + 1))
                    dve.wait_ge(S("sa"), 2 * (d + 1))
                    link(nc.vector.tensor_tensor(tile_view(rr_), cv, cv[:, :, MID:MID + 1].to_broadcast([P, 2 * TILES, P]), ALU.subtract))
                if step == 1:
                    link(nc.vector.tensor_tensor(al, rr_, tiles(sg, 2 * d, 2), ALU.subtract))
                if step == 2:
                    for m in range(TILES - 1):
                        j0 = ORDER[d][m]
                        ins = nc.vector.tensor_tensor(fc[:, :, j0:j0 + 1], c4[:, :, j0, end:end + 1], c4[:, :, j0, MID:MID + 1], ALU.subtract)
                    link(ins)
                    for m in range(TILES - 1):
                        j0, j1 = ORDER[d][m], ORDER[d][m + 1]
                        ins = nc.vector.tensor_tensor(fc[:, :, j0:j0 + 1], fc[:, :, j0:j0 + 1], c4[:, :, j1, MID:MID + 1], ALU.add)
                    ins.then_inc(S("dv"), 1)
                if step == 3:
                    for i in range(2):
                        ins = nc.vector.tensor_scalar(tiles(tk, i, 1), tiles(sa, 2 * d + i, 1), -1.0, par[:, Q_KA + i:Q_KA + i + 1], ALU.add, ALU.mult)
                    link(ins)
                if step == 4:
                    link(nc.vector.scalar_tensor_tensor(out=tk, in0=tk, scalar=1.0, in1=tiles(pr, T_K, 2), op0=ALU.add, op1=ALU.mult))
                if step == 5:
                    dve.wait_ge(S("exp"), d + 1)
                    link(nc.vector.tensor_tensor(ks, tk, be, ALU.mult))
                if step == 6:
                    link(nc.vector.tensor_tensor(tk, kk, tiles(sa, 2 * d, 2), ALU.mult))
                if step == 7:
                    nc.vector.scalar_tensor_tensor(out=be, in0=be, scalar=-1.0, in1=tk, op0=ALU.mult, op1=ALU.mult)
                if step == 8:
                    nc.vector.tensor_tensor(al, al, kk, ALU.mult)
                if step == 9:
                    nc.vector.tensor_tensor(rr_, rr_, tiles(pr, T_R, 2), ALU.mult).then_inc(S("scaled"), 1)

            def bonus(step):
                if step == 0:
                    link(nc.vector.tensor_tensor(ks, tiles(sa, 0, 2), tiles(sa, 2, 2), ALU.add))
                if step == 1:
                    for i in range(2):
                        ins = nc.vector.tensor_scalar(tiles(ks, i, 1), tiles(ks, i, 1), -2.0, par[:, Q_KA + i:Q_KA + i + 1], ALU.add, ALU.mult)
                    link(ins)
                if step == 2:
                    link(nc.vector.scalar_tensor_tensor(out=ks, in0=ks, scalar=2.0, in1=tiles(pr, T_K, 2), op0=ALU.add, op1=ALU.mult))
                if step == 3:
                    for i in range(2):
                        ins = nc.vector.scalar_tensor_tensor(out=tiles(rr, i, 1), in0=tiles(pr, T_R + i, 1), scalar=par[:, Q_RK + i:Q_RK + i + 1],
                                                             in1=tiles(ks, i, 1), op0=ALU.mult, op1=ALU.mult)
                    ins.then_inc(S("bonus"), 1)

            def raw_out(d, n, j, bank):
                m0, msk = ((0, C_STRICT), (4096, C_TRI))[n]
                mask = c(msk + d * P).rearrange("p (b t) -> p b t", b=1).to_broadcast([P, HEADS, P])
                for m in range(2):
                    dst = free[:, m0 + 2048 * m:m0 + 2048 * (m + 1)].rearrange("p (j b t) -> p j b t", j=TILES, b=HEADS)[:, j]
                    ins = nc.vector.tensor_tensor(dst, ps[bank + m][:, :].rearrange("p (b t) -> p b t", b=HEADS), mask, ALU.mult)
                return ins

            def raw1_out(k):
                dve.wait_ge(S("raw1"), k + 1)
                raw_out(1, k // 4, k % 4, 4 + 2 * (k % 2) if k < TILES else 6).then_inc(S("raw1_out"), 1)

            for step in range(10):
                prepare(0, step)
            dve.wait_ge(S("scaled"), 1)
            dve.wait_ge(S("zeros"), 2)
            for q in range(2):
                nc.vector.tensor_copy(X[q * HD:(q + 1) * HD, q * 1024:(q + 1) * 1024], al[q * HD:(q + 1) * HD, :]).then_inc(S("al_alone"), 1)
            dve.wait_ge(S("tT"), 1)
            for n, (dst, b) in enumerate(((alTs[0], 0), (alTs[0], 1), (beTs[0], 2))):
                ins = nc.vector.tensor_copy(dst[:, (b % 2) * 512:(b % 2 + 1) * 512], ps[b][:, :])
            ins.then_inc(S("tT_out"), 1)
            for j in range(TILES):
                for n in range(2):
                    dve.wait_ge(S("raw"), 2 * j + n + 1)
                    raw_out(0, n, j, 4 * (j % 2) + 2 * n).then_inc(S("raw_out"), 1)
            dve.wait_ge(S("raw_out"), 2 * TILES)
            for d in range(2):
                U = Us[d]
                if d:
                    dve.wait_ge(S("y"), 1)
                    for i in range(2):
                        ins = nc.vector.tensor_copy(y[:, i * T + lo0:(i + 1) * T], ps[4 + i][:, lo0:])
                    ins.then_inc(S("y_out"), 1)
                    dve.wait_ge(S("raw1_out"), TILES)
                idb = ident.rearrange("p (b t) -> p b t", b=1).to_broadcast([P, HEADS, P])
                mask = c(C_LEVEL + d * LEVELS * P).rearrange("p (b t) -> p b t", b=1).to_broadcast([P, HEADS, P])
                for j in range(TILES):
                    nc.vector.tensor_tensor(four(X, j).rearrange("p (b t) -> p b t", b=HEADS), four(NT, j).rearrange("p (b t) -> p b t", b=HEADS),
                                            mask, ALU.mult).then_inc(S("x0T"), 1)
                dve.wait_ge(S("x0T"), TILES * (d + 1))
                for j in range(TILES):
                    ins = nc.vector.tensor_tensor(four(XT, j).rearrange("p (b t) -> p b t", b=HEADS),
                                                  four(X, j).rearrange("p (b t) -> p b t", b=HEADS), idb, ALU.add)
                link(ins)
                for j in range(TILES):
                    dve.wait_ge(S("x0"), TILES * d + j + 1)
                    nc.vector.tensor_tensor(four(X, j).rearrange("p (b t) -> p b t", b=HEADS), ps[j][:, :].rearrange("p (b t) -> p b t", b=HEADS),
                                            idb, ALU.add).then_inc(S("x_up"), 1)
                for u, (l, j) in enumerate(units):
                    dve.wait_ge(S("d_mm"), NU * d + u + 1)
                    dve.wait_ge(S("x_up"), (NU + TILES) * d + u + 1)
                    ins = nc.vector.tensor_tensor(four(XT, j), four(XT, j), ps[4 + u % 2][:, :], ALU.add)
                    if l < LEVELS - 1:
                        ins = nc.vector.tensor_tensor(four(X, j), four(X, j), ps[2 + u % 2][:, :], ALU.add)
                    ins.then_inc(S("x_up"), 1)
                    if d == 0 and u in PREPARE_AT:
                        prepare(1, PREPARE_AT.index(u))
                    if d == 1 and u in RAW_AT:
                        raw1_out(TILES + RAW_AT.index(u))
                    if d == 1 and u - RAW_AT[-1] in range(1, 5):
                        bonus(u - RAW_AT[-1] - 1)
                dve.wait_ge(S("x_up"), (NU + TILES) * (d + 1))
                dve.wait_ge(S("pq"), d + 1)
                nc.vector.tensor_copy(Qp[:, 0:512], ps[0][:, :])
                nc.vector.tensor_copy(Qp[:, 512:1024], ps[1][:, :]).then_inc(S("qp_out"), 1)
                dve.wait_ge(S("q"), d + 1)
                dve.wait_ge(S("pt_out"), d + 1)
                nc.vector.tensor_copy(Q[:, 0:512], ps[2][:, :])
                nc.vector.tensor_copy(Q[:, 512:1024], ps[3][:, :]).then_inc(S("q_out"), 1)
                dve.wait_ge(S("q_out"), d + 1)
                for m, j in enumerate(ORDER[d]):
                    if m:
                        dve.wait_ge(S("u_mm"), (TILES - 1) * d + m)
                        for q in range(2):
                            uv, qv = (t[:, j * 256:(j + 1) * 256].rearrange("p (i q v) -> p i q v", i=2, q=2)[:, :, q, :] for t in (U, Q))
                            ins = nc.vector.tensor_tensor(uv, qv, ps[q][:, 0:P].rearrange("p (i v) -> p i v", i=2), ALU.add)
                        ins.then_inc(S("u"), 1)
                    if m < TILES - 1:
                        dve.wait_ge(S("s_mm"), (TILES - 1) * d + m + 1)
                        j1 = ORDER[d][m + 1]
                        new, old = st[:, j1 * P:(j1 + 1) * P], st[:, j * P:(j + 1) * P]
                        if m:
                            link(nc.vector.tensor_tensor(new, old, ps[2][:, 0:P], ALU.add))
                        for i in range(2):
                            ins = nc.vector.tensor_scalar(new[:, i * HD:(i + 1) * HD], (new if m else ps[2][:, 0:P])[:, i * HD:(i + 1) * HD],
                                                          fcol[:, 8 * (1 - d) + i * TILES + j:8 * (1 - d) + i * TILES + j + 1], None, ALU.mult)
                        ins.then_inc(S("s"), 1)
                        dve.wait_ge(S("s"), (TILES - 1) * d + m + 1)
                    if d == 0:
                        raw1_out(m)
            dve.wait_ge(S("y"), 2)
            for i in range(2):
                v = y[:, i * T + lo0:(i + 1) * T]
                ins = nc.vector.tensor_tensor(v, v, ps[4 + i][:, lo0:], ALU.add)
            ins.then_inc(S("y_sum"), 1)
            dve.wait_ge(S("y_sum"), 1)
            dve.wait_ge(S("mean"), 1)
            for i in range(2):
                v = y[:, i * T + lo0:(i + 1) * T]
                ins = nc.vector.scalar_tensor_tensor(out=v, in0=ps[6 + i][:, lo0:], scalar=-1.0 / HD, in1=v, op0=ALU.mult, op1=ALU.add)
            link(ins)
            nc.vector.tensor_tensor(two(sq, layer), two(y, layer), two(y, layer), ALU.mult).then_inc(S("sq"), 1)
            for i in range(2):
                ins = nc.vector.tensor_tensor(be[:, i * T + lo0:(i + 1) * T], pr[:, (T_V + i) * T + lo0:(T_V + i + 1) * T], ps[2 + i][:, lo0:], ALU.mult)
            dve.wait_ge(S("rn"), 1)
            link(nc.vector.tensor_tensor(two(y, layer), two(y, layer), two(sq, layer), ALU.mult))
            for i in range(2):
                v = y[:, i * T + lo0:(i + 1) * T]
                ins = nc.vector.tensor_scalar(v, v, par[:, Q_XG + i:Q_XG + i + 1], par[:, Q_XB + i:Q_XB + i + 1], ALU.mult, ALU.add)
            link(ins)
            link(nc.vector.tensor_tensor(two(y, layer), two(y, layer), two(be, layer), ALU.add))
            for i in range(2):
                v = y[:, i * T + lo0:(i + 1) * T]
                nc.vector.tensor_tensor(v, v, ps[i][:, lo0:], ALU.mult)

        @block.scalar
        def _(act):
            act.wait_ge(S("kk_max"), 1)
            nc.scalar.activation(al, al, ACT.Sqrt).then_inc(S("kk_norm"), 1)
            for m, (t, bias, done) in enumerate(((sg, Q_W0, "sg"), (sa, Q_A0, "sa"))):
                for n in range(4):
                    act.wait_ge(S("lora"), 4 * m + n + 1)
                    nc.scalar.activation(tiles(t, n, 1), ps[4 * m + n][:, :], ACT.Sigmoid, bias=par[:, bias + n:bias + n + 1]).then_inc(S(done), 1)
            act.wait_ge(S("cum"), 2)
            for n in range(2, 4):
                ins = nc.scalar.copy(tiles(cum, n, 1), ps[n][:, :])
            ins.then_inc(S("cum1_out"), 1)

            def exps(d, step):
                if step == 0:
                    act.wait_ge(S("dv"), d + 1)
                    nc.scalar.activation(be, rrs[d], ACT.Exp, scale=KAPPA).then_inc(S("be_exp"), 1)
                if step == 1:
                    act.wait_ge(S("be_exp"), d + 1)
                    nc.scalar.activation(rrs[d], rrs[d], ACT.Exp, scale=-KAPPA)
                    nc.scalar.activation(al, al, ACT.Exp, scale=-KAPPA)
                if step == 2:
                    fc = fcol[:, 0:8].rearrange("p (i j) -> p i j", i=2)
                    fo = fcol[:, 8 * (1 - d):8 * (1 - d) + 8].rearrange("p (i j) -> p i j", i=2)
                    last = ORDER[d][-1]
                    for a, b in ((0, last), (last + 1, TILES)):
                        if b > a:
                            ins = nc.scalar.activation(fo[:, :, a:b], fc[:, :, a:b], ACT.Exp, scale=-KAPPA)
                    ins.then_inc(S("exp"), 1)

            for step in range(3):
                exps(0, step)

            def rr_alone(d):
                for q in range(2):
                    nc.scalar.copy(alone[d][1][q * HD:(q + 1) * HD, q * 1024:(q + 1) * 1024], rrs[d][q * HD:(q + 1) * HD, :]).then_inc(S("rr_alone"), 1)

            act.wait_ge(S("scaled"), 1)
            act.wait_ge(S("zeros"), 2)
            rr_alone(0)
            act.wait_ge(S("tT"), 1)
            nc.scalar.copy(beTs[0][:, 512:1024], ps[3][:, :])
            nc.scalar.copy(kTs[0][:, 0:512], ps[4][:, :])
            nc.scalar.copy(kTs[0][:, 512:1024], ps[5][:, :]).then_inc(S("tT_out"), 1)
            for d in range(2):
                for u in range(NU):
                    act.wait_ge(S("t1"), NU * d + u + 1)
                    if u >= 2:
                        act.wait_ge(S("d_mm"), NU * d + u - 1)
                    nc.scalar.copy(t1[:, (u % 2) * 512:(u % 2 + 1) * 512], ps[u % 2][:, :]).then_inc(S("t1_out"), 1)
                    if d == 1 and u == 1:
                        act.wait_ge(S("zeros"), 4)
                        rr_alone(1)
                    if d == 0 and u in EXP_AT:
                        exps(1, EXP_AT.index(u))
                    if d == 0 and u - 1 in TURN_AT:
                        r = TURN_AT.index(u - 1)
                        act.wait_ge(S("turned1"), r + 1)
                        dst = (alTs, beTs, kTs)[r][1]
                        nc.scalar.copy(dst[:, 0:512], ps[6][:, :])
                        nc.scalar.copy(dst[:, 512:1024], ps[7][:, :]).then_inc(S("turned1_out"), 1)
                if d == 0:
                    act.wait_ge(S("zeros"), 3)
                    for q in range(2):
                        nc.scalar.copy(X[q * HD:(q + 1) * HD, q * 1024:(q + 1) * 1024], al[q * HD:(q + 1) * HD, :]).then_inc(S("al_alone"), 1)
                act.wait_ge(S("pq"), d + 1)
                nc.scalar.copy(PT[:, 0:512], ps[6][:, :])
                nc.scalar.copy(PT[:, 512:1024], ps[7][:, :]).then_inc(S("pt_out"), 1)
            inverse_rms(E, S, act, (4, 5), sq, layer, 1.0 / HD, Q_EPS + 1)


def residual_norm(E, S, dve, act, layer, which, lnp):
    nc, h, gate, ps, par = (E[k] for k in ("nc", "h", "gate", "ps", "par"))
    js = active(layer)
    g0 = 2 * which
    tmp, stats = E["pr"][:, 30 * T:32 * T], E["pr"][:, 29 * T:29 * T + 128]
    if dve:
        link = linker(dve, S("link"))

        def residual(m, j):
            dve.wait_ge(S("y"), m + 1)
            side = j // 2
            hj = h[:, j * D:(j + 1) * D]
            for b in range(2):
                ins = nc.vector.tensor_tensor(tmp[:, b * 512:(b + 1) * 512], ps[2 * j + b][:, :],
                                              gate[:, (g0 + side) * D + b * 512:(g0 + side) * D + (b + 1) * 512], ALU.mult)
            link(ins)
            link(nc.vector.scalar_tensor_tensor(out=hj, in0=hj, scalar=ALPHA, in1=tmp, op0=ALU.mult, op1=ALU.add))
            s = stats[:, 32 * m:32 * m + 32]
            for b in range(2):
                ins = nc.vector.bn_stats(s[:, 6 * b:6 * b + 6], hj[:, b * 512:(b + 1) * 512])
            link(ins)
            nc.vector.bn_aggr(s[:, 12:14], s[:, 0:12]).then_inc(S("var"), 1)

        def normed(m, j):
            hj, s = h[:, j * D:(j + 1) * D], stats[:, 32 * m:32 * m + 32]
            if m == 0:
                dve.wait_ge(S("ln_par"), 16)
            dve.wait_ge(S("var"), m + 1)
            link(nc.vector.scalar_tensor_tensor(out=hj, in0=hj, scalar=s[:, 12:13], in1=lnp[:, 0:D], op0=ALU.subtract, op1=ALU.mult))
            dve.wait_ge(S("rstd"), m + 1)
            nc.vector.scalar_tensor_tensor(out=hj, in0=hj, scalar=s[:, 15:16], in1=lnp[:, D:2 * D], op0=ALU.mult, op1=ALU.add)

        for m in range(len(js) + 1):
            if m < len(js):
                residual(m, js[m])
            if m >= 1:
                normed(m - 1, js[m - 1])
    if act:
        for m, j in enumerate(js):
            s = stats[:, 32 * m:32 * m + 32]
            act.wait_ge(S("var"), m + 1)
            nc.scalar.activation(s[:, 14:15], s[:, 13:14], ACT.Ln, bias=par[:, Q_EPS:Q_EPS + 1]).then_inc(S("lnv"), 1)
            act.wait_ge(S("lnv"), m + 1)
            nc.scalar.activation(s[:, 15:16], s[:, 14:15], ACT.Exp, scale=-0.5).then_inc(S("rstd"), 1)


def output_projection(E, layer):
    nc, A, mix, pr, ps = (E[k] for k in ("nc", "A", "mix", "pr", "ps"))
    js = active(layer)
    lo, n = span(layer)
    lnp = pr[:, 24 * T:28 * T]
    RAW = 8
    with Stage(nc) as S, nc.Block() as block:
        wr = S.sb("wr", KD * 2 * D // 2, F32R)
        xr = S.sb("xr", 4 * 2 * T, F32R)

        def raw(k):
            return pr[:, (k % RAW) * D:(k % RAW + 1) * D]

        def part(k, p):
            return wr[:, (2 * (k % 4) + p) * D:(2 * (k % 4) + p + 1) * D]

        def xpart(k, p, a=0, b=T):
            return xr[:, (2 * (k % 4) + p) * T + a:(2 * (k % 4) + p) * T + b]

        @block.sync
        def _(sp):
            for k in range(KD):
                sp.dma_start(raw(k), A["w_out"][layer, k]).then_inc(S(f"w{k}"), 16)
            sp.dma_start(lnp, A["ln"][layer, 0]).then_inc(S("ln_par"), 16)

        @block.tensor
        def _(pe):
            def slice_of(k, j):
                for b in range(2):
                    mm = product(nc, ps[2 * j + b][:, :], [xpart(k, p, j * P, (j + 1) * P) for p in (0, 1)],
                                 [part(k, p)[:, b * 512:(b + 1) * 512] for p in (0, 1)], k == 0, k == KD - 1)
                return mm

            for k in range(KD - 4):
                pe.wait_ge(S("low"), k + 1)
                for j in js:
                    mm = slice_of(k, j)
                mm.then_inc(S("mm"), 1)
            for j in js:
                for k in range(KD - 4, KD):
                    pe.wait_ge(S("low"), k + 1)
                    mm = slice_of(k, j)
                mm.then_inc(S("y"), 1)

        @block.vector
        def _(dve):
            for k in range(KD):
                dve.wait_ge(S("high"), k + 1)
                if k >= 4:
                    dve.wait_ge(S("mm"), k - 3)
                split_low(nc, dve, mix[:, k * T + lo:(k + 1) * T], xpart(k, 0, lo), xpart(k, 1, lo))
                split_low(nc, dve, raw(k), part(k, 0), part(k, 1)).then_inc(S("low"), 1)
            residual_norm(E, S, dve, None, layer, 0, lnp)

        @block.scalar
        def _(act):
            for k in range(KD):
                act.wait_ge(S(f"w{k}"), 16)
                if k >= 4:
                    act.wait_ge(S("mm"), k - 3)
                split_high(nc, act, mix[:, k * T + lo:(k + 1) * T], xpart(k, 0, lo))
                split_high(nc, act, raw(k), part(k, 0)).then_inc(S("high"), 1)
            residual_norm(E, S, None, act, layer, 0, lnp)


def ffn(E, layer):
    nc, A, par, pr, mix, ps = (E[k] for k in ("nc", "A", "par", "pr", "mix", "ps"))
    js = active(layer)
    lo0, n0 = span(layer)
    ns = n0 // SIDE
    lnp = pr[:, 24 * T:28 * T]
    W = 2 * D
    raws = (pr[:, 22 * T:26 * T], pr[:, 26 * T:30 * T], pr[:, 30 * T:34 * T], mix[:, 0:W], mix[:, W:2 * W])
    RAW = len(raws)
    LOADS = KF + KF // 2
    with Stage(nc) as S, nc.Block() as block:
        hr = [S.sb(f"hr{p}", KD * T, F32R) for p in range(2)]
        wr = S.sb("wr", 2 * 2 * W, F32R)
        tb = S.sb("tmp", 2 * T)

        def part(n, p):
            return wr[:, (2 * (n % 2) + p) * W:(2 * (n % 2) + p + 1) * W]

        def xpart(k, p, a=0, b=T):
            return hr[p][:, (k % 4) * T + a:(k % 4) * T + b]

        @block.sync
        def _(sp):
            for n in range(LOADS):
                if n >= RAW:
                    sp.wait_ge(S("low"), n - RAW + 1)
                if n < KF:
                    sp.dma_start(raws[n % RAW], A["w_up"][layer, n]).then_inc(S(f"w{n % RAW}"), 16)
                else:
                    k = 2 * (n - KF)
                    sp.dma_start(raws[n % RAW].rearrange("p (a n) -> p a n", a=2), A["w_down"][layer, k:k + 2].rearrange("a p n -> p a n"))\
                        .then_inc(S(f"w{n % RAW}"), 16)
            sp.wait_ge(S("low"), LOADS)
            sp.dma_start(lnp, A["ln"][layer, 1]).then_inc(S("ln_par"), 16)

        @block.tensor
        def _(pe):
            transpose_modulate(E, S, hr, js, tb, pe=pe)
            for f in range(KF):
                pe.wait_ge(S("low"), f + 1)
                if f >= 4:
                    pe.wait_ge(S("acts"), f - 3)
                for v in range(2):
                    for k in range(KD):
                        if f == 0 and v == 0:
                            pe.wait_ge(S("hT"), k + 1)
                        mm = product(nc, ps[2 * (f % 4) + v][:, lo0:], [part(f, p)[:, v * D + k * P:v * D + (k + 1) * P] for p in (0, 1)],
                                     [x[:, k * T + lo0:(k + 1) * T] for x in hr], k == 0, k == KD - 1)
                mm.then_inc(S("mm"), 1)

            def slice_of(k, j):
                n = KF + k // 2
                for b in range(2):
                    mm = product(nc, ps[2 * j + b][:, :], [xpart(k, p, j * P, (j + 1) * P) for p in (0, 1)],
                                 [part(n, p)[:, (k % 2) * D + b * 512:(k % 2) * D + (b + 1) * 512] for p in (0, 1)],
                                 k == 0, k == KF - 1)
                return mm

            for k in range(KF - 4):
                pe.wait_ge(S("low"), KF + k // 2 + 1)
                pe.wait_ge(S("x_low"), k + 1)
                for j in js:
                    if k == 0:
                        pe.wait_ge(S("acts"), KF - (KF - 1 - j) % 4)
                    mm = slice_of(k, j)
                mm.then_inc(S("down"), 1)
                if k % 2:
                    pe.wait_ge(S("down"), k + 1)
                    pe.sem_inc(S("mm"), 1)
            for j in js:
                for k in range(KF - 4, KF):
                    pe.wait_ge(S("low"), KF + k // 2 + 1)
                    pe.wait_ge(S("x_low"), k + 1)
                    mm = slice_of(k, j)
                mm.then_inc(S("y"), 1)

        @block.vector
        def _(dve):
            link = linker(dve, S("dd"))

            def low(n):
                dve.wait_ge(S("high"), n + 1)
                if n >= 2:
                    dve.wait_ge(S("mm"), n - 1)
                split_low(nc, dve, raws[n % RAW], part(n, 0), part(n, 1)).then_inc(S("low"), 1)

            def x_low(k):
                dve.wait_ge(S("x_high"), k + 1)
                if k >= 4:
                    dve.wait_ge(S("down"), k - 3)
                split_low(nc, dve, pr[:, k * T + lo0:(k + 1) * T], xpart(k, 0, lo0), xpart(k, 1, lo0)).then_inc(S("x_low"), 1)

            low(0)
            transpose_modulate(E, S, hr, js, tb, dve=dve)
            for f in range(KF + 1):
                if f < KF:
                    low(f + 1)
                    dve.wait_ge(S("mm"), f + 1)
                    if f >= 2:
                        dve.wait_ge(S("gelu"), f - 1)
                    z = ps[2 * (f % 4)][:, lo0:]
                    t = tb[:, (f % 2) * T + lo0:(f % 2 + 1) * T]
                    z3, t3 = (v.rearrange("p (s t) -> p s t", s=ns) for v in (z, t))
                    a = Q_FCW + 3 * f
                    link(nc.vector.tensor_scalar(t, z, par[:, a + 1:a + 2], par[:, Q_FCB + f:Q_FCB + f + 1], ALU.mult, ALU.add))
                    link(nc.vector.scalar_tensor_tensor(out=t3[:, :, 1:], in0=z3[:, :, :-1], scalar=par[:, a:a + 1], in1=t3[:, :, 1:],
                                                        op0=ALU.mult, op1=ALU.add))
                    nc.vector.scalar_tensor_tensor(out=t3[:, :, :-1], in0=z3[:, :, 1:], scalar=par[:, a + 2:a + 3], in1=t3[:, :, :-1],
                                                   op0=ALU.mult, op1=ALU.add).then_inc(S("conv"), 1)
                if f >= 1:
                    g = f - 1
                    dve.wait_ge(S("gelu"), g + 1)
                    o = pr[:, g * T + lo0:(g + 1) * T]
                    nc.vector.tensor_tensor(o, o, ps[2 * (g % 4) + 1][:, lo0:], ALU.mult).then_inc(S("acts"), 1)
            for k in range(KF):
                if k % 2 == 0 and k:
                    low(KF + k // 2)
                x_low(k)
            residual_norm(E, S, dve, None, layer, 1, lnp)

        @block.scalar
        def _(act):
            def high(n):
                act.wait_ge(S(f"w{n % RAW}"), 16 * (n // RAW + 1))
                if n >= 2:
                    act.wait_ge(S("mm"), n - 1)
                split_high(nc, act, raws[n % RAW], part(n, 0)).then_inc(S("high"), 1)

            high(0)
            transpose_modulate(E, S, hr, js, tb, act=act, shift=3, scale=4)
            for f in range(KF):
                high(f + 1)
                act.wait_ge(S("conv"), f + 1)
                nc.scalar.activation(pr[:, f * T + lo0:(f + 1) * T], tb[:, (f % 2) * T + lo0:(f % 2 + 1) * T],
                                     ACT.Gelu_apprx_tanh).then_inc(S("gelu"), 1)
            act.wait_ge(S("mm"), KF)
            for k in range(KF):
                if k % 2 == 0 and k:
                    high(KF + k // 2)
                act.wait_ge(S("acts"), k + 1)
                if k >= 4:
                    act.wait_ge(S("down"), k - 3)
                split_high(nc, act, pr[:, k * T + lo0:(k + 1) * T], xpart(k, 0, lo0)).then_inc(S("x_high"), 1)
            residual_norm(E, S, None, act, layer, 1, lnp)


def store_output(E):
    nc, h, out = (E[k] for k in ("nc", "h", "out"))
    with Stage(nc) as S, nc.Block() as block:
        @block.sync
        def _(sp):
            sp.dma_start(out.rearrange("(j p) d -> p j d", p=P), h[:, :].rearrange("p (j d) -> p j d", j=TILES)[:, 2:4, :])\
                .then_inc(E["stored"], 16)
            sp.wait_ge(E["stored"], 16)


def constants():
    t = np.zeros((P, N_CONST), np.float32)
    s, q = np.arange(P)[:, None], np.arange(P)[None, :]
    t[:, C_ID:C_ID + P] = s == q
    for d in range(2):
        before = (s <= q) if d == 0 else (s >= q)
        t[:, C_TRI + d * P:C_TRI + (d + 1) * P] = before
        t[:, C_STRICT + d * P:C_STRICT + (d + 1) * P] = before & (s != q)
        t[:, C_BASE + d * P:C_BASE + (d + 1) * P] = before & (s // 2 == q // 2)
        for l in range(LEVELS):
            a = C_LEVEL + (d * LEVELS + l) * P
            t[:, a:a + P] = (s // (2 << l) == q // (2 << l)) & (s // (1 << l) != q // (1 << l)) & before
    t[:, C_ONES:C_ONES + P] = 1
    t[:, C_HONES:C_HONES + P] = s // HD == q // HD
    t[:, C_ROT:C_ROT + P] = np.where(s // 32 == q // 32, np.where((q % 32 < 16) & (s == q + 16), -1.0, 0.0) + ((q % 32 >= 16) & (s == q - 16)), 0.0)
    tok = np.arange(SIDE)
    n_freq = HD // 8
    inv = (np.float32(10000.0) ** (-np.arange(n_freq, dtype=np.float32) / np.float32(n_freq))).astype(np.float32)
    ang = np.concatenate([(tok // 64).astype(np.float32)[:, None] * inv, (tok % 64).astype(np.float32)[:, None] * inv], axis=1)
    ch = np.arange(P) % 16
    t[:, C_COS:C_COS + SIDE] = np.cos(ang)[:, ch].T
    t[:, C_SIN:C_SIN + SIDE] = np.sin(ang)[:, ch].T
    for hd in range(HEADS):
        t[hd, C_SELH + hd * P:C_SELH + (hd + 1) * P] = 1
        t[hd, C_SELP + (hd // 2) * P + (hd % 2) * HD:C_SELP + (hd // 2) * P + (hd % 2 + 1) * HD] = 1
    for side in range(2):
        t[side, C_SEL2 + side * P:C_SEL2 + (side + 1) * P] = 1
    return t


def lay_out(x, c, ctx, c_ctx, ada_w, ada_b, w_in, rwkv_mu, rwkv_w0, rwkv_w2, rwkv_a0, rwkv_a2, rwkv_g2, rwkv_k_k, rwkv_k_a,
            rwkv_r_k, rwkv_lnx_g, rwkv_lnx_b, diff_lambda, diff_norm_g, hgrn_lb_logits, hgrn_norm_g, mlstm_conv_w, mlstm_conv_b,
            mlstm_gate_b, mlstm_norm_g, w_out, ffn_w_up, ffn_conv_w, ffn_conv_b, ffn_w_down, ln_g, ln_b):
    L = DEPTH
    w = np.zeros((L, D, IN_TILES * P), np.float32)
    w[:, :, 0:1184] = w_in[:, :, 0:1184]
    w[:, :, 1184:1200] = w_in[:, :, 4256:4272]
    w[:, :, 10 * P:] = w_in[:, :, 1184:4256]
    w = w.reshape(L, KD, P, IN_TILES, P).transpose(0, 3, 2, 1, 4).reshape(L, IN_TILES, P, KD * P)
    up = ffn_w_up.reshape(L, KD, P, 2, KF, P).transpose(0, 4, 2, 3, 1, 5).reshape(L, KF, P, 2 * KD * P)
    ada = ada_w.reshape(L, KD, P, 12, 512).transpose(0, 3, 2, 1, 4).reshape(L, 12, P, KD * 512)
    par = np.zeros((L, P, N_PAR), np.float32)

    def put(o, a, n):
        par[:, :, o:o + n] = a.reshape(L, n, P).transpose(0, 2, 1)

    mu = np.zeros((L, 10 * P), np.float32)
    mu[:, 0:1184] = rwkv_mu
    put(Q_MU, mu, 10)
    put(Q_W0, rwkv_w0, 4)
    put(Q_A0, rwkv_a0, 4)
    for o, a in ((Q_KK, rwkv_k_k), (Q_KA, rwkv_k_a), (Q_RK, rwkv_r_k), (Q_XG, rwkv_lnx_g), (Q_XB, rwkv_lnx_b), (Q_MN, mlstm_norm_g)):
        put(o, a, 2)
    put(Q_DN, np.tile(diff_norm_g, (1, 2)), 1)
    put(Q_HN, np.tile(hgrn_norm_g, (1, 2)), 1)
    for l in range(L):
        put(Q_LB + 2 * l, np.broadcast_to(hgrn_lb_logits[l], (L, 256)), 2)
    par[:, :, Q_MCW:Q_MCW + 12] = mlstm_conv_w.reshape(L, 3, 4, P).transpose(0, 3, 2, 1).reshape(L, P, 12)
    put(Q_MCB, mlstm_conv_b, 4)
    par[:, :, Q_FCW:Q_FCW + 3 * KF] = ffn_conv_w.reshape(L, 3, KF, P).transpose(0, 3, 2, 1).reshape(L, P, 3 * KF)
    put(Q_FCB, ffn_conv_b, KF)
    par[:, :, Q_GB:Q_GB + 16] = mlstm_gate_b.reshape(L, 1, 16)
    par[:, :, Q_LAM:Q_LAM + 128] = diff_lambda.reshape(L, 1, 128)
    par[:, :, Q_EPS] = LN_EPS
    par[:, :, Q_EPS + 1] = LNX_EPS
    par[:, :, Q_LORA:Q_LORA + 256] = rwkv_w2.reshape(L, P, 256)
    par[:, :, Q_LORA + 256:Q_LORA + 512] = rwkv_a2.reshape(L, P, 256)
    par[:, :, Q_LORA + 512:Q_LORA + 768] = rwkv_g2[:, 0:P]
    par[:, 0:32, Q_LORA + 768:Q_LORA + 1024] = rwkv_g2[:, P:160]
    ln = np.stack([ln_g, ln_b], axis=2).reshape(L, 2, 1, 2 * D)
    return {
        "x": x[0], "ctx": ctx[0], "const": constants(), "par": par,
        "cond": np.stack([c_ctx.reshape(KD, P), c.reshape(KD, P)], axis=0).transpose(2, 1, 0).reshape(P, 2 * KD),
        "ada_w": ada, "ada_b": np.broadcast_to(ada_b[:, None, :], (L, 2, 6 * D)), "w_in": w, "w_out": w_out.reshape(L, KD, P, D),
        "w_up": up, "w_down": ffn_w_down.reshape(L, KF, P, D), "ln": np.broadcast_to(ln, (L, 2, P, 2 * D)),
    }


def kernel(**inputs):
    import concourse.bacc as bacc
    from concourse.bass_utils import run_bass_kernel_spmd

    nc = bacc.Bacc("TRN2", target_bir_lowering=False, num_devices=1)
    arrays = {k: np.ascontiguousarray(v) for k, v in lay_out(**{k: np.asarray(v) for k, v in inputs.items()}).items()}
    A = {k: nc.dram_tensor(f"in_{k}", v.shape, F32, kind="ExternalInput").ap() for k, v in arrays.items()}
    out = nc.dram_tensor("out", (SIDE, D), F32, kind="ExternalOutput").ap()
    build(nc, A, out)
    r = run_bass_kernel_spmd(nc, [{f"in_{k}": v for k, v in arrays.items()}], core_ids=[0])
    return r.results[0]["out"].reshape(1, SIDE, D)
```
